# Optimizing a Trainium2 kernel written in Bass

```python
import jax, jax.numpy as jnp
from jax import lax
import numpy as np

D_MODEL = 1024
BATCH = 1
SEQ = 512
DEPTH = 1

CONV_CH = D_MODEL
CONV_K = 31
HEAD_DIM = 128
N_HEADS = D_MODEL // HEAD_DIM
DELTA_W = N_HEADS * HEAD_DIM
SHORT_CONV = 5
N_DIR = 2
CHUNK = 64
D_FF = -(-8 * D_MODEL // (3 * 256)) * 256
PLE_DIM = 256
NORM_EPS = 1e-6
LN_EPS = 1e-5
IN_SIZES = (CONV_CH, CONV_CH, DELTA_W, DELTA_W, DELTA_W, DELTA_W,
            N_DIR * N_HEADS, N_DIR * N_HEADS, D_MODEL, D_MODEL)
IN_TOTAL = sum(IN_SIZES)


def rms_norm(x, g):
    xf = x.astype(jnp.float32)
    y = xf * lax.rsqrt(jnp.mean(xf * xf, axis=-1, keepdims=True) + NORM_EPS)
    return (y * g.astype(jnp.float32)).astype(x.dtype)

def layer_norm(x, g, b):
    xf = x.astype(jnp.float32)
    mu = jnp.mean(xf, axis=-1, keepdims=True)
    xc = xf - mu
    y = xc * lax.rsqrt(jnp.mean(xc * xc, axis=-1, keepdims=True) + LN_EPS)
    return (y * g.astype(jnp.float32) + b.astype(jnp.float32)).astype(x.dtype)

def l2_norm(x):
    xf = x.astype(jnp.float32)
    return xf * lax.rsqrt(jnp.sum(xf * xf, axis=-1, keepdims=True) + NORM_EPS)

def depthwise_conv(x, w):
    k = w.shape[0]
    return lax.conv_general_dilated(
        x, w[:, None, :].astype(x.dtype), window_strides=(1,),
        padding=[(k // 2, k // 2)], dimension_numbers=("NWC", "WIO", "NWC"),
        feature_group_count=x.shape[-1])

def split_cols(t, sizes):
    out, start = [], 0
    for s in sizes:
        out.append(t[..., start:start + s])
        start += s
    return out

def gated_delta_rule(q, k, v, g, beta):
    out_dtype = v.dtype
    bsz, t_len, n_h, _ = q.shape
    n_blk = t_len // CHUNK

    def blocks(t):
        t = t.astype(jnp.float32).reshape((bsz, n_blk, CHUNK, n_h) + t.shape[3:])
        return jnp.moveaxis(t, 3, 1)

    q, k, v, g, beta = (blocks(t) for t in (q, k, v, g, beta))
    g = jnp.cumsum(g, axis=-1)
    idx = jnp.arange(CHUNK)
    tri_incl = idx[:, None] >= idx[None, :]
    tri_strict = idx[:, None] > idx[None, :]
    decay = jnp.exp(jnp.where(tri_incl, g[..., :, None] - g[..., None, :], -jnp.inf))
    k_beta = k * beta[..., None]
    lower = jnp.where(tri_strict, jnp.einsum('bhncd,bhnsd->bhncs', k_beta, k) * decay, 0.0)
    dv = v.shape[-1]
    rhs = jnp.concatenate([v * beta[..., None], k_beta * jnp.exp(g)[..., None]], axis=-1)
    sol = lax.linalg.triangular_solve(lower, rhs, left_side=True, lower=True, unit_diagonal=True)
    u, w = sol[..., :dv], sol[..., dv:]
    qk = jnp.einsum('bhncd,bhnsd->bhncs', q, k) * decay
    g_last = g[..., -1]
    q_dec = q * jnp.exp(g)[..., None]
    k_tail = k * jnp.exp(g_last[..., None] - g)[..., None]

    def step(state, xs):
        qd, kt, ui, wi, qki, gl = xs
        v_new = ui - jnp.einsum('bhck,bhkv->bhcv', wi, state)
        o = jnp.einsum('bhck,bhkv->bhcv', qd, state) + jnp.einsum('bhcs,bhsv->bhcv', qki, v_new)
        state = state * jnp.exp(gl)[..., None, None] + jnp.einsum('bhck,bhcv->bhkv', kt, v_new)
        return state, o

    xs = tuple(jnp.moveaxis(t, 2, 0) for t in (q_dec, k_tail, u, w, qk, g_last))
    s0 = jnp.zeros((bsz, n_h, q.shape[-1], dv), jnp.float32)
    _, o = lax.scan(step, s0, xs)
    o = jnp.transpose(o, (1, 0, 3, 2, 4)).reshape(bsz, t_len, n_h, dv)
    return o.astype(out_dtype)

def first_inputs(seed: int = 0) -> dict:
    key = jax.random.key(seed)
    ks = jax.random.split(key, 32)
    f32 = jnp.float32

    def nrm(k, shape, fan_in):
        return jax.random.normal(k, shape, f32) * (fan_in ** -0.5)

    def gain(k, shape):
        return 1.0 + 0.05 * jax.random.normal(k, shape, f32)

    def small(k, shape):
        return 0.01 * jax.random.normal(k, shape, f32)

    a_log = jnp.log(jax.random.uniform(ks[10], (DEPTH, N_DIR, N_HEADS), f32, 1.0, 16.0))
    dt = jnp.exp(jax.random.uniform(ks[11], (DEPTH, N_DIR, N_HEADS), f32,
                                    float(np.log(1e-3)), float(np.log(1e-1))))
    dt_bias = dt + jnp.log(-jnp.expm1(-dt))
    return {
        "x": jax.random.normal(ks[0], (BATCH, SEQ, D_MODEL), f32),
        "p": jax.random.normal(ks[1], (DEPTH, BATCH, SEQ, PLE_DIM), f32),
        "g_mix": gain(ks[2], (DEPTH, D_MODEL)),
        "w_in": nrm(ks[3], (DEPTH, D_MODEL, IN_TOTAL), D_MODEL),
        "conv_dw_w": nrm(ks[4], (DEPTH, CONV_K, CONV_CH), CONV_K),
        "conv_dw_b": small(ks[5], (DEPTH, CONV_CH)),
        "conv_ln_g": gain(ks[6], (DEPTH, CONV_CH)),
        "conv_ln_b": small(ks[7], (DEPTH, CONV_CH)),
        "w_conv_out": nrm(ks[8], (DEPTH, CONV_CH, D_MODEL), CONV_CH),
        "qkv_conv_w": nrm(ks[9], (DEPTH, SHORT_CONV, 3 * DELTA_W), SHORT_CONV),
        "a_log": a_log,
        "dt_bias": dt_bias,
        "delta_norm_g": gain(ks[12], (DEPTH, HEAD_DIM)),
        "w_delta_out": nrm(ks[13], (DEPTH, DELTA_W, D_MODEL), DELTA_W),
        "w_o": nrm(ks[14], (DEPTH, D_MODEL, D_MODEL), D_MODEL),
        "g_ffn": gain(ks[15], (DEPTH, D_MODEL)),
        "w_gate_up": nrm(ks[16], (DEPTH, D_MODEL, 2 * D_FF), D_MODEL),
        "w_down": nrm(ks[17], (DEPTH, D_FF, D_MODEL), D_FF),
        "g_pl": gain(ks[18], (DEPTH, D_MODEL)),
        "w_pl_gate": nrm(ks[19], (DEPTH, D_MODEL, D_MODEL), D_MODEL),
        "w_pl_proj": nrm(ks[20], (DEPTH, PLE_DIM, D_MODEL), PLE_DIM),
        "g_pl_proj": gain(ks[21], (DEPTH, D_MODEL)),
        "g_final": gain(ks[22], (D_MODEL,)),
    }

def first_block(x, p, g_mix, w_in, conv_dw_w, conv_dw_b, conv_ln_g, conv_ln_b, w_conv_out,
              qkv_conv_w, a_log, dt_bias, delta_norm_g, w_delta_out, w_o, g_ffn,
              w_gate_up, w_down, g_pl, w_pl_gate, w_pl_proj, g_pl_proj, g_final):
    bsz, t_len, _ = x.shape
    for i in range(DEPTH):
        h = rms_norm(x, g_mix[i])
        proj = h @ w_in[i]
        glu_a, glu_b, q, k, v, z, a_in, b_in, gate_a, gate_b = split_cols(proj, IN_SIZES)

        c = glu_a * jax.nn.sigmoid(glu_b)
        c = depthwise_conv(c, conv_dw_w[i]) + conv_dw_b[i]
        c = jax.nn.silu(layer_norm(c, conv_ln_g[i], conv_ln_b[i]))
        y_conv = c @ w_conv_out[i]

        qkv = jax.nn.silu(depthwise_conv(jnp.concatenate([q, k, v], axis=-1), qkv_conv_w[i]))
        q, k, v = split_cols(qkv, (DELTA_W, DELTA_W, DELTA_W))
        q = l2_norm(q.reshape(bsz, t_len, N_HEADS, HEAD_DIM)) * (HEAD_DIM ** -0.5)
        k = l2_norm(k.reshape(bsz, t_len, N_HEADS, HEAD_DIM))
        v = v.reshape(bsz, t_len, N_HEADS, HEAD_DIM)
        a_in = a_in.astype(jnp.float32).reshape(bsz, t_len, N_DIR, N_HEADS)
        b_in = b_in.astype(jnp.float32).reshape(bsz, t_len, N_DIR, N_HEADS)
        g = -jnp.exp(a_log[i].astype(jnp.float32)) * jax.nn.softplus(a_in + dt_bias[i].astype(jnp.float32))
        beta = jax.nn.sigmoid(b_in)
        o_fwd = gated_delta_rule(q, k, v, g[:, :, 0], beta[:, :, 0])
        rev = lambda t: jnp.flip(t, axis=1)
        o_bwd = rev(gated_delta_rule(rev(q), rev(k), rev(v), rev(g[:, :, 1]), rev(beta[:, :, 1])))
        o = rms_norm(o_fwd + o_bwd, delta_norm_g[i]) * jax.nn.silu(z.reshape(bsz, t_len, N_HEADS, HEAD_DIM))
        y_delta = o.reshape(bsz, t_len, DELTA_W).astype(x.dtype) @ w_delta_out[i]

        y = jax.nn.sigmoid(gate_a) * y_conv + jax.nn.sigmoid(gate_b) * y_delta
        x = x + y @ w_o[i]

        h = rms_norm(x, g_ffn[i])
        gt, up = split_cols(h @ w_gate_up[i], (D_FF, D_FF))
        x = x + (jax.nn.silu(gt) * up) @ w_down[i]

        pl = rms_norm(p[i] @ w_pl_proj[i], g_pl_proj[i])
        x = x + jax.nn.sigmoid(rms_norm(x, g_pl[i]) @ w_pl_gate[i]) * pl
    return rms_norm(x, g_final)


POOL_WINDOWS = (2, 4, 8, 16)
POOL_WIDTH = D_MODEL // 2
POOL_GROUP = POOL_WIDTH // len(POOL_WINDOWS)
HEAD_DIM_2 = 64
N_HEADS_2 = (D_MODEL // 2) // HEAD_DIM_2
N_KV_HEADS = 2
ATTN_WIDTH = N_HEADS_2 * HEAD_DIM_2
KV_WIDTH = N_KV_HEADS * HEAD_DIM_2
WINDOW = 128
BLOCK = 128
ROPE_THETA = 500000.0
ROT_DIM = HEAD_DIM_2 // 4
MIX_WIDTH = POOL_WIDTH + ATTN_WIDTH
IN_WIDTH = POOL_WIDTH + ATTN_WIDTH + 2 * KV_WIDTH
D_FF_2 = 2816
EPS = 1e-6
NEG_INF = -1e30


def rms_norm_2(x, g):
    xf = x.astype(jnp.float32)
    y = xf * lax.rsqrt(jnp.mean(xf * xf, axis=-1, keepdims=True) + EPS)
    return (y * g.astype(jnp.float32)).astype(x.dtype)

def swiglu(h, w_gu, w_down):
    gate, up = jnp.split(h @ w_gu, 2, axis=-1)
    return (jax.nn.silu(gate) * up) @ w_down

def pool_mix(u, w_pool, pool_scale):
    B, S, C = u.shape
    uf = u.astype(jnp.float32)
    cs = jnp.concatenate([jnp.zeros((B, 1, C), jnp.float32), jnp.cumsum(uf, axis=1)], axis=1)
    t = jnp.arange(S)
    outs = []
    for g, w in enumerate(POOL_WINDOWS):
        lo, hi = g * POOL_GROUP, (g + 1) * POOL_GROUP
        start = jnp.maximum(t + 1 - w, 0)
        cnt = (t + 1 - start).astype(jnp.float32)
        csg = cs[:, :, lo:hi]
        mean = (csg[:, 1:] - csg[:, start]) / cnt[None, :, None]
        outs.append(mean - uf[:, :, lo:hi])
    d = jnp.stack(outs, axis=2).astype(u.dtype)
    y = jnp.einsum('bsgc,gcd->bsgd', d, w_pool).reshape(B, S, POOL_WIDTH)
    return y * pool_scale

def apply_partial_rope(x, cos, sin):
    half = ROT_DIM // 2
    x1, x2 = x[..., :half], x[..., half:ROT_DIM]
    rot = jnp.concatenate([x1 * cos - x2 * sin, x2 * cos + x1 * sin], axis=-1)
    return jnp.concatenate([rot, x[..., ROT_DIM:]], axis=-1)

def swa_with_sinks(q, k, v, sinks):
    B, S = q.shape[0], q.shape[1]
    nb = S // BLOCK
    G = N_HEADS_2 // N_KV_HEADS
    qb = q.reshape(B, nb, BLOCK, N_KV_HEADS, G, HEAD_DIM_2)
    pad = ((0, 0), (BLOCK, 0), (0, 0), (0, 0))
    kp = jnp.pad(k, pad).reshape(B, nb + 1, BLOCK, N_KV_HEADS, HEAD_DIM_2)
    vp = jnp.pad(v, pad).reshape(B, nb + 1, BLOCK, N_KV_HEADS, HEAD_DIM_2)
    kb = jnp.concatenate([kp[:, :-1], kp[:, 1:]], axis=2)
    vb = jnp.concatenate([vp[:, :-1], vp[:, 1:]], axis=2)
    s = jnp.einsum('bnqkgd,bnjkd->bnkgqj', qb, kb,
                   preferred_element_type=jnp.float32) * (HEAD_DIM_2 ** -0.5)
    qi = jnp.arange(BLOCK)[:, None]
    kj = jnp.arange(2 * BLOCK)[None, :]
    diff = qi + BLOCK - kj
    band = (diff >= 0) & (diff < WINDOW)
    key_abs = jnp.arange(nb)[:, None] * BLOCK - BLOCK + kj
    valid = band[None] & (key_abs >= 0)[:, None, :]
    s = jnp.where(valid[None, :, None, None], s, NEG_INF)
    sink = jnp.broadcast_to(sinks.astype(jnp.float32).reshape(1, 1, N_KV_HEADS, G, 1, 1),
                            s.shape[:-1] + (1,))
    p = jax.nn.softmax(jnp.concatenate([s, sink], axis=-1), axis=-1)[..., :-1]
    o = jnp.einsum('bnkgqj,bnjkd->bnqkgd', p.astype(v.dtype), vb)
    return o.reshape(B, S, ATTN_WIDTH)

def token_mixer(h, cos, sin, w_in, w_pool, pool_scale, sinks, g_pool, g_attn, w_out):
    B, S, _ = h.shape
    z = h @ w_in
    u = z[..., :POOL_WIDTH]
    q = z[..., POOL_WIDTH:MIX_WIDTH].reshape(B, S, N_HEADS_2, HEAD_DIM_2)
    k = z[..., MIX_WIDTH:MIX_WIDTH + KV_WIDTH].reshape(B, S, N_KV_HEADS, HEAD_DIM_2)
    v = z[..., MIX_WIDTH + KV_WIDTH:].reshape(B, S, N_KV_HEADS, HEAD_DIM_2)
    pool_out = pool_mix(u, w_pool, pool_scale)
    q = apply_partial_rope(q, cos, sin)
    k = apply_partial_rope(k, cos, sin)
    attn_out = swa_with_sinks(q, k, v, sinks)
    y = jnp.concatenate([rms_norm_2(pool_out, g_pool), rms_norm_2(attn_out, g_attn)], axis=-1)
    return y @ w_out

def second_inputs(seed: int = 0) -> dict:
    key = jax.random.key(seed)
    ks = jax.random.split(key, 24)
    f32 = jnp.float32

    def w(k, shape, fan_in):
        return jax.random.normal(k, shape, f32) * fan_in ** -0.5

    def gain(k, n):
        return 1.0 + 0.05 * jax.random.normal(k, (DEPTH, n), f32)

    x = jax.random.normal(ks[0], (BATCH, SEQ, D_MODEL), f32)
    offset = jax.random.randint(ks[1], (BATCH, 1), 0, 4096, jnp.int32)
    positions = offset + jnp.arange(SEQ, dtype=jnp.int32)[None, :]
    return {
        "x": x,
        "positions": positions,
        "ffn1_pre": gain(ks[2], D_MODEL),
        "ffn1_w_gu": w(ks[3], (DEPTH, D_MODEL, 2 * D_FF_2), D_MODEL),
        "ffn1_w_down": w(ks[4], (DEPTH, D_FF_2, D_MODEL), D_FF_2),
        "ffn1_post": gain(ks[5], D_MODEL),
        "mix_pre": gain(ks[6], D_MODEL),
        "w_in": w(ks[7], (DEPTH, D_MODEL, IN_WIDTH), D_MODEL),
        "w_pool": w(ks[8], (DEPTH, len(POOL_WINDOWS), POOL_GROUP, POOL_GROUP), POOL_GROUP),
        "pool_scale": 0.5 + 0.05 * jax.random.normal(ks[9], (DEPTH, POOL_WIDTH), f32),
        "sinks": 0.5 * jax.random.normal(ks[10], (DEPTH, N_HEADS_2), f32),
        "g_pool": gain(ks[11], POOL_WIDTH),
        "g_attn": gain(ks[12], ATTN_WIDTH),
        "w_out": w(ks[13], (DEPTH, MIX_WIDTH, D_MODEL), MIX_WIDTH),
        "mix_post": gain(ks[14], D_MODEL),
        "ffn2_pre": gain(ks[15], D_MODEL),
        "ffn2_w_gu": w(ks[16], (DEPTH, D_MODEL, 2 * D_FF_2), D_MODEL),
        "ffn2_w_down": w(ks[17], (DEPTH, D_FF_2, D_MODEL), D_FF_2),
        "ffn2_post": gain(ks[18], D_MODEL),
    }

def second_block(x, positions, ffn1_pre, ffn1_w_gu, ffn1_w_down, ffn1_post,
              mix_pre, w_in, w_pool, pool_scale, sinks, g_pool, g_attn, w_out, mix_post,
              ffn2_pre, ffn2_w_gu, ffn2_w_down, ffn2_post):
    inv_freq = ROPE_THETA ** (-jnp.arange(0, ROT_DIM, 2, dtype=jnp.float32) / ROT_DIM)
    ang = positions.astype(jnp.float32)[..., None] * inv_freq
    cos = jnp.cos(ang)[:, :, None, :].astype(x.dtype)
    sin = jnp.sin(ang)[:, :, None, :].astype(x.dtype)
    for l in range(DEPTH):
        h = swiglu(rms_norm_2(x, ffn1_pre[l]), ffn1_w_gu[l], ffn1_w_down[l])
        x = x + 0.5 * rms_norm_2(h, ffn1_post[l])
        h = token_mixer(rms_norm_2(x, mix_pre[l]), cos, sin, w_in[l], w_pool[l], pool_scale[l],
                        sinks[l], g_pool[l], g_attn[l], w_out[l])
        x = x + rms_norm_2(h, mix_post[l])
        h = swiglu(rms_norm_2(x, ffn2_pre[l]), ffn2_w_gu[l], ffn2_w_down[l])
        x = x + 0.5 * rms_norm_2(h, ffn2_post[l])
    return x


def setup_inputs(seed=0):
    out = dict(first_inputs(seed))
    for name, value in second_inputs(seed + 1).items():
        if name != "x":
            out[name + "_2"] = value
    return out


def reference(
    x, p, g_mix, w_in, conv_dw_w, conv_dw_b, conv_ln_g, conv_ln_b, w_conv_out, qkv_conv_w,
    a_log, dt_bias, delta_norm_g, w_delta_out, w_o, g_ffn, w_gate_up, w_down, g_pl, w_pl_gate,
    w_pl_proj, g_pl_proj, g_final, positions_2, ffn1_pre_2, ffn1_w_gu_2, ffn1_w_down_2,
    ffn1_post_2, mix_pre_2, w_in_2, w_pool_2, pool_scale_2, sinks_2, g_pool_2, g_attn_2,
    w_out_2, mix_post_2, ffn2_pre_2, ffn2_w_gu_2, ffn2_w_down_2, ffn2_post_2,
):
    x = first_block(
        x, p, g_mix, w_in, conv_dw_w, conv_dw_b, conv_ln_g, conv_ln_b, w_conv_out, qkv_conv_w,
        a_log, dt_bias, delta_norm_g, w_delta_out, w_o, g_ffn, w_gate_up, w_down, g_pl,
        w_pl_gate, w_pl_proj, g_pl_proj, g_final,
    )
    return second_block(
        x, positions_2, ffn1_pre_2, ffn1_w_gu_2, ffn1_w_down_2, ffn1_post_2, mix_pre_2, w_in_2,
        w_pool_2, pool_scale_2, sinks_2, g_pool_2, g_attn_2, w_out_2, mix_post_2, ffn2_pre_2,
        ffn2_w_gu_2, ffn2_w_down_2, ffn2_post_2,
    )


_drawn_inputs = setup_inputs


def setup_inputs(seed=0):
    import zlib

    import numpy as np

    out = dict(_drawn_inputs(seed))
    spreads = {}
    factors = {'conv_dw_b': 5.456,
     'conv_ln_b': 8.0,
     'delta_norm_g': 3.019,
     'g_pl': 5.85,
     'sinks_2': 5.755,
     'ffn2_post_2': 3.535}
    for name, (base, spread) in spreads.items():
        noise = np.random.default_rng([zlib.crc32(name.encode()), seed]).standard_normal(out[name].shape)
        drawn = base * np.exp(spread * noise) if base else spread * noise
        out[name] = __import__('jax').numpy.asarray(drawn.astype(out[name].dtype))
    for name, factor in factors.items():
        out[name] = (out[name] * factor).astype(out[name].dtype)
    return out
```

```python
import numpy as np
import concourse.bass as bass
from concourse import mybir
from contextlib import ExitStack

F32 = mybir.dt.float32
F32R = mybir.dt.float32r
ALU = mybir.AluOpType
ACT = mybir.ActivationFunctionType

P = 128
T = 512
D = 1024
KT = D // P
FT = 2816 // P
KH = FT // 2
H = 8
HH = 4
NC = T // P
CK = 31
CP = CK // 2
SK = 5
SP_ = SK // 2
W64 = 64
LEVELS = 6
PT_ = 4
HD2 = 64
NB = T // P
ROT = HD2 // 4
THETA = 500000.0
POOL_W = (2, 4, 8, 16)
NEG = -1e30
EPS = 1e-6
LN_EPS = 1e-5

VEC = ["g_mix", "conv_b", "ln_g", "ln_b", "g_ffn", "g_pl", "g_plp", "g_final",
       "ffn1_pre", "ffn1_post", "mix_pre", "mix_post", "ffn2_pre", "ffn2_post"]
NV = len(VEC) + CK

C_ID, C_ONE, C_TRI, C_LVL, C_I64 = 0, P, 2 * P, 4 * P, 4 * P + 2 * LEVELS * W64
C_END = C_I64 + W64


def constant_table():
    c = np.zeros((P, C_END), np.float32)
    r = np.arange(P)
    c[:, C_ID:C_ID + P] = np.eye(P)
    c[:, C_ONE:C_ONE + P] = 1.0
    c[:, C_TRI:C_TRI + P] = r[:, None] <= r[None, :]
    c[:, C_TRI + P:C_TRI + 2 * P] = r[:, None] >= r[None, :]
    row, col = r[:, None] % W64, np.arange(W64)[None, :]
    for lv in range(LEVELS):
        s = 1 << lv
        same = row // (2 * s) == col // (2 * s)
        low = same & (row // s % 2 == 1) & (col // s % 2 == 0)
        up = same & (row // s % 2 == 0) & (col // s % 2 == 1)
        at = C_LVL + lv * 2 * W64
        c[:, at:at + W64] = low
        c[:, at + W64:at + 2 * W64] = up
    c[:, C_I64:C_I64 + W64] = row == col
    return c


def mixer_table():
    perm = np.zeros((P, P), np.float32)
    for h in range(0, P, HD2):
        for d in range(ROT // 2):
            perm[h + d + ROT // 2, h + d] = -1.0
            perm[h + d, h + d + ROT // 2] = 1.0
    q, k = np.arange(P)[:, None], np.arange(2 * P)[None, :]
    band = np.where((k > q) & (k <= q + P), 0.0, NEG)
    t = np.arange(16)
    edge = np.concatenate([1.0 / np.minimum(t + 1, w) for w in POOL_W])
    return np.concatenate([perm, band, np.broadcast_to(edge, (P, 64))], 1).astype(np.float32)


class Units:

    def __init__(self):
        self.src, self.cols, self.at = [], [], {}

    def add(self, name, src, cols):
        self.at[name] = len(self.src)
        self.src.append(src)
        self.cols.append(cols)


class Outs:

    def __init__(self):
        self.reader, self.at = [], {}

    def add(self, name, reader):
        self.at[name] = len(self.reader)
        self.reader.append(reader)

    def count(self, o):
        return self.reader[:o + 1].count(self.reader[o])


def build(nc, a, out):
    ctx = ExitStack()
    with ctx:
        sems = {}

        def S(name):
            if name not in sems:
                sems[name] = ctx.enter_context(nc.semaphore(name))
            return sems[name]

        ALL = 212832
        base = [nc.sbuf_base + (-nc.sbuf_base) % 32]
        first = base[0]

        def at(name, cols, dtype=F32, offset=None, shape=None):
            if offset is None:
                offset = base[0]
                base[0] += cols * 4 + (-cols * 4) % 32
            assert offset + cols * 4 <= first + ALL, (name, offset + cols * 4 - first - ALL)
            return nc.alloc_sbuf_tensor_at(name, shape or [P, cols], dtype, offset=offset)

        UC = KH * P
        w_raw = at("w_raw", 4 * UC, shape=[P, 4, UC])
        w_hi = at("w_hi", 2 * UC, F32R, shape=[P, 2, UC])
        w_lo = at("w_lo", 2 * UC, F32R, shape=[P, 2, UC])
        A_OFF = base[0]
        a_hi = at("a_hi", KT * T, F32R, shape=[P, KT, T])
        a_lo = at("a_lo", KT * T, F32R, shape=[P, KT, T])
        X_OFF = base[0]
        x = at("x", KT * T, shape=[P, KT, T])
        consts = at("consts", C_END)
        vec = at("vec", KT * NV, shape=[P, KT, NV])
        swt = at("swt", 3 * H * SK, shape=[P, 3 * H, SK])
        gate_p = at("gate_p", 59)
        eps_t = gate_p[:, 33:37]
        tmp1 = at("tmp1", T)
        tmp2 = at("tmp2", T)
        sq = at("sq", 2 * T, shape=[P, 2, T])
        acc = at("acc", T)
        rstd = at("rstd", T)
        R_OFF = base[0]

        ident = consts[:, C_ID:C_ID + P]
        ones = consts[:, C_ONE:C_ONE + P]
        tri = [consts[:, C_TRI + d * P:C_TRI + (d + 1) * P] for d in range(2)]
        id64 = consts[:, C_I64:C_I64 + W64]

        def v(name, t):
            return vec[:, t, VEC.index(name):VEC.index(name) + 1]

        base[0] = R_OFF
        PAD = T + 2 * CP
        cpad = at("cpad", KT * PAD, shape=[P, KT, PAD])
        cacc = at("cacc", 2 * T, shape=[P, 2, T])
        qT = at("qT", HH * T, shape=[P, HH, T])
        kT = at("kT", HH * T, shape=[P, HH, T])
        ktok = at("ktok", HH * T, shape=[P, HH, NC, P])
        vtok = at("vtok", HH * T, shape=[P, HH, NC, P])
        oT = at("oT", KT * T, offset=X_OFF, shape=[P, KT, T])
        gat = at("gat", 6 * 64, shape=[P, 6, NC, 16])
        D_OFF = base[0]
        J = 2 * HH
        en = at("en", J * P, shape=[P, J, P])
        et = at("et", J * P, shape=[P, J, P])
        lc = at("lc", J * W64, shape=[P, J, W64])
        ls = at("ls", 2 * J * W64, shape=[P, 2, J, W64])
        tb = at("tb", J * W64, shape=[P, J, W64])
        ub = at("ub", J * W64, shape=[P, J, W64])
        yb = at("yb", J * W64, shape=[P, J, W64])
        kb = at("kb", J * P, shape=[P, J, P])
        bv = at("bv", J * P, shape=[P, J, P])
        kt = at("kt", J * P, shape=[P, J, P])
        st = at("st", J * P, shape=[P, J, P])
        qd = at("qd", J * P, shape=[P, J, P])
        xin = at("xin", KT * T, offset=D_OFF, shape=[P, KT, T])
        praw = at("praw", 2 * T, offset=D_OFF + 16384, shape=[P, 2, T])
        p_hi = at("p_hi", 2 * T, F32R, offset=D_OFF + 20480, shape=[P, 2, T])
        p_lo = at("p_lo", 2 * T, F32R, offset=D_OFF + 24576, shape=[P, 2, T])
        ptile = at("ptile", KT * T, offset=R_OFF + KT * PAD * 4 + 4096, shape=[P, KT, T])
        pad = at("pad", 3 * (T + 4), offset=D_OFF, shape=[P, 3, T + 4])
        sacc = at("sacc", 6 * T, offset=D_OFF + 8192, shape=[P, 2, 3, T])
        l2r = at("l2r", 2 * T, offset=D_OFF + 8192 + 12288, shape=[P, 2, T])
        ya = at("ya", KT * T, offset=R_OFF, shape=[P, KT, T])
        yb_hi = at("yb_hi", KT * T, F32R, offset=D_OFF, shape=[P, KT, T])
        yb_lo = at("yb_lo", KT * T, F32R, offset=D_OFF + 16384, shape=[P, KT, T])
        gst = at("gst", 2 * T, offset=D_OFF + 32768, shape=[P, 2, T])
        base[0] = R_OFF
        h_hi = at("h_hi", FT * T, F32R, shape=[P, FT, T])
        h_lo = at("h_lo", FT * T, F32R, shape=[P, FT, T])
        pl = at("pl", KT * T, offset=R_OFF, shape=[P, KT, T])
        hb = at("hb", KT * T, offset=A_OFF, shape=[P, KT, T])

        rcos = at("rcos", T)
        rsin = at("rsin", T)
        rpos = at("rpos", T, mybir.dt.int32)
        base[0] = R_OFF
        PW = 16
        c2 = at("c2", P + 2 * P + 4 * 16 + PT_ * P)
        perm, band = c2[:, 0:P], c2[:, P:3 * P]
        edge = c2[:, 3 * P:3 * P + 64].rearrange("p (g t) -> p g t", g=4)
        wpool = c2[:, 3 * P + 64:].rearrange("p (g d) -> p g d", g=4)
        Q_OFF = base[0]
        zq = at("zq", 5 * T, shape=[P, 5, T])
        kz = at("kz", 2 * T, shape=[P, 2, T])
        qk2 = at("qk2", 4 * T, shape=[P, 4, T])
        rt = at("rt", 2 * T, shape=[P, 2, T])
        zv = at("zv", T)
        vt2 = at("vt2", T, shape=[P, NB, P])
        up = at("up", PT_ * (PW + T), shape=[P, PT_, PW + T])
        win = at("win", 2 * (PW + T), shape=[P, 2, PW + T])
        wd = at("wd", PT_ * T, shape=[P, PT_, T])
        mo = at("mo", KT * T, shape=[P, KT, T])
        sm = at("sm", 3 * T, shape=[P, 3, 2, 2 * P])
        ptb = at("ptb", 2 * T, shape=[P, 2, 2, 2, P])
        sml = at("sml", 5 * 32, shape=[P, 5, 16, 2])
        nsink = at("nsink", 8, shape=[P, 4, 2])
        hb2 = at("hb2", KT * T, offset=Q_OFF, shape=[P, KT, T])

        pg = ctx.enter_context(nc.psum_tensor("pg", [P, 2, T], F32))
        pA = ctx.enter_context(nc.psum_tensor("pA", [P, J, P], F32))
        pB = ctx.enter_context(nc.psum_tensor("pB", [P, J, P], F32))
        pC = ctx.enter_context(nc.psum_tensor("pC", [P, J, P], F32))
        c0 = pC[:, 0:HH, :].rearrange("p (j a) b -> p (j a b)", a=1).rearrange("p (j c) -> p j c", c=W64)
        c1 = pC[:, HH:J, :].rearrange("p (j a) b -> p (j a b)", a=1).rearrange("p (j c) -> p j c", c=W64)

        spill_g = nc.dram_tensor("spill_g", [16, P, T], F32, kind="Internal").ap()
        spill_z = nc.dram_tensor("spill_z", [H, P, T], F32, kind="Internal").ap()
        spill_p = nc.dram_tensor("spill_p", [KT, P, T], F32, kind="Internal").ap()

        U = Units()
        for i in range(4):
            U.add(("pl", i), a["w_plp"][i], 4 * P)
        for t in range(KT):
            U.add(("glb", t), a["w_in"][KT + t], KT * P)
            U.add(("gla", t), a["w_in"][t], KT * P)
        U.add(("ab",), a["w_ab"], KT * 32)

        def qkv_units(half):
            for h in range(HH * half, HH * half + HH):
                for i in range(3):
                    U.add(("qkv", 3 * h + i), a["w_in"][(2 + i) * KT + h], KT * P)

        qkv_units(0)
        for i in range(16):
            U.add(("gate", i), a["w_in"][6 * KT + i], KT * P)
        qkv_units(1)
        for i in range(8):
            U.add(("z", i), a["w_in"][5 * KT + i], KT * P)
        for nm in ("co", "do", "wo"):
            for i in range(KT):
                U.add((nm, i), a["w_" + nm][i], KT * P)

        def ffn_units(f):
            for m in range(FT):
                U.add(("fg" + f, m), a["w_gu" + f][m], KT * P)
                U.add(("fu" + f, m), a["w_gu" + f][FT + m], KT * P)
            for m in range(KT):
                for i in range(2):
                    U.add(("fd" + f, 2 * m + i), a["w_dn" + f][m, i], KH * P)

        MIX = [("mk", 0), ("mv", 0), ("mq", 0), ("mq", 1), ("mq", 2), ("mu", 3), ("mq", 3),
               ("mu", 2), ("mu", 1), ("mu", 0)]
        MFILL = MIX[5:]
        COL = {"mu": 0, "mq": 4, "mk": 8, "mv": 9}

        ffn_units("0")
        for i in range(KT):
            U.add(("pg", i), a["w_pg"][i], KT * P)
        ffn_units("1")
        for key in MIX:
            U.add(key, a["w_in2"][COL[key[0]] + key[1]], KT * P)
        for i in range(KT):
            U.add(("mo", i), a["w_out2"][i], KT * P)
        ffn_units("2")
        N_UNITS = len(U.src)

        O = Outs()
        AUX = {}

        def aux(key, reader):
            O.add(key, reader)
            AUX[key] = len(AUX)

        for t in range(KT):
            O.add(("pl", t), "A")
        aux(("n", 0), "A")
        for t in range(KT):
            O.add(("glb", t), "A")
            O.add(("gla", t), "D")
            if t == 1:
                aux(("n", 1), "A")
        O.add(("ab",), "D")
        aux(("gc",), "A")

        def qkv_outs(half):
            for hh in range(HH + 1):
                h = HH * half + hh
                if hh < HH:
                    O.add(("qkv", 3 * h), "A")
                if hh:
                    aux(("l2", h - 1, 0), "A")
                    aux(("l2", h - 1, 1), "A")
                if hh < HH:
                    O.add(("qkv", 3 * h + 1), "A")
                    O.add(("qkv", 3 * h + 2), "A")
                if hh:
                    aux(("tr", h - 1, 0), "A")
                    aux(("tr", h - 1, 1), "A")

        qkv_outs(0)
        for i in range(16):
            O.add(("gate", i), "A")
        qkv_outs(1)
        aux(("mean",), "A")
        for i in range(4):
            O.add(("z", i), "A")
        aux(("var",), "A")
        for i in range(4, 8):
            O.add(("z", i), "A")
        for i in range(8):
            O.add(("co", i), "D")
        for h in range(H):
            aux(("on", h), "A")
        for i in range(8):
            O.add(("do", i), "D")
        for i in range(8):
            O.add(("wo", i), "D")

        def ffn_outs(f, nu):
            for m in range(FT):
                O.add(("fg" + f, m), "D")
                if m == 0:
                    aux(("n", nu), "A")
                O.add(("fu" + f, m), "D")
            for m in range(KT):
                O.add(("fd" + f, m), "D" if f == "0" else "A")

        ffn_outs("0", 2)
        for i in range(KT):
            O.add(("pg", i), "D")
            if i == 0:
                aux(("n", 3), "A")
        aux(("n", 4), "A")
        ffn_outs("1", 5)
        aux(("n", 6), "A")
        MAUX = {2: [("rp", 3)], 8: [("rp", 4), ("yp", 3)], 11: [("yp", 2)], 14: [("yp", 1)]}
        O.add(("mk", 0), "D")
        aux(("n", 7), "A")
        O.add(("mv", 0), "D")
        O.add(("mq", 0), "D")
        aux(("rp", 0), "D")
        aux(("vt",), "A")
        O.add(("mq", 1), "D")
        aux(("rp", 1), "D")
        O.add(("mq", 2), "D")
        aux(("rp", 2), "D")
        for i, key in enumerate(MFILL):
            O.add(key, "D")
            for k in MAUX.get(3 * i + 2, []):
                aux(k, "D" if k[0] == "rp" else "A")
        aux(("yp", 0), "A")
        aux(("n", 8), "A")
        aux(("n", 9), "A")
        for i in range(KT):
            O.add(("mo", i), "A")
        aux(("n", 10), "A")
        ffn_outs("2", 11)
        aux(("n", 12), "A")

        NORMS = [KT] * 8 + [PT_] * 2 + [KT] * 3
        SQ = [sum(NORMS[:i]) for i in range(len(NORMS))]
        AD = [sum(NORMS[:i]) - i for i in range(len(NORMS))]

        TAPS = [(2 * pr + i, j) for pr in range(KT // 2) for j in range(CK) for i in range(2)]
        taps_unit, taps_gap = 12, 4

        def cslot(t):
            return cacc[:, t, :] if t < 2 else cpad[:, t - 2, 0:T]

        def wait(eng, name, value):
            if not isinstance(value, int) or value > 0:
                eng.wait_ge(S(name), value)

        def ev_wait(eng, key):
            o = O.at[key]
            eng.wait_ge(S("ev" + O.reader[o]), O.count(o))

        def unit_out(eng, key, n=None):
            eng.wait_ge(S("gemm"), (U.at[key] if n is None else n) + 1)

        def aux_out(eng, key):
            eng.wait_ge(S("aux"), AUX[key] + 1)

        def bank(key):
            return pg[:, O.at[key] % 2, :]

        def quad(ap, n=HH):
            return ap.rearrange("p (n c) -> p n c", n=n)

        pa2 = pA[:, :, :].rearrange("p (b h k) c -> p b h (k c)", b=2, h=2)
        pb2 = pB[:, :, :].rearrange("p (b h k) c -> p b h k c", b=2, h=2)
        pc2 = pC[:, :, :].rearrange("p (b k) c -> p b (k c)", b=2)

        def chunk(d, r):
            return r if d == 0 else NC - 1 - r

        def filler(R):
            name, i = (("gate", 4 * R) if R < 4 else ("z", 4 * (R - 4)) if R < 6 else ("co", 4 * (R - 6)))
            return [(name, i + f) for f in range(4)]

        tmps = (tmp1, tmp2)
        SETS = ["h", "conv", "o", "ffn0", "pg", "ffn1", "mix", "out", "ffn2"]

        def set_count(s, t):
            return SETS.index(s) * KT + t + 1

        block = ctx.enter_context(nc.Block())

        @block.sync
        def _(sp):
            def load(n, src=None, i=0):
                if not (isinstance(i, int) and n < 4):
                    sp.wait_ge(S("w_lo"), n - 3 + 4 * i)
                sp.dma_start(w_raw[:, n % 4, 0:U.cols[n]], U.src[n] if src is None else src)\
                    .then_inc(S(f"w_in{n % 4}"), 16)

            def side(t, src, ready):
                sp.wait_ge(S(ready[0]), ready[1])
                sp.dma_start(tmps[t % 2][:], src).then_inc(S(f"side{t % 2}"), 16)

            def ev(key):
                return ("ev" + O.reader[O.at[key]], O.count(O.at[key]))

            sp.dma_start(praw[:], a["p"]).then_inc(S("in_p"), 16)
            load(0)
            sp.dma_start(xin[:], a["x"]).then_inc(S("in_x"), 16)
            sp.dma_start(consts[:], a["consts"]).then_inc(S("in_c"), 16)
            sp.dma_start(vec[:], a["vec"]).then_inc(S("in_v"), 16)
            load(1)
            sp.dma_start(swt[:], a["swt"]).then_inc(S("in_s"), 16)
            sp.dma_start(gate_p[:], a["gate_p"]).then_inc(S("in_g"), 16)
            for n in range(2, U.at[("fg0", 0)] + 4):
                for t in range(KT):
                    if n == U.at[("co", max(t - 1, 0))] + 4:
                        if t < 2:
                            sp.wait_ge(S(f"spill{t}"), 16 * 12)
                        side(t, spill_g[t], ("spill1", 16 * 12) if t < 2 else ev(("co", t - 2)))
                    if n == U.at[("do", 0)] + 4:
                        side(t, spill_z[t], ev(("co", 6 + t)) if t < 2 else ("on_z", t - 1))
                    if n == U.at[("do", max(t - 1, 0))] + 4:
                        if t < 2:
                            sp.wait_ge(S("s_upd"), 6)
                            sp.wait_ge(S("o_acc"), 8)
                        else:
                            sp.wait_ge(S("yv"), t - 1)
                        sp.dma_start(gst[:, t % 2], spill_g[KT + t]).then_inc(S(f"sgb{t % 2}"), 16)
                    if n == U.at[("wo", max(t - 1, 0))] + 4:
                        side(t, a["x"][:, t], ("on_z", 7 + t) if t < 2 else ev(("wo", t - 2)))
                load(n)
                if n == U.at[("glb", 5)]:
                    sp.wait_ge(S("plf"), KT)
                    sp.dma_start(spill_p.rearrange("t p n -> p t n"), ptile[:]).then_inc(S("spp"), 16)

            def ffn(f, more):
                g0 = U.at[("fg" + f, 0)]
                with sp.Fori(1, FT // 2) as i:
                    for j in range(4):
                        at_ = bass.ds(2 * i + (j // 2 + (j % 2) * FT), 1)
                        load(g0 + j, a["w_gu" + f][at_].rearrange("a p c -> (a p) c"), i)
                for n in range(U.at[("fd" + f, 0)], more):
                    if n == U.at[("pg", 0)] + 2:
                        unit_out(sp, ("fd0", 2 * KT - 1))
                        sp.dma_start(pl[:], spill_p.rearrange("t p n -> p t n")).then_inc(S("in_pl"), 16)
                    if n == U.at[("mk", 0)] + 3:
                        unit_out(sp, ("fd1", 2 * KT - 1))
                        sp.dma_start(c2[:], a["c2"]).then_inc(S("in_c2"), 16)
                    load(n)

            sp.dma_start(rpos[:], a["pos"]).then_inc(S("in_r"), 16)
            ffn("0", U.at[("fg1", 0)] + 4)
            ffn("1", U.at[("fg2", 0)] + 4)
            ffn("2", N_UNITS)
            for t in range(KT):
                sp.wait_ge(S("xu"), 2 * KT + t + 1)
                sp.dma_start(out[t], x[:, t]).then_inc(S("out"), 16)
            sp.wait_ge(S("out"), 16 * KT)

        @block.tensor
        def _(pe):
            def begin(key):
                o = O.at[key]
                if o >= 2:
                    q = o - 2
                    pe.wait_ge(S("ev" + O.reader[q]), O.count(q))
                return pg[:, o % 2, :]

            def products(n, act, k_n, dst, w_of, part=None, first=True, last=True, i=0):
                hi, lo = act
                todo = [(k, w, b) for k in range(k_n) for w, b in ((w_hi, hi), (w_hi, lo), (w_lo, hi))]
                size = len(todo) if part is None else len(todo) // 3
                at0 = 0 if part is None else part * size
                for q in range(at0, at0 + size):
                    k, w, b = todo[q]
                    ins = pe.matmul(dst, w_of(w, n % 2, k), b(k), start=first and q == 0,
                                    stop=last and q == len(todo) - 1)
                return ins

            def w_tile(w, slot, k):
                return w[:, slot, k * P:(k + 1) * P]

            def act_a(k0=0):
                return (lambda k: a_hi[:, k0 + k, :]), (lambda k: a_lo[:, k0 + k, :])

            def unit(key, act=None, k_n=KT, part=None, dst=None, first=True, last=True, i=0):
                n = U.at[key]
                if part in (None, 0):
                    pe.wait_ge(S("w_lo"), n + 1 + 4 * i)
                    if dst is None:
                        begin(key)
                ins = products(n, act or act_a(), k_n, bank(key) if dst is None else dst, w_tile, part,
                               first, last)
                if part in (None, 2):
                    ins.then_inc(S("gemm"), 1)

            def column_sums(key, src, lhs=ones):
                pe.matmul(begin(key), lhs, src, start=True, stop=True).then_inc(S("aux"), 1)

            pe.wait_ge(S("p_lo"), 1)
            for n in range(4):
                pe.wait_ge(S("w_lo"), n + 1)
                for q in range(2):
                    dst = begin(("pl", 2 * n + q))
                    ins = products(n, ((lambda k: p_hi[:, k, :]), (lambda k: p_lo[:, k, :])), 2, dst,
                                   lambda w, s, k: w[:, s, (2 * q + k) * P:(2 * q + k + 1) * P])
                ins.then_inc(S("gemm"), 1)
            pe.wait_ge(S("in_c"), 16)
            pe.wait_ge(S("add"), AD[0] + KT - 1)
            column_sums(("n", 0), acc[:])
            pe.wait_ge(S("a_lo"), set_count("h", KT - 1))
            for t in range(KT):
                unit(("glb", t))
                unit(("gla", t))
                if t == 1:
                    pe.wait_ge(S("add"), AD[1] + KT - 1)
                    column_sums(("n", 1), acc[:])
            n = U.at[("ab",)]
            pe.wait_ge(S("w_lo"), n + 1)
            dst = begin(("ab",))
            for c in range(NC):
                tok = slice(c * P, (c + 1) * P)
                for k in range(KT):
                    for p_, (b, w) in enumerate(((a_hi, w_hi), (a_lo, w_hi), (a_hi, w_lo))):
                        ins = pe.matmul(dst[:, c * 32:(c + 1) * 32], b[:, k, tok],
                                        w[:, n % 2, k * 32:(k + 1) * 32],
                                        start=k == 0 and p_ == 0, stop=k == KT - 1 and p_ == 2)
            ins.then_inc(S("gemm"), 1)
            pe.wait_ge(S("g_raw"), 1)
            dst = begin(("gc",))
            for d in range(2):
                pe.matmul(quad(dst[:, 0:64], NC)[:, :, d * 8:d * 8 + 8], tri[d], gat[:, 0, :, d * 8:d * 8 + 8],
                          start=True, stop=True)
            pe.matmul(quad(dst[:, 64:128], NC), ones, gat[:, 0], start=True, stop=True).then_inc(S("aux"), 1)

            def qkv(half):
                for hh in range(HH + 1):
                    h = HH * half + hh
                    if hh < HH:
                        unit(("qkv", 3 * h))
                    if hh:
                        for i in range(2):
                            pe.wait_ge(S("l2sq"), 2 * (h - 1) + i + 1)
                            column_sums(("l2", h - 1, i), sq[:, i, :])
                    if hh < HH:
                        unit(("qkv", 3 * h + 1))
                        unit(("qkv", 3 * h + 2))
                    if hh:
                        pe.wait_ge(S("qk_fin"), 2 * h)
                        dst = begin(("tr", h - 1, 0))
                        for c in range(NC):
                            ins = pe.transpose(dst[:, c * P:(c + 1) * P], kT[:, hh - 1, c * P:(c + 1) * P], ident)
                        ins.then_inc(S("aux"), 1)
                        pe.wait_ge(S("silu"), 3 * h)
                        dst = begin(("tr", h - 1, 1))
                        for c in range(NC):
                            ins = pe.transpose(dst[:, c * P:(c + 1) * P],
                                               sacc[:, (h - 1) % 2, 2, c * P:(c + 1) * P], ident)
                        ins.then_inc(S("aux"), 1)

            def gap(R, g):
                unit(filler(R)[g // 3], part=g % 3)

            halves = (slice(0, W64), slice(W64, P))

            def small(dst, lhs, rhs):
                for j in range(J):
                    for s in halves:
                        ins = pe.matmul(dst[s, j, :], lhs[s, j, :], rhs[s, j, :] if rhs is not None else id64[s, :],
                                        start=True, stop=True)
                return ins

            def delta(R):
                half, r = divmod(R, NC)
                prob = [(j, j // HH, j % HH, chunk(j // HH, r)) for j in range(J)]
                wait(pe, "g_all", 1)
                wait(pe, "o_acc", R)
                for j, d, hh, c in prob:
                    g_col = gat[:, 0, c, d * 8 + HH * half + hh:d * 8 + HH * half + hh + 1]
                    ins = pe.matmul(pA[:, j, :], g_col.to_broadcast([P, P]), tri[d], start=True, stop=True)
                ins.then_inc(S("grow"), 1)
                for j, d, hh, c in prob:
                    tok = slice(c * P, (c + 1) * P)
                    ins = pe.matmul(pB[:, j, :], kT[:, hh, tok], kT[:, hh, tok], start=True, stop=True)
                ins.then_inc(S("gram"), 1)
                gap(R, 0)
                pe.wait_ge(S("eg"), R + 1)
                for j, d, hh, c in prob:
                    tok = slice(c * P, (c + 1) * P)
                    ins = pe.matmul(pA[:, j, :], kT[:, hh, tok], qT[:, hh, tok], start=True, stop=True)
                ins.then_inc(S("kq"), 1)
                gap(R, 1)
                for lv in range(LEVELS):
                    pe.wait_ge(S("ls"), LEVELS * R + lv + 1)
                    if lv == 0:
                        wait(pe, "s_upd", (NC - 1) * half + r)
                        small(c0, ls[:, 0], None).then_inc(S("y"), 1)
                        continue
                    pe.wait_ge(S("t_upd"), LEVELS * R + lv)
                    small(c0, ls[:, lv % 2], ub).then_inc(S("y"), 1)
                    gap(R, 2 * lv)
                    pe.wait_ge(S("ycp"), LEVELS * R + lv)
                    small(c1, tb, yb).then_inc(S("uy"), 1)
                    small(c0, yb, tb).then_inc(S("yt"), 1)
                    gap(R, 2 * lv + 1)
                pe.wait_ge(S("t_upd"), LEVELS * (R + 1))
                lo, hi = halves
                for j in range(J):
                    s, b = (hi, lo) if j < HH else (lo, hi)
                    ins = pe.matmul(c0[b, j, :], en[s, j, b], en[s, j, s], start=True, stop=True)
                ins.then_inc(S("yf"), 1)
                pe.wait_ge(S("ycp"), LEVELS * (R + 1))
                for j in range(J):
                    b = lo if j < HH else hi
                    ins = pe.matmul(c1[b, j, :], tb[b, j, :], yb[b, j, :], start=True, stop=True)
                ins.then_inc(S("u12"), 1)
                pe.wait_ge(S("u12s"), R + 1)
                pe.wait_ge(S("kb"), R + 1)
                pe.wait_ge(S("qk"), R + 1)
                for j in range(J):
                    ins = pe.matmul(pA[:, j, :], kb[:, j, :], en[:, j, :], start=True, stop=True)
                ins.then_inc(S("wt"), 1)
                pe.wait_ge(S("bv"), R + 1)
                pe.wait_ge(S("wtcp"), R + 1)
                wait(pe, "s_upd", (NC - 1) * half + r)
                for j in range(J):
                    ins = pe.matmul(pB[:, j, :], en[:, j, :], bv[:, j, :], start=True, stop=r == 0)
                    if r:
                        ins = pe.matmul(pB[:, j, :], kb[:, j, :], st[:, j, :], start=False, stop=True)
                ins.then_inc(S("vn"), 1)
                pe.wait_ge(S("vcp"), R + 1)
                pe.wait_ge(S("qdm"), R + 1)
                for j in range(J):
                    if r:
                        pe.matmul(pA[:, j, :], st[:, j, :], qd[:, j, :], start=True, stop=False)
                    ins = pe.matmul(pA[:, j, :], bv[:, j, :], et[:, j, :], start=r == 0, stop=True)
                ins.then_inc(S("o"), 1)
                if r < NC - 1:
                    pe.wait_ge(S("kt"), R + 1)
                    for j in range(J):
                        ins = pe.matmul(pC[:, j, :], kt[:, j, :], bv[:, j, :], start=True, stop=True)
                    ins.then_inc(S("s"), 1)

            qkv(0)
            for R in range(4):
                delta(R)
            qkv(1)
            pe.wait_ge(S("csum"), KT - 1)
            column_sums(("mean",), acc[:])
            delta(4)
            pe.wait_ge(S("cva"), KT - 1)
            column_sums(("var",), rstd[:])
            delta(5)
            pe.wait_ge(S("a_lo"), set_count("conv", KT - 1))
            delta(6)
            delta(7)
            for h in range(H):
                pe.wait_ge(S("onsq"), h + 1)
                column_sums(("on", h), sq[:, h % 2, :])
            pe.wait_ge(S("a_lo"), set_count("o", KT - 1))
            for t in range(KT):
                unit(("do", t))
            pe.wait_ge(S("yb_lo"), KT)
            for t in range(KT):
                unit(("wo", t), ((lambda k: yb_hi[:, k, :]), (lambda k: yb_lo[:, k, :])))

            def norm(nu, key=None):
                pe.wait_ge(S("add"), AD[nu] + KT - 1)
                column_sums(("n", nu), acc[:])

            def ffn(f, nu, s):
                pe.wait_ge(S("a_lo"), set_count(s, KT - 1))

                def step(i):
                    for j in range(4):
                        nm = ("fg" if j % 2 == 0 else "fu") + f
                        n = U.at[(nm, j // 2)] + 4 * i
                        pe.wait_ge(S("w_lo"), n + 1)
                        if isinstance(i, int):
                            dst = begin((nm, 2 * i + j // 2))
                        else:
                            o = O.at[(nm, 2 + j // 2)]
                            pe.wait_ge(S("evD"), O.count(o - 2) - 4 + 4 * i)
                            dst = pg[:, o % 2, :]
                        products(U.at[(nm, j // 2)], act_a(), KT, dst, w_tile).then_inc(S("gemm"), 1)
                        if isinstance(i, int) and i == 0 and j == 0:
                            norm(nu)

                step(0)
                with pe.Fori(1, FT // 2) as i:
                    step(i)
                pe.wait_ge(S("h_lo"), FT * (1 + int(f)))
                for m in range(KT):
                    dst = begin(("fd" + f, m))
                    for q in range(2):
                        n = U.at[("fd" + f, 2 * m + q)]
                        pe.wait_ge(S("w_lo"), n + 1)
                        products(n, ((lambda k: h_hi[:, KH * q + k, :]), (lambda k: h_lo[:, KH * q + k, :])),
                                 KH, dst, w_tile, None, q == 0, q == 1).then_inc(S("gemm"), 1)

            ffn("0", 2, "ffn0")
            pe.wait_ge(S("a_lo"), set_count("pg", KT - 1))
            for t in range(KT):
                unit(("pg", t))
                if t == 0:
                    norm(3)
            norm(4)
            ffn("1", 5, "ffn1")
            norm(6)
            pe.wait_ge(S("a_lo"), set_count("mix", KT - 1))

            def rotate(i):
                if i == 0:
                    pe.wait_ge(S("in_c2"), 16)
                ev_wait(pe, ("mq", i - 1) if i else ("mk", 0))
                column_sums(("rp", i), zq[:, i], perm)

            def pooled(g):
                pe.wait_ge(S("wd"), PT_ - g)
                column_sums(("yp", g), wd[:, g], wpool[:, g])

            unit(("mk", 0))
            norm(7)
            unit(("mv", 0))
            unit(("mq", 0))
            rotate(0)
            ev_wait(pe, ("mv", 0))
            dst = begin(("vt",))
            for c in range(NB):
                ins = pe.transpose(dst[:, c * P:(c + 1) * P], zv[:, c * P:(c + 1) * P], ident)
            ins.then_inc(S("aux"), 1)
            unit(("mq", 1))
            rotate(1)
            unit(("mq", 2))
            rotate(2)
            heads = (slice(0, HD2), slice(HD2, P))

            def scores(s):
                i, n = divmod(s, NB)
                pe.wait_ge(S("qk2"), i + 2)
                wait(pe, "smask", s - 1)
                k0 = 1 if n == 0 else 0
                pe.matmul(pa2[:, s % 2, :, k0 * P:2 * P], qk2[:, i, n * P:(n + 1) * P],
                          kz[:, :, (n - 1 + k0) * P:(n + 1) * P], start=True, stop=True).then_inc(S("scores"), 1)

            def turn(s):
                k0 = 1 if s % NB == 0 else 0
                pe.wait_ge(S("prob"), s + 1)
                wait(pe, "ptcp", s - 1)
                for h in range(2):
                    for kb_ in range(k0, 2):
                        ins = pe.transpose(pb2[:, s % 2, h, kb_, :], sm[:, s % 3, h, kb_ * P:(kb_ + 1) * P], ident)
                ins.then_inc(S("turn"), 1)

            def values(s):
                i, n = divmod(s, NB)
                k0 = 1 if n == 0 else 0
                pe.wait_ge(S("ptcp"), s + 1)
                if s == 0:
                    ev_wait(pe, ("vt",))
                if n == 0:
                    wait(pe, "oat", i - 1)
                for h in range(2):
                    for kb_ in range(k0, 2):
                        ins = pe.matmul(pc2[heads[h], i % 2, n * P:(n + 1) * P],
                                        vt2[:, n - 1 + kb_, heads[h]], ptb[:, s % 2, h, kb_, :],
                                        start=kb_ == k0, stop=kb_ == 1)
                ins.then_inc(S("values"), 1)

            for s in range(16 + 3):
                if s < 16:
                    scores(s)
                if 0 <= s - 2 < 16:
                    turn(s - 2)
                if 0 <= s - 3 < 16:
                    values(s - 3)
                if s < 15:
                    unit(MFILL[s // 3], part=s % 3)
                for k in MAUX.get(s, []):
                    (rotate if k[0] == "rp" else pooled)(k[1])
            pooled(0)

            def norm4(nu):
                pe.wait_ge(S("add"), AD[nu] + PT_ - 1)
                column_sums(("n", nu), acc[:])

            norm4(8)
            norm4(9)
            pe.wait_ge(S("a_lo"), set_count("out", KT - 1))
            for t in range(KT):
                unit(("mo", t))
            norm(10)
            ffn("2", 11, "ffn2")
            norm(12)

        @block.scalar
        def _(act):
            def hi(n, i=0, cols=None):
                act.wait_ge(S(f"w_in{n % 4}"), 16 * (n // 4 + 1) + 16 * i)
                if not (isinstance(i, int) and n < 2):
                    act.wait_ge(S("gemm"), n - 1 + 4 * i)
                c = U.cols[n] if cols is None else cols
                act.activation(w_hi[:, n % 2, 0:c], w_raw[:, n % 4, 0:c], ACT.Copy).then_inc(S("w_hi"), 1)

            def after(key):
                n = U.at[key]
                unit_out(act, key)
                if n + 2 < N_UNITS:
                    hi(n + 2)

            def square(nu, t, src):
                if t == 0:
                    wait(act, "recip", nu)
                    dst = acc[:]
                else:
                    wait(act, "add", AD[nu] + t - 2 if t > 2 else 0)
                    dst = sq[:, t % 2, :]
                act.activation(dst, src, ACT.Square).then_inc(S("sq"), 1)

            def root(nu):
                aux_out(act, ("n", nu))
                act.activation(acc[:], bank(("n", nu)), ACT.Sqrt, scale=1.0 / (P * NORMS[nu]), bias=eps_t[:, 0:1])\
                    .then_inc(S("evA"), 1)

            def high_o(h):
                act.wait_ge(S("on_z"), h + 1)
                act.activation(a_hi[:, h], oT[:, h], ACT.Copy).then_inc(S("a_hi"), 1)

            def root_o(h):
                aux_out(act, ("on", h))
                if h >= 2:
                    act.wait_ge(S("on_g"), h - 1)
                act.activation((acc, rstd)[h % 2][:], bank(("on", h)), ACT.Sqrt, scale=1.0 / P,
                               bias=eps_t[:, 0:1]).then_inc(S("evA"), 1)

            act.wait_ge(S("in_p"), 16)
            act.activation(p_hi[:], praw[:], ACT.Copy).then_inc(S("p_hi"), 1)
            hi(0)
            hi(1)
            act.wait_ge(S("in_x"), 16)
            for t in range(KT):
                square(0, t, xin[:, t])
            for n in range(4):
                after(("pl", n))
                for q in range(2):
                    t = 2 * n + q
                    act.activation(ptile[:, t], bank(("pl", t)), ACT.Copy).then_inc(S("evA"), 1)
            act.wait_ge(S("in_g"), 16)
            root(0)
            for t in range(KT):
                act.wait_ge(S("hx"), t + 1)
                act.activation(a_hi[:, t], xin[:, t], ACT.Copy).then_inc(S("a_hi"), 1)
            act.wait_ge(S("evA"), 9)
            for t in range(KT):
                square(1, t, ptile[:, t])
            for t in range(KT):
                after(("glb", t))
                if t >= 2:
                    ev_wait(act, ("gla", t - 2))
                act.activation(tmps[t % 2][:], bank(("glb", t)), ACT.Sigmoid).then_inc(S("evA"), 1)
                after(("gla", t))
                if t == 1:
                    root(1)
            after(("ab",))
            act.wait_ge(S("in_g"), 16)
            act.activation(gat[:, 5, 0, :], gate_p[:, 0:16], ACT.Exp).then_inc(S("gA"), 1)
            act.wait_ge(S("gD"), 1)
            act.activation(gat[:, 2], gat[:, 3], ACT.Exp).then_inc(S("gA"), 1)
            act.wait_ge(S("gA"), 2)
            act.activation(gat[:, 4], gat[:, 2], ACT.Ln, bias=1.0).then_inc(S("gA"), 1)
            ev_wait(act, ("ab",))
            act.activation(gat[:, 1], gat[:, 1], ACT.Sigmoid).then_inc(S("gA"), 1)
            aux_out(act, ("gc",))
            b = bank(("gc",))
            act.activation(gat[:, 2], quad(b[:, 0:64], NC), ACT.Copy).then_inc(S("gA"), 1)
            act.activation(gat[:, 4], quad(b[:, 64:128], NC), ACT.Copy).then_inc(S("evA"), 1)
            act.wait_ge(S("gA"), 5)
            act.activation(gat[:, 3], gat[:, 2], ACT.Exp).then_inc(S("gA"), 1)
            ev_wait(act, ("gc",))
            act.activation(gat[:, 5], gat[:, 4], ACT.Exp).then_inc(S("gA"), 1)
            act.wait_ge(S("gD"), 3)
            act.activation(gat[:, 4], gat[:, 4], ACT.Exp).then_inc(S("g_all"), 1)

            def qkv(half):
                def padded(h, i):
                    key = ("qkv", 3 * h + i)
                    after(key)
                    if h == 0 and i == 0:
                        act.wait_ge(S("a_lo"), KT)
                        act.wait_ge(S("spp"), 16)
                    wait(act, "stap", SK * (3 * (h - 1) + i + 1))
                    act.activation(pad[:, i, SP_:SP_ + T], bank(key), ACT.Copy).then_inc(S("evA"), 1)

                def silu(h, i):
                    act.wait_ge(S("stap"), SK * (3 * h + i + 1))
                    y = sacc[:, h % 2, i]
                    act.activation(y, y, ACT.Silu).then_inc(S("silu"), 1)
                    if i < 2:
                        act.wait_ge(S("silu"), 3 * h + i + 1)
                        if h:
                            aux_out(act, ("l2", h - 1, i))
                        act.activation(sq[:, i, :], y, ACT.Square).then_inc(S("l2sq"), 1)

                for hh in range(HH + 1):
                    h = HH * half + hh
                    if hh < HH:
                        if hh == 0 and half:
                            act.wait_ge(S("o"), 4)
                            act.wait_ge(S("s_upd"), 3)
                        padded(h, 0)
                    if hh:
                        silu(h - 1, 2)
                        for i, s in enumerate((float(P), 1.0)):
                            aux_out(act, ("l2", h - 1, i))
                            wait(act, "qk_fin", 2 * (h - 2) + i + 1)
                            act.activation(l2r[:, i, :], bank(("l2", h - 1, i)), ACT.Sqrt, scale=s,
                                           bias=eps_t[:, 1 + i:2 + i]).then_inc(S("evA"), 1)
                    if hh < HH:
                        padded(h, 1)
                        silu(h, 0)
                        padded(h, 2)
                        silu(h, 1)
                    if hh:
                        if half and hh == 1:
                            act.wait_ge(S("bv"), 4)
                            act.wait_ge(S("kb"), 4)
                            act.wait_ge(S("kt"), 4)
                        for i, dst in enumerate((ktok, vtok)):
                            aux_out(act, ("tr", h - 1, i))
                            act.activation(dst[:, hh - 1], quad(bank(("tr", h - 1, i)), NC), ACT.Copy)\
                                .then_inc(S("evA"), 1)

            spilled = [0]

            def gap(R, g):
                if g % 3 != 2:
                    return
                key = filler(R)[g // 3]
                after(key)
                if key[0] == "co":
                    return
                k = spilled[0]
                spilled[0] += 1
                if k >= 2:
                    act.wait_ge(S(f"spill{k % 2}"), 16 * (k // 2))
                else:
                    ev_wait(act, ("gla", 6 + k))
                func, dst = (ACT.Sigmoid, spill_g[key[1]]) if key[0] == "gate" else (ACT.Silu, spill_z[key[1]])
                act.activation(tmps[k % 2][:], bank(key), func).then_inc(S("evA"), 1)
                ev_wait(act, key)
                act.dma_start(dst, tmps[k % 2][:]).then_inc(S(f"spill{k % 2}"), 16)

            lo, hi_ = slice(0, W64), slice(W64, P)

            def delta(R):
                half, r = divmod(R, NC)
                act.wait_ge(S("pre"), 2 * R + 1)
                act.activation(en[:], en[:], ACT.Exp, scale=-1.0).then_inc(S("en"), 1)
                act.wait_ge(S("pre"), 2 * R + 2)
                act.activation(et[:], et[:], ACT.Exp).then_inc(S("et"), 1)
                wait(act, "o", R)
                act.activation(qd[:], pA[:], ACT.Exp).then_inc(S("eg"), 1)
                act.wait_ge(S("L"), R + 1)
                wait(act, "ls", LEVELS * R)
                act.activation(lc[lo], en[lo, :, lo], ACT.Copy)
                act.activation(lc[hi_], en[hi_, :, hi_], ACT.Copy).then_inc(S("lc"), 1)
                gap(R, 0)
                gap(R, 1)
                for lv in range(1, LEVELS):
                    act.wait_ge(S("y"), LEVELS * R + lv + 1)
                    act.activation(yb[:], c0, ACT.Copy).then_inc(S("ycp"), 1)
                    gap(R, 2 * lv)
                    gap(R, 2 * lv + 1)
                act.wait_ge(S("yf"), R + 1)
                act.activation(yb[lo, 0:HH], c0[lo, 0:HH], ACT.Copy)
                act.activation(yb[hi_, HH:J], c0[hi_, HH:J], ACT.Copy).then_inc(S("ycp"), 1)
                act.wait_ge(S("wt"), R + 1)
                act.activation(kb[:, 0:HH], pA[:, 0:HH], ACT.Copy, scale=-1.0)
                act.activation(kb[:, HH:J], pA[:, HH:J], ACT.Copy, scale=-1.0).then_inc(S("wtcp"), 1)
                act.wait_ge(S("vn"), R + 1)
                act.activation(bv[:, 0:HH], pB[:, 0:HH], ACT.Copy)
                act.activation(bv[:, HH:J], pB[:, HH:J], ACT.Copy).then_inc(S("vcp"), 1)

            qkv(0)
            for R in range(4):
                delta(R)
            qkv(1)
            aux_out(act, ("mean",))
            act.activation(acc[:], bank(("mean",)), ACT.Copy, scale=1.0 / D).then_inc(S("evA"), 1)
            for t in range(KT):
                act.wait_ge(S("xc"), t + 1)
                if t > 2:
                    act.wait_ge(S("cva"), t - 2)
                act.activation(rstd[:] if t == 0 else sq[:, t % 2, :], cslot(t), ACT.Square).then_inc(S("cvs"), 1)
            delta(4)
            aux_out(act, ("var",))
            act.activation(acc[:], bank(("var",)), ACT.Sqrt, scale=1.0 / D, bias=eps_t[:, 3:4]).then_inc(S("evA"), 1)
            delta(5)
            for t in range(KT):
                act.wait_ge(S("xn"), t + 1)
                act.activation(cslot(t), cslot(t), ACT.Silu, scale=v("ln_g", t), bias=v("ln_b", t))\
                    .then_inc(S("ca"), 1)
            for t in range(KT):
                act.wait_ge(S("ca"), t + 1)
                act.activation(a_hi[:, t], cslot(t), ACT.Copy).then_inc(S("a_hi"), 1)
            delta(6)
            delta(7)
            for h in range(H):
                act.wait_ge(S("o_acc"), 8)
                if h >= 2:
                    aux_out(act, ("on", h - 2))
                act.activation(sq[:, h % 2, :], oT[:, h], ACT.Square).then_inc(S("onsq"), 1)
                if h:
                    root_o(h - 1)
                if h >= 2:
                    high_o(h - 2)
            root_o(H - 1)
            high_o(H - 2)
            high_o(H - 1)
            for t in range(KT):
                after(("do", t))
                act.wait_ge(S("yv"), t + 1)
                act.activation(yb_hi[:, t], ya[:, t], ACT.Copy).then_inc(S("yb_hi"), 1)

            def xset(s, t, g, nu):
                act.activation(a_hi[:, t], x[:, t], ACT.Copy, scale=v(g, t)).then_inc(S("a_hi"), 1)
                square(nu, t, x[:, t])

            for t in range(KT):
                after(("wo", t))
                ev_wait(act, ("wo", t))
                xset("ffn0", t, "g_ffn", 2)

            def ffn(f, nu, g, nu2):
                def step(i):
                    for q in range(2):
                        n = U.at[("fg" + f, q)]
                        act.wait_ge(S("gemm"), n + 1 + 4 * i)
                        hi(n + 2, i, U.cols[n + 2 + (4 * i if isinstance(i, int) else 0)])
                        if q == 0 and isinstance(i, int) and i == 0:
                            root(nu)
                        dg = O.count(O.at[("fg" + f, q)])
                        act.wait_ge(S("evD"), dg + 4 * i)
                        act.activation(tmp1[:], tmp1[:], ACT.Silu).then_inc(S("sil"), 1)
                        act.wait_ge(S("gemm"), n + 2 + 4 * i)
                        hi(n + 3, i, U.cols[n + 3 + (4 * i if isinstance(i, int) else 0)])
                        act.wait_ge(S("hm"), FT * int(f) + q + 1 + 2 * i)
                        m = 2 * i + q
                        act.activation(h_hi[:, m] if isinstance(i, int) else
                                       h_hi[:, bass.ds(m, 1)].rearrange("p a n -> p (a n)"),
                                       tmp2[:], ACT.Copy).then_inc(S("h_hi"), 1)

                step(0)
                with act.Fori(1, FT // 2 - 1) as i:
                    step(i)
                step(FT // 2 - 1)
                if f == "0":
                    rope_tables()
                for m in range(KT):
                    after(("fd" + f, 2 * m))
                    after(("fd" + f, 2 * m + 1))
                    if f == "0":
                        ev_wait(act, ("fd" + f, m))
                        xset("pg", m, g, nu2)
                    else:
                        act.activation(hb[:, m], bank(("fd" + f, m)), ACT.Copy).then_inc(S("evA"), 1)
                        ev_wait(act, ("fd" + f, m))
                        square(nu2, m, hb[:, m])

            def rope_tables():
                act.wait_ge(S("rope"), 1)
                act.activation(rsin[:], rcos[:], ACT.Sin).then_inc(S("rsin"), 1)
                act.wait_ge(S("rsin"), 1)
                act.activation(rcos[:], rpos[:].bitcast(F32), ACT.Sin, scale=-1.0, bias=gate_p[:, 58:59])\
                    .then_inc(S("rsin"), 1)

            ffn("0", 2, "g_pl", 3)
            for t in range(KT):
                after(("pg", t))
                if t == 0:
                    root(3)
                ev_wait(act, ("pg", t))
                act.activation(tmps[t % 2][:], tmps[t % 2][:], ACT.Sigmoid).then_inc(S("pgs"), 1)
                act.wait_ge(S("x2"), t + 1)
                square(4, t, x[:, t])
            root(4)

            for t in range(KT):
                act.wait_ge(S("xf"), t + 1)
                xset("ffn1", t, "ffn1_pre", 5)
            ffn("1", 5, None, 6)

            def post(nu, k, s, g, nu2):
                root(nu)
                if s:
                    for t in range(KT):
                        act.wait_ge(S("xu"), KT * k + t + 1)
                        xset(s, t, g, nu2)

            post(6, 0, "mix", "mix_pre", 7)
            after(("mk", 0))
            root(7)
            after(("mv", 0))
            after(("mq", 0))
            aux_out(act, ("vt",))
            act.activation(vt2[:], quad(bank(("vt",)), NB), ACT.Copy).then_inc(S("evA"), 1)
            after(("mq", 1))
            after(("mq", 2))

            def prob(s):
                k0 = P if s % NB == 0 else 0
                act.wait_ge(S("bias"), s + 1)
                for h in range(2):
                    y = sm[:, s % 3, h, k0:]
                    act.activation(y, y, ACT.Exp, scale=HD2 ** -0.5, bias=sml[:, 1, s, h:h + 1],
                                   accum_out=sml[:, 2, s, h:h + 1])
                act.activation(sml[:, 3, s], sml[:, 3, s], ACT.Exp).then_inc(S("exp"), 1)

            def pt_copy(s):
                k0 = 1 if s % NB == 0 else 0
                act.wait_ge(S("turn"), s + 1)
                wait(act, "values", s - 1)
                act.activation(ptb[:, s % 2, :, k0:], pb2[:, s % 2, :, k0:], ACT.Copy).then_inc(S("ptcp"), 1)

            def pooled(g):
                aux_out(act, ("yp", g))
                act.activation(mo[:, g], bank(("yp", g)), ACT.Copy, scale=gate_p[:, 46 + g:47 + g])\
                    .then_inc(S("evA"), 1)
                ev_wait(act, ("yp", g))
                square(8, PT_ - 1 - g, mo[:, g])

            for s in range(16 + 3):
                if s < 16:
                    prob(s)
                if 0 <= s - 2 < 16:
                    pt_copy(s - 2)
                if s < 15 and s % 3 == 2:
                    after(MFILL[s // 3])
                for k in MAUX.get(s, []):
                    if k[0] == "yp":
                        pooled(k[1])
            pooled(0)
            root(8)
            for i in range(PT_):
                act.wait_ge(S("oat"), i + 1)
                square(9, i, mo[:, PT_ + i])
            for t in range(PT_):
                act.wait_ge(S("mh"), t + 1)
                act.activation(a_hi[:, t], mo[:, t], ACT.Copy).then_inc(S("a_hi"), 1)
            root(9)
            for t in range(PT_, KT):
                act.wait_ge(S("mh"), t + 1)
                act.activation(a_hi[:, t], mo[:, t], ACT.Copy).then_inc(S("a_hi"), 1)
            for t in range(KT):
                after(("mo", t))
                act.activation(hb2[:, t], bank(("mo", t)), ACT.Copy).then_inc(S("evA"), 1)
                ev_wait(act, ("mo", t))
                square(10, t, hb2[:, t])
            post(10, 1, "ffn2", "ffn2_pre", 11)
            ffn("2", 11, None, 12)
            post(12, 2, None, None, None)

        @block.vector
        def _(dve):
            def lo(n, i=0, cols=None):
                dve.wait_ge(S("w_hi"), n + 1 + 4 * i)
                c = U.cols[n] if cols is None else cols
                dve.tensor_tensor(w_lo[:, n % 2, 0:c], w_raw[:, n % 4, 0:c],
                                  w_hi[:, n % 2, 0:c].bitcast(F32), ALU.subtract).then_inc(S("w_lo"), 1)

            def after(key):
                if U.at[key] + 2 < N_UNITS:
                    lo(U.at[key] + 2)

            def recip(nu):
                ev_wait(dve, ("n", nu))
                dve.reciprocal(rstd[:], acc[:]).then_inc(S("recip"), 1)
                dve.wait_ge(S("recip"), nu + 1)

            def low(s, t, src, scale=None):
                dve.wait_ge(S("a_hi"), set_count(s, t))
                if scale is None:
                    ins = dve.tensor_tensor(a_lo[:, t], src, a_hi[:, t].bitcast(F32), ALU.subtract)
                else:
                    ins = dve.scalar_tensor_tensor(a_lo[:, t], src, scale, a_hi[:, t].bitcast(F32),
                                                   ALU.mult, ALU.subtract)
                ins.then_inc(S("a_lo"), 1)

            done_taps = [0]

            def taps(count):
                for q in range(done_taps[0], min(done_taps[0] + count, len(TAPS))):
                    t, j = TAPS[q]
                    src, w = cpad[:, t, j:j + T], vec[:, t, len(VEC) + j:len(VEC) + j + 1]
                    if j == 0:
                        ev_wait(dve, ("gla", t))
                        wait(dve, "tap", q - 1)
                        ins = dve.tensor_scalar(cslot(t), src, w, v("conv_b", t), ALU.mult, ALU.add)
                    else:
                        dve.wait_ge(S("tap"), q - 1)
                        ins = dve.scalar_tensor_tensor(cslot(t), src, w, cslot(t), ALU.mult, ALU.add)
                    ins.then_inc(S("tap"), 1)
                done_taps[0] = min(done_taps[0] + count, len(TAPS))

            dve.memset(cpad[:, :, 0:CP], 0.0)
            dve.memset(cpad[:, :, CP + T:PAD], 0.0).then_inc(S("czero"), 1)
            dve.wait_ge(S("p_hi"), 1)
            dve.tensor_tensor(p_lo[:], praw[:], p_hi[:].bitcast(F32), ALU.subtract).then_inc(S("p_lo"), 1)
            lo(0)
            lo(1)
            for n in range(4):
                after(("pl", n))
            recip(0)
            dve.wait_ge(S("in_v"), 16)
            dve.wait_ge(S("in_x"), 16)
            for t in range(KT + 1):
                if t < KT:
                    dve.scalar_tensor_tensor(xin[:, t], xin[:, t], v("g_mix", t), rstd[:], ALU.mult, ALU.mult)\
                        .then_inc(S("hx"), 1)
                if t:
                    low("h", t - 1, xin[:, t - 1])
            dve.wait_ge(S("a_lo"), KT)
            dve.wait_ge(S("a_hi"), KT)
            dve.memset(pad[:, :, 0:SP_], 0.0)
            dve.memset(pad[:, :, SP_ + T:], 0.0).then_inc(S("pzero"), 1)
            dve.wait_ge(S("czero"), 1)
            for t in range(KT):
                after(("glb", t))
                unit_out(dve, ("gla", t))
                ev_wait(dve, ("glb", t))
                dve.tensor_tensor(cpad[:, t, CP:CP + T], bank(("gla", t)), tmps[t % 2][:], ALU.mult)\
                    .then_inc(S("evD"), 1)
                after(("gla", t))
                if t == 2:
                    recip(1)
                    for q in range(KT):
                        dve.wait_ge(S("sq"), 2 * KT)
                        dve.scalar_tensor_tensor(ptile[:, q], ptile[:, q], v("g_plp", q), rstd[:],
                                                 ALU.mult, ALU.mult).then_inc(S("plf"), 1)
                if t >= 2:
                    taps(taps_unit)
            after(("ab",))
            unit_out(dve, ("ab",))
            ab = quad(bank(("ab",))[:, 0:P], NC)
            dve.wait_ge(S("in_g"), 16)
            dt = gate_p[:, 16:32].unsqueeze(1).to_broadcast([P, NC, 16])
            dve.tensor_tensor(gat[:, 2], ab[:, :, 0:16], dt, ALU.add).then_inc(S("gd"), 1)
            dve.tensor_copy(gat[:, 1], ab[:, :, 16:32]).then_inc(S("evD"), 1)
            dve.wait_ge(S("gd"), 1)
            dve.scalar_tensor_tensor(gat[:, 3], gat[:, 2], -1.0, gat[:, 2], ALU.mult, ALU.min).then_inc(S("gd"), 1)
            dve.wait_ge(S("gd"), 2)
            dve.tensor_scalar(gat[:, 0], gat[:, 2], 0.0, None, ALU.max).then_inc(S("gD"), 1)
            dve.wait_ge(S("gD"), 1)
            dve.wait_ge(S("gA"), 3)
            dve.tensor_tensor(gat[:, 0], gat[:, 0], gat[:, 4], ALU.add).then_inc(S("gD"), 1)
            dve.wait_ge(S("gD"), 2)
            ea = gat[:, 5, 0, :].unsqueeze(1).to_broadcast([P, NC, 16])
            dve.scalar_tensor_tensor(gat[:, 0], gat[:, 0], -1.0, ea, ALU.mult, ALU.mult).then_inc(S("g_raw"), 1)
            dve.wait_ge(S("gA"), 7)
            dve.tensor_tensor(gat[:, 4], gat[:, 4], gat[:, 2], ALU.subtract).then_inc(S("gD"), 1)
            dve.tensor_tensor(gat[:, 3], gat[:, 3], gat[:, 1], ALU.mult).then_inc(S("g_k"), 1)

            def qkv(half):
                def short_taps(h, i):
                    n = 3 * h + i
                    ev_wait(dve, ("qkv", n))
                    if h == 0 and i == 0:
                        dve.wait_ge(S("in_s"), 16)
                        dve.wait_ge(S("pzero"), 1)
                    y = sacc[:, h % 2, i]
                    if i < 2:
                        wait(dve, "qk_fin", 2 * (h - 2) + i + 1)
                    else:
                        if h >= 2:
                            dve.wait_ge(S("aux"), AUX[("tr", h - 2, 1)] + 1)
                    for j in range(SK):
                        src, w = pad[:, i, j:j + T], swt[:, i * H + h, j:j + 1]
                        if j == 0:
                            ins = dve.tensor_scalar(y, src, w, None, ALU.mult)
                        else:
                            dve.wait_ge(S("stap"), SK * n + j)
                            ins = dve.scalar_tensor_tensor(y, src, w, y, ALU.mult, ALU.add)
                        ins.then_inc(S("stap"), 1)

                for hh in range(HH + 1):
                    h = HH * half + hh
                    if hh < HH:
                        after(("qkv", 3 * h))
                        if hh == 0 and half:
                            dve.wait_ge(S("o"), 4)
                            dve.memset(pad[:, :, 0:SP_], 0.0)
                            dve.memset(pad[:, :, SP_ + T:], 0.0).then_inc(S("pzero"), 1)
                            dve.wait_ge(S("pzero"), 2)
                        short_taps(h, 0)
                    if hh:
                        for i, dst in enumerate((qT, kT)):
                            ev_wait(dve, ("l2", h - 1, i))
                            dve.reciprocal(l2r[:, i, :], l2r[:, i, :]).then_inc(S("l2i"), 1)
                            dve.wait_ge(S("l2i"), 2 * (h - 1) + i + 1)
                            if half and hh == 1:
                                dve.wait_ge(S("qdm"), 4)
                            dve.tensor_tensor(dst[:, hh - 1], sacc[:, (h - 1) % 2, i], l2r[:, i, :], ALU.mult)\
                                .then_inc(S("qk_fin"), 1)
                    if hh < HH:
                        after(("qkv", 3 * h + 1))
                        short_taps(h, 1)
                        after(("qkv", 3 * h + 2))
                        short_taps(h, 2)

            def gap(R, g):
                if g % 3 == 2:
                    key = filler(R)[g // 3]
                    after(key)
                    if key[0] == "co":
                        t = key[1]
                        unit_out(dve, key)
                        dve.wait_ge(S(f"side{t % 2}"), 16 * (t // 2 + 1))
                        dve.tensor_tensor(ya[:, t], bank(key), tmps[t % 2][:], ALU.mult).then_inc(S("evD"), 1)
                if R < 4:
                    taps(taps_gap)

            lo_, hi_ = slice(0, W64), slice(W64, P)

            def delta(R):
                half, r = divmod(R, NC)

                def scal(k, j):
                    d, hh = divmod(j, HH)
                    q = d * 8 + HH * half + hh
                    return gat[:, k, chunk(d, r), q:q + 1]

                dve.wait_ge(S("grow"), R + 1)
                if r == 0:
                    dve.wait_ge(S("g_all"), 1)
                    dve.wait_ge(S("aux"), AUX[("tr", HH * half + HH - 1, 1)] + 1)
                    dve.wait_ge(S("evA"), O.count(O.at[("tr", HH * half + HH - 1, 1)]))
                wait(dve, "vn", R)
                for j in range(J):
                    ins = dve.tensor_scalar(en[:, j], pA[:, j], scal(2, j), 0.0, ALU.subtract, ALU.max)
                ins.then_inc(S("pre"), 1)
                wait(dve, "o", R)
                for j in range(J):
                    ins = dve.tensor_scalar(et[:, j], pA[:, j], scal(2, j), 0.0, ALU.subtract, ALU.min)
                ins.then_inc(S("pre"), 1)
                dve.wait_ge(S("gram"), R + 1)
                dve.wait_ge(S("en"), R + 1)
                for j in range(J):
                    ins = dve.scalar_tensor_tensor(en[:, j], pB[:, j], scal(1, j), en[:, j], ALU.mult, ALU.mult)
                ins.then_inc(S("L"), 1)
                gap(R, 0)
                gap(R, 1)
                dve.wait_ge(S("y"), LEVELS * R + 1)
                i64 = id64.unsqueeze(1).to_broadcast([P, J, W64])
                dve.tensor_tensor(ub[:], i64, c0, ALU.subtract).then_inc(S("u_upd"), 1)
                dve.tensor_tensor(tb[:], i64, ls[:, 0], ALU.subtract).then_inc(S("t_upd"), 1)
                dve.wait_ge(S("kq"), R + 1)
                dve.wait_ge(S("etm"), R + 1)
                for d in range(2):
                    s = slice(d * HH, d * HH + HH)
                    ins = dve.tensor_tensor(et[:, s], pA[:, s], et[:, s], ALU.mult)
                ins.then_inc(S("qk"), 1)
                for lv in range(1, LEVELS):
                    gap(R, 2 * lv)
                    dve.wait_ge(S("uy"), (LEVELS - 1) * R + lv)
                    if lv < LEVELS - 1:
                        dve.tensor_tensor(ub[:], ub[:], c1, ALU.subtract).then_inc(S("u_upd"), 1)
                    else:
                        dve.tensor_tensor(en[lo_, :, lo_], ub[lo_], c1[lo_], ALU.subtract)
                        dve.tensor_tensor(en[hi_, :, hi_], ub[hi_], c1[hi_], ALU.subtract).then_inc(S("u_upd"), 1)
                    dve.wait_ge(S("yt"), (LEVELS - 1) * R + lv)
                    dve.tensor_tensor(tb[:], tb[:], c0, ALU.subtract).then_inc(S("t_upd"), 1)
                    gap(R, 2 * lv + 1)
                dve.wait_ge(S("yf"), R + 1)
                dve.memset(en[hi_, 0:HH, lo_], 0.0)
                dve.memset(en[lo_, HH:J, hi_], 0.0)
                dve.wait_ge(S("u12"), R + 1)
                dve.tensor_scalar(en[lo_, 0:HH, hi_], c1[lo_, 0:HH], -1.0, None, ALU.mult)
                dve.tensor_scalar(en[hi_, HH:J, lo_], c1[hi_, HH:J], -1.0, None, ALU.mult).then_inc(S("u12s"), 1)
                dve.wait_ge(S("o"), R + 1)
                for d in range(2):
                    c = chunk(d, r)
                    dst = oT[:, HH * half:HH * half + HH, c * P:(c + 1) * P]
                    src = pA[:, d * HH:d * HH + HH]
                    if r < NC // 2:
                        ins = dve.tensor_copy(dst, src)
                    else:
                        if d == 0:
                            dve.wait_ge(S("o_acc"), R)
                        ins = dve.tensor_tensor(dst, dst, src, ALU.add)
                ins.then_inc(S("o_acc"), 1)
                if r < NC - 1:
                    dve.wait_ge(S("s"), (NC - 1) * half + r + 1)
                    if r == 0:
                        for d in range(2):
                            ins = dve.tensor_copy(st[:, d * HH:d * HH + HH], pC[:, d * HH:d * HH + HH])
                    else:
                        for j in range(J):
                            ins = dve.scalar_tensor_tensor(st[:, j], st[:, j], scal(5, j), pC[:, j],
                                                           ALU.mult, ALU.add)
                    ins.then_inc(S("s_upd"), 1)

            qkv(0)
            for R in range(4):
                delta(R)
            assert done_taps[0] == len(TAPS)
            qkv(1)
            ev_wait(dve, ("mean",))
            for t in range(KT):
                dve.tensor_tensor(cslot(t), cslot(t), acc[:], ALU.subtract).then_inc(S("xc"), 1)
            delta(4)
            ev_wait(dve, ("var",))
            dve.reciprocal(rstd[:], acc[:]).then_inc(S("rv"), 1)
            dve.wait_ge(S("rv"), 1)
            for t in range(KT):
                dve.tensor_tensor(cslot(t), cslot(t), rstd[:], ALU.mult).then_inc(S("xn"), 1)
            delta(5)
            for t in range(KT):
                low("conv", t, cslot(t))
            delta(6)
            delta(7)
            for h in range(H):
                b = (acc, rstd)[h % 2]
                ev_wait(dve, ("on", h))
                dve.reciprocal(b[:], b[:]).then_inc(S("on_r"), 1)
                dve.wait_ge(S("on_r"), h + 1)
                dve.scalar_tensor_tensor(oT[:, h], oT[:, h], gate_p[:, 32:33], b[:], ALU.mult, ALU.mult)\
                    .then_inc(S("on_g"), 1)
                dve.wait_ge(S("on_g"), h + 1)
                dve.wait_ge(S(f"side{h % 2}"), 16 * (4 + h // 2 + 1))
                dve.tensor_tensor(oT[:, h], oT[:, h], tmps[h % 2][:], ALU.mult).then_inc(S("on_z"), 1)
                if h >= 2:
                    low("o", h - 2, oT[:, h - 2])
            low("o", H - 2, oT[:, H - 2])
            low("o", H - 1, oT[:, H - 1])
            for t in range(KT):
                after(("do", t))
                unit_out(dve, ("do", t))
                dve.wait_ge(S(f"sgb{t % 2}"), 16 * (t // 2 + 1))
                dve.tensor_tensor(gst[:, t % 2], bank(("do", t)), gst[:, t % 2], ALU.mult).then_inc(S("evD"), 1)
                ev_wait(dve, ("do", t))
                dve.tensor_tensor(ya[:, t], ya[:, t], gst[:, t % 2], ALU.add).then_inc(S("yv"), 1)
                dve.wait_ge(S("yb_hi"), t + 1)
                dve.tensor_tensor(yb_lo[:, t], ya[:, t], yb_hi[:, t].bitcast(F32), ALU.subtract)\
                    .then_inc(S("yb_lo"), 1)
            for t in range(KT):
                after(("wo", t))
                unit_out(dve, ("wo", t))
                dve.wait_ge(S(f"side{t % 2}"), 16 * (8 + t // 2 + 1))
                dve.tensor_tensor(x[:, t], bank(("wo", t)), tmps[t % 2][:], ALU.add).then_inc(S("evD"), 1)
                low("ffn0", t, x[:, t], v("g_ffn", t))

            def ffn(f, nu, g):
                def step(i):
                    for q in range(2):
                        n = U.at[("fg" + f, q)]
                        du = O.at[("fu" + f, q)]
                        last = isinstance(i, int)
                        if last and i == 0 and q == 0:
                            lo(n + 2)
                            recip(nu)
                            pass
                        dve.wait_ge(S("gemm"), n + 1 + 4 * i)
                        if not (last and i == 0 and q == 0):
                            dve.wait_ge(S("h_hi"), FT * int(f) + q + 2 * i)
                        bg, bu = (pg[:, O.at[(k + f, 2 * i + q if last else 2 + q)] % 2, :] for k in ("fg", "fu"))
                        dve.tensor_tensor(tmp1[:], bg, rstd[:], ALU.mult).then_inc(S("evD"), 1)
                        if not (last and i == 0 and q == 0):
                            lo(n + 2, i, U.cols[n + 2 + (4 * i if last else 0)])
                        dve.wait_ge(S("gemm"), n + 2 + 4 * i)
                        wait(dve, "h_lo", FT * int(f) + q + 2 * i)
                        dve.tensor_tensor(tmp2[:], bu, rstd[:], ALU.mult).then_inc(S("evD"), 1)
                        lo(n + 3, i, U.cols[n + 3 + (4 * i if last else 0)])
                        dve.wait_ge(S("sil"), FT * int(f) + q + 1 + 2 * i)
                        dve.wait_ge(S("evD"), O.count(du) + 4 * i)
                        dve.tensor_tensor(tmp2[:], tmp2[:], tmp1[:], ALU.mult).then_inc(S("hm"), 1)
                        dve.wait_ge(S("h_hi"), FT * int(f) + q + 1 + 2 * i)
                        m = 2 * i + q
                        at_m = (lambda b: b[:, m]) if last else \
                            (lambda b: b[:, bass.ds(m, 1)].rearrange("p a n -> p (a n)"))
                        dve.tensor_tensor(at_m(h_lo), tmp2[:], at_m(h_hi).bitcast(F32), ALU.subtract)\
                            .then_inc(S("h_lo"), 1)

                step(0)
                with dve.Fori(1, FT // 2 - 1) as i:
                    step(i)
                step(FT // 2 - 1)
                if f == "0":
                    rope_angles()
                for m in range(KT):
                    after(("fd" + f, 2 * m))
                    after(("fd" + f, 2 * m + 1))
                    if f != "0":
                        continue
                    unit_out(dve, ("fd" + f, 2 * m + 1))
                    dve.tensor_tensor(x[:, m], bank(("fd" + f, m)), x[:, m], ALU.add).then_inc(S("evD"), 1)
                    low("pg", m, x[:, m], v(g, m))

            def rope_angles():
                def step(k, ins):
                    ins.then_inc(S("ra"), 1)
                    dve.wait_ge(S("ra"), k)

                whole = 12582912.0
                c_a, c_b = 6.28125, 0.00193500518798828125
                c_c = float(np.float64(2 * np.pi) - c_a - c_b)
                dve.wait_ge(S("in_r"), 16)
                step(1, dve.tensor_scalar(rcos[:], rpos[:], gate_p[:, 37:38], None, ALU.mult))
                step(2, dve.tensor_scalar(rsin[:], rcos[:], float(1 / (2 * np.pi)), whole, ALU.mult, ALU.add))
                step(3, dve.tensor_scalar(rsin[:], rsin[:], -whole, None, ALU.add))
                for q, c_ in enumerate((c_a, c_b, c_c)):
                    step(4 + q, dve.scalar_tensor_tensor(rcos[:], rsin[:], -c_, rcos[:], ALU.mult, ALU.add))
                step(7, dve.tensor_scalar(rcos[:], rcos[:], 3.1415925, -3.1415925, ALU.min, ALU.max))
                dve.scalar_tensor_tensor(rpos[:].bitcast(F32), rcos[:], -1.0, rcos[:], ALU.mult, ALU.max)\
                    .then_inc(S("rope"), 1)

            ffn("0", 2, "g_pl")
            for t in range(KT):
                after(("pg", t))
                if t == 0:
                    recip(3)
                    dve.wait_ge(S("in_pl"), 16)
                unit_out(dve, ("pg", t))
                dve.tensor_tensor(tmps[t % 2][:], bank(("pg", t)), rstd[:], ALU.mult).then_inc(S("evD"), 1)
                dve.wait_ge(S("pgs"), t + 1)
                dve.tensor_tensor(tmps[t % 2][:], tmps[t % 2][:], pl[:, t], ALU.mult).then_inc(S("pgm"), 1)
                dve.wait_ge(S("pgm"), t + 1)
                dve.tensor_tensor(x[:, t], x[:, t], tmps[t % 2][:], ALU.add).then_inc(S("x2"), 1)
            recip(4)
            for t in range(KT):
                dve.scalar_tensor_tensor(x[:, t], x[:, t], v("g_final", t), rstd[:], ALU.mult, ALU.mult)\
                    .then_inc(S("xf"), 1)
            for t in range(KT):
                low("ffn1", t, x[:, t], v("ffn1_pre", t))
            ffn("1", 5, None)

            def post(nu, k, src, g, half_, s, g2):
                recip(nu)
                for t in range(KT + 1):
                    if t < KT:
                        q = KT * k + t
                        wait(dve, "xu", q - 1)
                        dve.scalar_tensor_tensor(tmps[t % 2][:], src[:, t], v(g, t), rstd[:], ALU.mult, ALU.mult)\
                            .then_inc(S("xt"), 1)
                        dve.wait_ge(S("xt"), q + 1)
                        dve.scalar_tensor_tensor(x[:, t], tmps[t % 2][:], half_, x[:, t], ALU.mult, ALU.add)\
                            .then_inc(S("xu"), 1)
                    if t and s:
                        low(s, t - 1, x[:, t - 1], v(g2, t - 1))

            post(6, 0, hb, "ffn1_post", 0.5, "mix", "mix_pre")
            dve.memset(up[:, :, 0:PW], 0.0)
            dve.memset(kz[0:HD2, 1], 0.0)
            dve.memset(kz[HD2:P, 0], 0.0)
            dve.memset(win[:, :, 0:PW], 0.0).then_inc(S("uzero"), 1)
            dve.tensor_scalar(nsink[:], gate_p[:, 38:46].rearrange("p (h i) -> p i h", h=2), -1.0, None, ALU.mult)\
                .then_inc(S("nsink"), 1)
            dve.wait_ge(S("nsink"), 1)

            def rotated(i):
                dve.wait_ge(S("rsin"), 2)
                aux_out(dve, ("rp", i))
                wait(dve, "qk2", i)
                dve.tensor_tensor(rt[:, 0], zq[:, i], rcos[:], ALU.mult).then_inc(S("rt"), 1)
                dve.tensor_tensor(rt[:, 1], bank(("rp", i)), rsin[:], ALU.mult).then_inc(S("evD"), 1)
                ev_wait(dve, ("rp", i))
                if i:
                    dve.tensor_tensor(qk2[:, i - 1], rt[:, 0], rt[:, 1], ALU.add).then_inc(S("qk2"), 1)
                else:
                    for h, p_ in enumerate((slice(0, HD2), slice(HD2, P))):
                        ins = dve.tensor_tensor(kz[p_, h], rt[p_, 0], rt[p_, 1], ALU.add)
                    ins.then_inc(S("qk2"), 1)

            def evac(key, dst):
                unit_out(dve, key)
                dve.tensor_tensor(dst, bank(key), rstd[:], ALU.mult).then_inc(S("evD"), 1)

            def mixed(key):
                after(key)
                if key == ("mk", 0):
                    recip(7)
                name, i = key
                dst = {"mk": zq[:, 0], "mv": zv[:], "mq": zq[:, 1 + i] if name == "mq" else None,
                       "mu": up[:, i, PW:] if name == "mu" else None}[name]
                evac(key, dst)

            for key in MIX[:3]:
                mixed(key)
            rotated(0)
            mixed(("mq", 1))
            rotated(1)
            mixed(("mq", 2))
            rotated(2)

            def bias(s):
                i, n = divmod(s, NB)
                k0 = P if n == 0 else 0
                dve.wait_ge(S("scores"), s + 1)
                wait(dve, "turn", s - 2)
                y = sm[:, s % 3, :, k0:]
                mask = band[:, k0:].unsqueeze(1).to_broadcast([P, 2, 2 * P - k0])
                dve.tensor_tensor(y, pa2[:, s % 2, :, k0:], mask, ALU.add).then_inc(S("smask"), 1)
                dve.wait_ge(S("smask"), s + 1)
                dve.tensor_reduce(out=sml[:, 0, s], in_=y, axis=mybir.AxisListType.X, op=ALU.max)\
                    .then_inc(S("smax"), 1)
                dve.wait_ge(S("smax"), s + 1)
                dve.scalar_tensor_tensor(sml[:, 1, s], sml[:, 0, s], -HD2 ** -0.5, nsink[:, i], ALU.mult, ALU.min)\
                    .then_inc(S("sneg"), 1)
                dve.wait_ge(S("sneg"), s + 1)
                dve.tensor_tensor(sml[:, 3, s], sml[:, 1, s], nsink[:, i], ALU.subtract).then_inc(S("bias"), 1)

            def normed(s):
                k0 = P if s % NB == 0 else 0
                dve.wait_ge(S("exp"), s + 1)
                dve.tensor_tensor(sml[:, 4, s], sml[:, 2, s], sml[:, 3, s], ALU.add).then_inc(S("den"), 1)
                dve.wait_ge(S("den"), 2 * s + 1)
                dve.reciprocal(sml[:, 4, s], sml[:, 4, s]).then_inc(S("den"), 1)
                dve.wait_ge(S("den"), 2 * s + 2)
                for h in range(2):
                    y = sm[:, s % 3, h, k0:]
                    ins = dve.tensor_scalar(y, y, sml[:, 4, s, h:h + 1], None, ALU.mult)
                ins.then_inc(S("prob"), 1)

            def means(g):
                w, u = win[:, g % 2, PW:], up[:, g, PW:]
                dve.wait_ge(S("win"), PT_ - g)
                dve.scalar_tensor_tensor(wd[:, g], w, 1.0 / POOL_W[g], u, ALU.mult, ALU.subtract)\
                    .then_inc(S("wdm"), 1)
                dve.tensor_tensor(tmp1[:, 0:16], w[:, 0:16], edge[:, g], ALU.mult).then_inc(S("wdm"), 1)
                dve.wait_ge(S("wdm"), 2 * (PT_ - g))
                dve.tensor_tensor(wd[:, g, 0:16], tmp1[:, 0:16], u[:, 0:16], ALU.subtract).then_inc(S("wd"), 1)
                dve.wait_ge(S("wd"), PT_ - g)

            MEANS = {7: 3, 10: 2, 13: 1, 16: 0}
            for s in range(16 + 3):
                if s < 16:
                    bias(s)
                if 0 <= s - 1 < 16:
                    normed(s - 1)
                if s < 15 and s % 3 == 2:
                    mixed(MFILL[s // 3])
                for k in MAUX.get(s, []):
                    if k[0] == "rp":
                        rotated(k[1])
                if s in MEANS:
                    means(MEANS[s])
                if s >= 3 and (s - 3) % NB == NB - 1:
                    i = (s - 3) // NB
                    dve.wait_ge(S("values"), s - 2)
                    dve.tensor_copy(mo[:, PT_ + i], pc2[:, i % 2]).then_inc(S("oat"), 1)
            for nu, t0, at_ in ((8, 0, 50), (9, PT_, 54)):
                recip(nu)
                for t in range(t0, t0 + PT_):
                    g = at_ + t - t0
                    dve.scalar_tensor_tensor(mo[:, t], mo[:, t], gate_p[:, g:g + 1], rstd[:], ALU.mult, ALU.mult)\
                        .then_inc(S("mh"), 1)
                for t in range(t0, t0 + PT_):
                    low("out", t, mo[:, t])
            for t in range(KT):
                after(("mo", t))
            post(10, 1, hb2, "mix_post", 1.0, "ffn2", "ffn2_pre")
            ffn("2", 11, None)
            post(12, 2, hb, "ffn2_post", 0.5, None, None)

        @block.gpsimd
        def _(pool):
            def adds(nu):
                for t in range(1, NORMS[nu]):
                    pool.wait_ge(S("sq"), SQ[nu] + t + 1)
                    wait(pool, "add", AD[nu] + t - 1)
                    pool.tensor_tensor(acc[:], acc[:], sq[:, t % 2, :], ALU.add).then_inc(S("add"), 1)

            def delta(R):
                half, r = divmod(R, NC)

                def toks(k, d):
                    q = d * 8 + HH * half
                    return gat[:, k, chunk(d, r), q:q + HH].unsqueeze(2).to_broadcast([P, HH, P])

                def level(lv):
                    pool.wait_ge(S("lc"), R + 1)
                    wait(pool, "y", LEVELS * R + lv - 1)
                    if lv == 2:
                        pool.wait_ge(S("t_upd"), LEVELS * R + 1)
                    q = C_LVL + lv * 2 * W64
                    mask = quad(consts[:, q:q + 2 * W64], 2).unsqueeze(2).to_broadcast([P, 2, HH, W64])
                    pool.tensor_tensor(ls[:, lv % 2].rearrange("p (d h) c -> p d h c", d=2),
                                       lc[:].rearrange("p (d h) c -> p d h c", d=2), mask, ALU.mult)\
                        .then_inc(S("ls"), 1)

                pool.wait_ge(S("et"), R + 1)
                for d in range(2):
                    s = slice(d * HH, d * HH + HH)
                    ins = pool.tensor_tensor(et[:, s], et[:, s], tri[d].unsqueeze(1).to_broadcast([P, HH, P]), ALU.mult)
                ins.then_inc(S("etm"), 1)
                level(0)
                level(1)
                pool.wait_ge(S("eg"), R + 1)
                for d in range(2):
                    s, c = slice(d * HH, d * HH + HH), chunk(d, r)
                    ins = pool.tensor_tensor(qd[:, s], qd[:, s], qT[:, :, c * P:(c + 1) * P], ALU.mult)
                ins.then_inc(S("qdm"), 1)
                pool.wait_ge(S("g_k"), 1)
                wait(pool, "s", (NC - 1) * half + r)
                wait(pool, "vn", R)
                level(2)
                for dst, src, k, name, lv in ((kb, ktok, 3, "kb", 3), (bv, vtok, 1, "bv", 4), (kt, ktok, 4, "kt", 5)):
                    if name != "kb":
                        wait(pool, "o", R)
                    for d in range(2):
                        ins = pool.tensor_tensor(dst[:, d * HH:d * HH + HH], src[:, :, chunk(d, r), :], toks(k, d),
                                                 ALU.mult)
                    ins.then_inc(S(name), 1)
                    level(lv)

            pool.wait_ge(S("in_c"), 16)
            adds(0)
            adds(1)
            for R in range(4):
                if R == 0:
                    pool.wait_ge(S("g_all"), 1)
                    pool.wait_ge(S("evA"), O.count(O.at[("tr", HH - 1, 1)]))
                delta(R)
            pool.wait_ge(S("tap"), len(TAPS))
            for t in range(1, KT):
                wait(pool, "csum", t - 1)
                pool.tensor_tensor(acc[:], cslot(0) if t == 1 else acc[:], cslot(t), ALU.add)\
                    .then_inc(S("csum"), 1)
            for t in range(1, KT):
                pool.wait_ge(S("cvs"), t + 1)
                wait(pool, "cva", t - 1)
                pool.tensor_tensor(rstd[:], rstd[:], sq[:, t % 2, :], ALU.add).then_inc(S("cva"), 1)
            for R in range(4, 8):
                delta(R)
            for nu in range(2, 8):
                adds(nu)
            pool.wait_ge(S("uzero"), 1)
            for g in reversed(range(PT_)):
                ev_wait(pool, ("mu", g))
                wait(pool, "wd", PT_ - 1 - g)
                for q in range(g + 1):
                    src = up[:, g] if q == 0 else win[:, (q - 1) % 2]
                    ins = pool.tensor_tensor(win[:, q % 2, PW:], src[:, PW:], src[:, PW - (1 << q):PW + T - (1 << q)],
                                             ALU.add)
                    if q < g:
                        n_add = sum(range(g + 1, PT_)) + q + 1
                        ins.then_inc(S("wadd"), 1)
                        pool.wait_ge(S("wadd"), n_add)
                ins.then_inc(S("win"), 1)
            for nu in range(8, 13):
                adds(nu)

    return


def kernel(**inputs):
    import concourse.bacc as bacc
    from concourse.bass_utils import run_bass_kernel_spmd

    def tiles(w):
        k, n = w.shape
        return np.ascontiguousarray(w.reshape(k // P, P, n // P, P).transpose(2, 1, 0, 3).reshape(n // P, P, k))

    def cols(w):
        return np.ascontiguousarray(w.T.reshape(w.shape[1] // P, P, w.shape[0]).transpose(1, 0, 2))

    f = {k: np.asarray(w) for k, w in inputs.items()}
    w_in = f["w_in"][0]
    pre = 2 * D + 4 * D
    arrays = {
        "x": cols(f["x"][0]),
        "p": cols(f["p"][0, 0]),
        "consts": constant_table(),
        "w_in": tiles(np.concatenate([w_in[:, :pre], w_in[:, pre + 32:]], 1)),
        "w_ab": np.ascontiguousarray(w_in[:, pre:pre + 32].reshape(KT, P, 32).transpose(1, 0, 2).reshape(P, KT * 32)),
        "w_plp": np.ascontiguousarray(
            tiles(f["w_pl_proj"][0]).reshape(4, 2, P, 2 * P).transpose(0, 2, 1, 3).reshape(4, P, 4 * P)),
        "w_co": tiles(f["w_conv_out"][0]),
        "w_do": tiles(f["w_delta_out"][0]),
        "w_wo": tiles(f["w_o"][0]),
        "w_gu0": tiles(f["w_gate_up"][0]),
        "w_dn0": np.ascontiguousarray(
            f["w_down"][0].reshape(2, KH, P, KT, P).transpose(3, 0, 2, 1, 4).reshape(KT, 2, P, KH * P)),
        "w_pg": tiles(f["w_pl_gate"][0]),
    }

    def down(w):
        return np.ascontiguousarray(w.reshape(2, KH, P, KT, P).transpose(3, 0, 2, 1, 4).reshape(KT, 2, P, KH * P))

    pairs = np.concatenate([np.arange(HD2) + HD2 * h for i in range(4) for h in (i, i + 4)])
    w2, half = f["w_in_2"][0], D // 2
    arrays.update({
        "w_gu1": tiles(f["ffn1_w_gu_2"][0]), "w_dn1": down(f["ffn1_w_down_2"][0]),
        "w_gu2": tiles(f["ffn2_w_gu_2"][0]), "w_dn2": down(f["ffn2_w_down_2"][0]),
        "w_in2": tiles(np.concatenate([w2[:, :half], w2[:, half + pairs], w2[:, D:]], 1)),
        "w_out2": tiles(np.concatenate([f["w_out_2"][0][:half], f["w_out_2"][0][half + pairs]], 0)),
        "pos": np.ascontiguousarray(np.broadcast_to(f["positions_2"].reshape(1, T), (P, T))),
        "c2": np.concatenate([mixer_table(), f["w_pool_2"][0].transpose(1, 0, 2).reshape(P, PT_ * P)], 1),
    })
    names = ["g_mix", "conv_dw_b", "conv_ln_g", "conv_ln_b", "g_ffn", "g_pl", "g_pl_proj", "g_final",
             "ffn1_pre_2", "ffn1_post_2", "mix_pre_2", "mix_post_2", "ffn2_pre_2", "ffn2_post_2"]
    rows = np.concatenate([f[n].reshape(1, D) for n in names] + [f["conv_dw_w"][0]], 0)
    arrays["vec"] = np.ascontiguousarray(rows.T.reshape(KT, P, NV).transpose(1, 0, 2))
    arrays["swt"] = np.ascontiguousarray(f["qkv_conv_w"][0].T.reshape(3 * H, P, SK).transpose(1, 0, 2))
    small = np.concatenate([f["a_log"].reshape(-1), f["dt_bias"].reshape(-1)])
    eps = np.array([EPS, P * EPS, EPS, LN_EPS], np.float32)
    dim = np.arange(P) % HD2
    freq = np.float32(THETA) ** (-np.arange(0, ROT, 2, dtype=np.float32) / np.float32(ROT))
    freq = np.where(dim < ROT, freq[dim % (ROT // 2)], 0).astype(np.float32).reshape(P, 1)
    arrays["gate_p"] = np.concatenate(
        [np.broadcast_to(small, (P, 32)), f["delta_norm_g"].reshape(P, 1), np.broadcast_to(eps, (P, 4)), freq,
         np.broadcast_to(f["sinks_2"].reshape(1, 8), (P, 8)), f["pool_scale_2"].reshape(PT_, P).T,
         f["g_pool_2"].reshape(PT_, P).T, f["g_attn_2"].reshape(-1)[pairs].reshape(PT_, P).T,
         np.full((P, 1), np.pi / 2, np.float32)], 1)
    nc = bacc.Bacc("TRN2", target_bir_lowering=False, num_devices=1)
    a = {n: nc.dram_tensor("in_" + n, w.shape, mybir.dt.from_np(w.dtype), kind="ExternalInput").ap()
         for n, w in arrays.items()}
    out = nc.dram_tensor("out", (KT, P, T), F32, kind="ExternalOutput").ap()
    build(nc, a, out)
    r = run_bass_kernel_spmd(nc, [{"in_" + n: w for n, w in arrays.items()}], core_ids=[0])
    y = np.asarray(r.results[0]["out"])
    return np.ascontiguousarray(y.transpose(2, 0, 1).reshape(1, T, D))
```

```python
import numpy as np
import concourse.bass as bass
from concourse import mybir
from contextlib import ExitStack

F32 = mybir.dt.float32
F32R = mybir.dt.float32r
ALU = mybir.AluOpType
ACT = mybir.ActivationFunctionType

P = 128
T = 512
D = 1024
KT = D // P
FT = 2816 // P
KH = FT // 2
H = 8
HH = 4
NC = T // P
CK = 31
CP = CK // 2
SK = 5
SP_ = SK // 2
W64 = 64
LEVELS = 6
PT_ = 4
HD2 = 64
NB = T // P
ROT = HD2 // 4
THETA = 500000.0
POOL_W = (2, 4, 8, 16)
NEG = -1e30
EPS = 1e-6
LN_EPS = 1e-5

VEC = ["g_mix", "conv_b", "ln_g", "ln_b", "g_ffn", "g_pl", "g_plp", "g_final",
       "ffn1_pre", "ffn1_post", "mix_pre", "mix_post", "ffn2_pre", "ffn2_post"]
NV = len(VEC) + CK

C_ID, C_ONE, C_TRI, C_LVL, C_I64 = 0, P, 2 * P, 4 * P, 4 * P + 2 * LEVELS * W64
C_END = C_I64 + W64


def constant_table():
    c = np.zeros((P, C_END), np.float32)
    r = np.arange(P)
    c[:, C_ID:C_ID + P] = np.eye(P)
    c[:, C_ONE:C_ONE + P] = 1.0
    c[:, C_TRI:C_TRI + P] = r[:, None] <= r[None, :]
    c[:, C_TRI + P:C_TRI + 2 * P] = r[:, None] >= r[None, :]
    row, col = r[:, None] % W64, np.arange(W64)[None, :]
    for lv in range(LEVELS):
        s = 1 << lv
        same = row // (2 * s) == col // (2 * s)
        low = same & (row // s % 2 == 1) & (col // s % 2 == 0)
        up = same & (row // s % 2 == 0) & (col // s % 2 == 1)
        at = C_LVL + lv * 2 * W64
        c[:, at:at + W64] = low
        c[:, at + W64:at + 2 * W64] = up
    c[:, C_I64:C_I64 + W64] = row == col
    return c


def mixer_table():
    perm = np.zeros((P, P), np.float32)
    for h in range(0, P, HD2):
        for d in range(ROT // 2):
            perm[h + d + ROT // 2, h + d] = -1.0
            perm[h + d, h + d + ROT // 2] = 1.0
    q, k = np.arange(P)[:, None], np.arange(2 * P)[None, :]
    band = np.where((k > q) & (k <= q + P), 0.0, NEG)
    t = np.arange(16)
    edge = np.concatenate([1.0 / np.minimum(t + 1, w) for w in POOL_W])
    return np.concatenate([perm, band, np.broadcast_to(edge, (P, 64))], 1).astype(np.float32)


class Units:

    def __init__(self):
        self.src, self.cols, self.at = [], [], {}

    def add(self, name, src, cols):
        self.at[name] = len(self.src)
        self.src.append(src)
        self.cols.append(cols)


class Outs:

    def __init__(self):
        self.reader, self.at = [], {}

    def add(self, name, reader):
        self.at[name] = len(self.reader)
        self.reader.append(reader)

    def count(self, o):
        return self.reader[:o + 1].count(self.reader[o])


def build(nc, a, out):
    ctx = ExitStack()
    with ctx:
        sems = {}

        def S(name):
            if name not in sems:
                sems[name] = ctx.enter_context(nc.semaphore(name))
            return sems[name]

        ALL = 212832
        base = [nc.sbuf_base + (-nc.sbuf_base) % 32]
        first = base[0]

        def at(name, cols, dtype=F32, offset=None, shape=None):
            if offset is None:
                offset = base[0]
                base[0] += cols * 4 + (-cols * 4) % 32
            assert offset + cols * 4 <= first + ALL, (name, offset + cols * 4 - first - ALL)
            return nc.alloc_sbuf_tensor_at(name, shape or [P, cols], dtype, offset=offset)

        UC = KH * P
        w_raw = at("w_raw", 4 * UC, shape=[P, 4, UC])
        w_hi = at("w_hi", 2 * UC, F32R, shape=[P, 2, UC])
        w_lo = at("w_lo", 2 * UC, F32R, shape=[P, 2, UC])
        A_OFF = base[0]
        a_hi = at("a_hi", KT * T, F32R, shape=[P, KT, T])
        a_lo = at("a_lo", KT * T, F32R, shape=[P, KT, T])
        X_OFF = base[0]
        x = at("x", KT * T, shape=[P, KT, T])
        consts = at("consts", C_END)
        vec = at("vec", KT * NV, shape=[P, KT, NV])
        swt = at("swt", 3 * H * SK, shape=[P, 3 * H, SK])
        gate_p = at("gate_p", 59)
        eps_t = gate_p[:, 33:37]
        tmp1 = at("tmp1", T)
        tmp2 = at("tmp2", T)
        sq = at("sq", 2 * T, shape=[P, 2, T])
        acc = at("acc", T)
        rstd = at("rstd", T)
        nst = at("nst", 16, shape=[P, 2, 8])
        ost = at("ost", 8 * NC, shape=[P, 8 * NC])
        R_OFF = base[0]

        ident = consts[:, C_ID:C_ID + P]
        ones = consts[:, C_ONE:C_ONE + P]
        tri = [consts[:, C_TRI + d * P:C_TRI + (d + 1) * P] for d in range(2)]
        id64 = consts[:, C_I64:C_I64 + W64]

        def v(name, t):
            return vec[:, t, VEC.index(name):VEC.index(name) + 1]

        base[0] = R_OFF
        PAD = T + 2 * CP
        cpad = at("cpad", KT * PAD, shape=[P, KT, PAD])
        cacc = at("cacc", 2 * T, shape=[P, 2, T])
        qT = at("qT", HH * T, shape=[P, HH, T])
        kT = at("kT", HH * T, shape=[P, HH, T])
        ktok = at("ktok", HH * T, shape=[P, HH, NC, P])
        vtok = at("vtok", HH * T, shape=[P, HH, NC, P])
        oT = at("oT", KT * T, offset=X_OFF, shape=[P, KT, T])
        gat = at("gat", 6 * 64, shape=[P, 6, NC, 16])
        D_OFF = base[0]
        J = 2 * HH
        en = at("en", J * P, shape=[P, J, P])
        et = at("et", J * P, shape=[P, J, P])
        lc = at("lc", J * W64, shape=[P, J, W64])
        ls = at("ls", 2 * J * W64, shape=[P, 2, J, W64])
        tb = at("tb", J * W64, shape=[P, J, W64])
        ub = at("ub", J * W64, shape=[P, J, W64])
        yb = at("yb", J * W64, shape=[P, J, W64])
        kb = at("kb", J * P, shape=[P, J, P])
        bv = at("bv", J * P, shape=[P, J, P])
        kt = at("kt", J * P, shape=[P, J, P])
        st = at("st", J * P, shape=[P, J, P])
        qd = at("qd", J * P, shape=[P, J, P])
        xin = at("xin", KT * T, offset=D_OFF, shape=[P, KT, T])
        praw = at("praw", 2 * T, offset=D_OFF + 16384, shape=[P, 2, T])
        p_hi = at("p_hi", 2 * T, F32R, offset=D_OFF + 20480, shape=[P, 2, T])
        p_lo = at("p_lo", 2 * T, F32R, offset=D_OFF + 24576, shape=[P, 2, T])
        ptile = at("ptile", KT * T, offset=R_OFF + KT * PAD * 4 + 4096, shape=[P, KT, T])
        pad = at("pad", 3 * (T + 4), offset=D_OFF, shape=[P, 3, T + 4])
        sacc = at("sacc", 6 * T, offset=D_OFF + 8192, shape=[P, 2, 3, T])
        ya = at("ya", KT * T, offset=R_OFF, shape=[P, KT, T])
        yb_hi = at("yb_hi", KT * T, F32R, offset=D_OFF, shape=[P, KT, T])
        yb_lo = at("yb_lo", KT * T, F32R, offset=D_OFF + 16384, shape=[P, KT, T])
        gst = at("gst", 2 * T, offset=D_OFF + 32768, shape=[P, 2, T])
        base[0] = R_OFF
        h_hi = at("h_hi", FT * T, F32R, shape=[P, FT, T])
        h_lo = at("h_lo", FT * T, F32R, shape=[P, FT, T])
        pl = at("pl", KT * T, offset=R_OFF, shape=[P, KT, T])
        hb = at("hb", KT * T, offset=A_OFF, shape=[P, KT, T])

        rcos = at("rcos", T)
        rsin = at("rsin", T)
        rpos = at("rpos", T, mybir.dt.int32)
        base[0] = R_OFF
        PW = 16
        c2 = at("c2", P + 2 * P + 4 * 16 + PT_ * P)
        perm, band = c2[:, 0:P], c2[:, P:3 * P]
        edge = c2[:, 3 * P:3 * P + 64].rearrange("p (g t) -> p g t", g=4)
        wpool = c2[:, 3 * P + 64:].rearrange("p (g d) -> p g d", g=4)
        Q_OFF = base[0]
        zq = at("zq", 5 * T, shape=[P, 5, T])
        kz = at("kz", 2 * T, shape=[P, 2, T])
        qk2 = at("qk2", 4 * T, shape=[P, 4, T])
        rt = at("rt", 2 * T, shape=[P, 2, T])
        zv = at("zv", T)
        vt2 = at("vt2", T, shape=[P, NB, P])
        up = at("up", PT_ * (PW + T), shape=[P, PT_, PW + T])
        win = at("win", 2 * (PW + T), shape=[P, 2, PW + T])
        wd = at("wd", PT_ * T, shape=[P, PT_, T])
        mo = at("mo", KT * T, shape=[P, KT, T])
        sm = at("sm", 3 * T, shape=[P, 3, 2, 2 * P])
        ptb = at("ptb", 2 * T, shape=[P, 2, 2, 2, P])
        sml = at("sml", 5 * 32, shape=[P, 5, 16, 2])
        nsink = at("nsink", 8, shape=[P, 4, 2])
        hb2 = at("hb2", KT * T, offset=Q_OFF, shape=[P, KT, T])

        pg = ctx.enter_context(nc.psum_tensor("pg", [P, 2, T], F32))
        pA = ctx.enter_context(nc.psum_tensor("pA", [P, J, P], F32))
        pB = ctx.enter_context(nc.psum_tensor("pB", [P, J, P], F32))
        pC = ctx.enter_context(nc.psum_tensor("pC", [P, J, P], F32))
        c0 = pC[:, 0:HH, :].rearrange("p (j a) b -> p (j a b)", a=1).rearrange("p (j c) -> p j c", c=W64)
        ctr = pB[:, 0:HH, :].rearrange("p (j a) b -> p (j a b)", a=1).rearrange("p (j c) -> p j c", c=W64)
        l2b = pC[:, :, :].rearrange("p (b k) c -> p b (k c)", b=2)
        trb = pA[:, :, :].rearrange("p (b k) c -> p b (k c)", b=2)
        nb = pB[:, HH:J, :].rearrange("p j c -> p (j c)")
        c1 = pC[:, HH:J, :].rearrange("p (j a) b -> p (j a b)", a=1).rearrange("p (j c) -> p j c", c=W64)

        spill_g = nc.dram_tensor("spill_g", [16, P, T], F32, kind="Internal").ap()
        spill_z = nc.dram_tensor("spill_z", [H, P, T], F32, kind="Internal").ap()
        spill_p = nc.dram_tensor("spill_p", [KT, P, T], F32, kind="Internal").ap()

        U = Units()
        for i in range(4):
            U.add(("pl", i), a["w_plp"][i], 4 * P)
        for t in range(KT):
            U.add(("glb", t), a["w_in"][KT + t], KT * P)
            U.add(("gla", t), a["w_in"][t], KT * P)
        U.add(("ab",), a["w_ab"], KT * 32)

        def qkv_units(half):
            for h in range(HH * half, HH * half + HH):
                for i in range(3):
                    U.add(("qkv", 3 * h + i), a["w_in"][(2 + i) * KT + h], KT * P)

        qkv_units(0)
        for i in range(16):
            U.add(("gate", i), a["w_in"][6 * KT + i], KT * P)
        qkv_units(1)
        for i in range(8):
            U.add(("z", i), a["w_in"][5 * KT + i], KT * P)
        for nm in ("co", "do", "wo"):
            for i in range(KT):
                U.add((nm, i), a["w_" + nm][i], KT * P)

        def ffn_units(f):
            for m in range(FT):
                U.add(("fg" + f, m), a["w_gu" + f][m], KT * P)
                U.add(("fu" + f, m), a["w_gu" + f][FT + m], KT * P)
            for m in range(KT):
                for i in range(2):
                    U.add(("fd" + f, 2 * m + i), a["w_dn" + f][m, i], KH * P)

        MIX = [("mk", 0), ("mv", 0), ("mq", 0), ("mq", 1), ("mq", 2), ("mu", 3), ("mq", 3),
               ("mu", 2), ("mu", 1), ("mu", 0)]
        MFILL = MIX[5:]
        COL = {"mu": 0, "mq": 4, "mk": 8, "mv": 9}

        ffn_units("0")
        for i in range(KT):
            U.add(("pg", i), a["w_pg"][i], KT * P)
        ffn_units("1")
        for key in MIX:
            U.add(key, a["w_in2"][COL[key[0]] + key[1]], KT * P)
        for i in range(KT):
            U.add(("mo", i), a["w_out2"][i], KT * P)
        ffn_units("2")
        N_UNITS = len(U.src)

        O = Outs()
        AUX = {}

        def aux(key, reader):
            O.add(key, reader)
            AUX[key] = len(AUX)

        for t in range(KT):
            O.add(("pl", t), "A")
        for t in range(KT):
            O.add(("glb", t), "A")
            O.add(("gla", t), "D")
        O.add(("ab",), "D")
        aux(("gc",), "A")

        def qkv_outs(half):
            for q in range(3 * HH):
                O.add(("qkv", 3 * HH * half + q), "A")

        qkv_outs(0)
        for i in range(16):
            O.add(("gate", i), "A")
        qkv_outs(1)
        aux(("mean",), "A")
        for i in range(4):
            O.add(("z", i), "A")
        aux(("var",), "A")
        for i in range(4, 8):
            O.add(("z", i), "A")
        for i in range(8):
            O.add(("co", i), "D")
        for h in range(H):
            aux(("on", h), "D")
        for i in range(8):
            O.add(("do", i), "D")
        for i in range(8):
            O.add(("wo", i), "D")

        def ffn_outs(f):
            for m in range(FT):
                O.add(("fg" + f, m), "D")
                O.add(("fu" + f, m), "D")
            for m in range(KT):
                O.add(("fd" + f, m), "D" if f == "0" else "A")

        ffn_outs("0")
        for i in range(KT):
            O.add(("pg", i), "D")
        ffn_outs("1")
        MAUX = {2: [("rp", 3)], 8: [("rp", 4), ("yp", 3)], 11: [("yp", 2)], 14: [("yp", 1)]}
        O.add(("mk", 0), "D")
        O.add(("mv", 0), "D")
        O.add(("mq", 0), "D")
        aux(("rp", 0), "D")
        aux(("vt",), "A")
        O.add(("mq", 1), "D")
        aux(("rp", 1), "D")
        O.add(("mq", 2), "D")
        aux(("rp", 2), "D")
        for i, key in enumerate(MFILL):
            O.add(key, "D")
            for k in MAUX.get(3 * i + 2, []):
                aux(k, "D" if k[0] == "rp" else "A")
        aux(("yp", 0), "A")
        for i in range(KT):
            O.add(("mo", i), "A")
        ffn_outs("2")

        NORMS = [KT] * 8 + [PT_] * 2 + [KT] * 3
        SQ = [sum(NORMS[:i]) for i in range(len(NORMS))]
        AD = [sum(NORMS[:i]) - 2 * i for i in range(len(NORMS))]

        TAPS = [(2 * pr + i, j) for pr in range(KT // 2) for j in range(CK) for i in range(2) if 2 * pr + i < KT - 1]
        taps_unit = 12
        A_, B_ = 4, 4
        GAP = [16, 12, 4] + [A_, B_] * (LEVELS - 1) + [4, 5, 6, 6, 3]
        TAP = [0, 4, 0] + [0, 3] * (LEVELS - 1) + [0, 2, 5, 5, 6]
        NORM_AT = 8
        UNIT = 3 * KT
        assert sum(GAP) == 4 * UNIT and taps_unit * (KT - 2) + 4 * sum(TAP) >= len(TAPS)

        def cslot(t):
            return cacc[:, t, :] if t < 2 else cpad[:, t - 2, 0:T]

        def csum_in(t):
            return oT[:, KT - 1] if t == KT - 1 else cslot(t)

        def wait(eng, name, value):
            if not isinstance(value, int) or value > 0:
                eng.wait_ge(S(name), value)

        def ev_wait(eng, key):
            o = O.at[key]
            eng.wait_ge(S("ev" + O.reader[o]), O.count(o))

        def unit_out(eng, key, n=None):
            eng.wait_ge(S("gemm"), (U.at[key] if n is None else n) + 1)

        def aux_out(eng, key):
            eng.wait_ge(S("aux"), AUX[key] + 1)

        def bank(key):
            return pg[:, O.at[key] % 2, :]

        def quad(ap, n=HH):
            return ap.rearrange("p (n c) -> p n c", n=n)

        pa2 = pA[:, :, :].rearrange("p (b h k) c -> p b h (k c)", b=2, h=2)
        pb2 = pB[:, :, :].rearrange("p (b h k) c -> p b h k c", b=2, h=2)
        pc2 = pC[:, :, :].rearrange("p (b k) c -> p b (k c)", b=2)

        def chunk(d, r):
            return r if d == 0 else NC - 1 - r

        def filler(R):
            name, i = (("gate", 4 * R) if R < 4 else ("z", 4 * (R - 4)) if R < 6 else ("co", 4 * (R - 6)))
            return [(name, i + f) for f in range(4)]

        def parts(R, g):
            q, end = sum(GAP[:g]), sum(GAP[:g + 1])
            while q < end:
                f = q // UNIT
                e = min(end, (f + 1) * UNIT)
                yield filler(R)[f], q - f * UNIT, e - f * UNIT
                q = e

        def filled(R, g):
            return [key for key, q, e in parts(R, g) if e == UNIT]

        tmps = (tmp1, tmp2)
        SETS = ["h", "conv", "o", "ffn0", "pg", "ffn1", "mix", "out", "ffn2"]

        def set_count(s, t):
            return SETS.index(s) * KT + t + 1

        block = ctx.enter_context(nc.Block())

        @block.sync
        def _(sp):
            def load(n, src=None, i=0):
                if not (isinstance(i, int) and n < 4):
                    sp.wait_ge(S("w_lo"), n - 3 + 4 * i)
                sp.dma_start(w_raw[:, n % 4, 0:U.cols[n]], U.src[n] if src is None else src)\
                    .then_inc(S(f"w_in{n % 4}"), 16)

            def side(t, src, ready):
                sp.wait_ge(S(ready[0]), ready[1])
                sp.dma_start(tmps[t % 2][:], src).then_inc(S(f"side{t % 2}"), 16)

            def ev(key):
                return ("ev" + O.reader[O.at[key]], O.count(O.at[key]))

            sp.dma_start(praw[:], a["p"]).then_inc(S("in_p"), 16)
            load(0)
            sp.dma_start(xin[:], a["x"]).then_inc(S("in_x"), 16)
            sp.dma_start(consts[:], a["consts"]).then_inc(S("in_c"), 16)
            sp.dma_start(vec[:], a["vec"]).then_inc(S("in_v"), 16)
            load(1)
            sp.dma_start(swt[:], a["swt"]).then_inc(S("in_s"), 16)
            sp.dma_start(gate_p[:], a["gate_p"]).then_inc(S("in_g"), 16)
            for n in range(2, U.at[("fg0", 0)] + 4):
                for t in range(KT):
                    if n == U.at[("co", max(t - 1, 0))] + 4:
                        if t < 2:
                            sp.wait_ge(S(f"spill{t}"), 16 * 12)
                        side(t, spill_g[t], ("spill1", 16 * 12) if t < 2 else ev(("co", t - 2)))
                    if n == U.at[("do", 0)] + 4:
                        side(t, spill_z[t], ev(("co", 6 + t)) if t < 2 else ("on_z", t - 1))
                    if n == U.at[("do", max(t - 1, 0))] + 4:
                        if t < 2:
                            sp.wait_ge(S("s_upd"), 6)
                            sp.wait_ge(S("o_acc"), 8)
                        else:
                            sp.wait_ge(S("yv"), t - 1)
                        sp.dma_start(gst[:, t % 2], spill_g[KT + t]).then_inc(S(f"sgb{t % 2}"), 16)
                    if n == U.at[("wo", max(t - 1, 0))] + 4:
                        side(t, a["x"][:, t], ("on_z", 7 + t) if t < 2 else ev(("wo", t - 2)))
                load(n)
                if n == U.at[("glb", 5)]:
                    sp.wait_ge(S("plf"), KT)
                    sp.dma_start(spill_p.rearrange("t p n -> p t n"), ptile[:]).then_inc(S("spp"), 16)

            def ffn(f, more):
                g0 = U.at[("fg" + f, 0)]
                with sp.Fori(1, FT // 2) as i:
                    for j in range(4):
                        at_ = bass.ds(2 * i + (j // 2 + (j % 2) * FT), 1)
                        load(g0 + j, a["w_gu" + f][at_].rearrange("a p c -> (a p) c"), i)
                for n in range(U.at[("fd" + f, 0)], more):
                    if n == U.at[("pg", 0)] + 2:
                        unit_out(sp, ("fd0", 2 * KT - 1))
                        sp.dma_start(pl[:], spill_p.rearrange("t p n -> p t n")).then_inc(S("in_pl"), 16)
                    if n == U.at[("mk", 0)] + 3:
                        unit_out(sp, ("fd1", 2 * KT - 1))
                        sp.dma_start(c2[:], a["c2"]).then_inc(S("in_c2"), 16)
                    load(n)

            sp.dma_start(rpos[:], a["pos"]).then_inc(S("in_r"), 16)
            ffn("0", U.at[("fg1", 0)] + 4)
            ffn("1", U.at[("fg2", 0)] + 4)
            ffn("2", N_UNITS)
            for t in range(KT):
                sp.wait_ge(S("xu"), 2 * KT + t + 1)
                sp.dma_start(out[t], x[:, t]).then_inc(S("out"), 16)
            sp.wait_ge(S("out"), 16 * KT)

        @block.tensor
        def _(pe):
            def begin(key):
                o = O.at[key]
                if o >= 2:
                    q = o - 2
                    pe.wait_ge(S("ev" + O.reader[q]), O.count(q))
                return pg[:, o % 2, :]

            def products(n, act, k_n, dst, w_of, part=None, first=True, last=True, ready=None):
                hi, lo = act
                todo = [(k, w, b) for k in range(k_n) for w, b in ((w_hi, hi), (w_hi, lo), (w_lo, hi))]
                for q in range(*(part or (0, len(todo)))):
                    k, w, b = todo[q]
                    if ready and q % 3 == 0:
                        pe.wait_ge(S(ready[0]), ready[1] + k)
                    ins = pe.matmul(dst, w_of(w, n % 2, k), b(k), start=first and q == 0,
                                    stop=last and q == len(todo) - 1)
                return ins

            def fresh(s):
                return ("a_lo", set_count(s, 0))

            def w_tile(w, slot, k):
                return w[:, slot, k * P:(k + 1) * P]

            def act_a(k0=0):
                return (lambda k: a_hi[:, k0 + k, :]), (lambda k: a_lo[:, k0 + k, :])

            def unit(key, act=None, part=None, ready=None):
                n = U.at[key]
                if part is None or part[0] == 0:
                    pe.wait_ge(S("w_lo"), n + 1)
                    begin(key)
                ins = products(n, act or act_a(), KT, bank(key), w_tile, part, ready=ready)
                if part is None or part[1] == UNIT:
                    ins.then_inc(S("gemm"), 1)

            def column_sums(key, src, lhs=ones):
                pe.matmul(begin(key), lhs, src, start=True, stop=True).then_inc(S("aux"), 1)

            def token_sums(dst, srcs):
                for c in range(NC):
                    for q, src in enumerate(srcs):
                        ins = pe.matmul(dst[:, c:c + 1], src[:, c * P:(c + 1) * P], ones[:, 0:1], start=q == 0,
                                        stop=q == len(srcs) - 1)
                return ins

            def spread(dst, factors):
                for c in range(NC):
                    ins = pe.matmul(dst[:, c * P:(c + 1) * P], factors[:, c:c + 1].to_broadcast([P, P]), ident,
                                    start=True, stop=True)
                return ins

            def norm(nu):
                n = NORMS[nu]
                pe.wait_ge(S("add"), AD[nu] + n - 2)
                pe.wait_ge(S("sq"), SQ[nu] + n)
                wait(pe, "rstd", nu)
                token_sums(nb[:, 0:NC], (acc[:], sq[:, (n - 1) % 2, :])).then_inc(S("nsum"), 1)

            def norm_out(nu):
                pe.wait_ge(S("recip"), nu + 1)
                spread(nb, nst[:, 1, 0:NC]).then_inc(S("nout"), 1)

            pe.wait_ge(S("p_lo"), 1)
            for n in range(4):
                pe.wait_ge(S("w_lo"), n + 1)
                for q in range(2):
                    dst = begin(("pl", 2 * n + q))
                    ins = products(n, ((lambda k: p_hi[:, k, :]), (lambda k: p_lo[:, k, :])), 2, dst,
                                   lambda w, s, k: w[:, s, (2 * q + k) * P:(2 * q + k + 1) * P])
                ins.then_inc(S("gemm"), 1)
            pe.wait_ge(S("in_c"), 16)
            norm(0)
            norm_out(0)
            for t in range(KT):
                unit(("glb", t), ready=None if t else fresh("h"))
                unit(("gla", t))
                if t == 1:
                    norm(1)
                if t == 2:
                    norm_out(1)
            n = U.at[("ab",)]
            pe.wait_ge(S("w_lo"), n + 1)
            dst = begin(("ab",))
            for c in range(NC):
                tok = slice(c * P, (c + 1) * P)
                for k in range(KT):
                    for p_, (b, w) in enumerate(((a_hi, w_hi), (a_lo, w_hi), (a_hi, w_lo))):
                        ins = pe.matmul(dst[:, c * 32:(c + 1) * 32], b[:, k, tok],
                                        w[:, n % 2, k * 32:(k + 1) * 32],
                                        start=k == 0 and p_ == 0, stop=k == KT - 1 and p_ == 2)
            ins.then_inc(S("gemm"), 1)
            pe.wait_ge(S("g_raw"), 1)
            dst = begin(("gc",))
            for d in range(2):
                pe.matmul(quad(dst[:, 0:64], NC)[:, :, d * 8:d * 8 + 8], tri[d], gat[:, 0, :, d * 8:d * 8 + 8],
                          start=True, stop=True)
            pe.matmul(quad(dst[:, 64:128], NC), ones, gat[:, 0], start=True, stop=True).then_inc(S("aux"), 1)

            def qkv(half):
                if half:
                    pe.wait_ge(S("o_acc"), NC)
                    pe.wait_ge(S("s_upd"), NC - 1)
                for hh in range(HH + 1):
                    h = HH * half + hh
                    if hh < HH:
                        unit(("qkv", 3 * h))
                    if hh:
                        pe.wait_ge(S("l2sq"), 2 * h)
                        for i in range(2):
                            ins = token_sums(nb[:, NC * i:NC * i + NC], (sq[:, i, :],))
                        ins.then_inc(S("l2s"), 1)
                    if hh < HH:
                        unit(("qkv", 3 * h + 1))
                    if hh:
                        pe.wait_ge(S("l2i"), h)
                        wait(pe, "qk_fin", 2 * (h - 1))
                        for i in range(2):
                            spread(l2b[:, i], nst[:, 1, NC * i:NC * i + NC]).then_inc(S("l2f"), 1)
                    if hh < HH:
                        unit(("qkv", 3 * h + 2))
                    if hh:
                        pe.wait_ge(S("qk_fin"), 2 * h)
                        wait(pe, "trc", 2 * (h - 1))
                        for c in range(NC):
                            ins = pe.transpose(trb[:, 0, c * P:(c + 1) * P], kT[:, hh - 1, c * P:(c + 1) * P], ident)
                        ins.then_inc(S("trp"), 1)
                        pe.wait_ge(S("silu"), 3 * h)
                        for c in range(NC):
                            ins = pe.transpose(trb[:, 1, c * P:(c + 1) * P],
                                               sacc[:, (h - 1) % 2, 2, c * P:(c + 1) * P], ident)
                        ins.then_inc(S("trp"), 1)

            def gap(R, g):
                for key, q, e in parts(R, g):
                    unit(key, part=(q, e))

            halves = (slice(0, W64), slice(W64, P))

            def turned(dst, src, s):
                if s == halves[0]:
                    return pe.transpose(dst, src, id64[s, :])
                return pe.matmul(dst, src, id64[s, :], start=True, stop=True)

            def small(dst, lhs, rhs):
                for j in range(J):
                    for s in halves:
                        if rhs is None:
                            ins = turned(dst[s, j, :], lhs[s, j, :], s)
                        else:
                            ins = pe.matmul(dst[s, j, :], lhs[s, j, :], rhs[s, j, :], start=True, stop=True)
                return ins

            def delta(R):
                half, r = divmod(R, NC)
                prob = [(j, j // HH, j % HH, chunk(j // HH, r)) for j in range(J)]
                wait(pe, "g_all", 1)
                wait(pe, "o_acc", R)
                if r == 0:
                    pe.wait_ge(S("trc"), 2 * HH * (half + 1))
                for j, d, hh, c in prob:
                    g_col = gat[:, 0, c, d * 8 + HH * half + hh:d * 8 + HH * half + hh + 1]
                    ins = pe.matmul(pA[:, j, :], g_col.to_broadcast([P, P]), tri[d], start=True, stop=True)
                ins.then_inc(S("grow"), 1)
                for j, d, hh, c in prob:
                    tok = slice(c * P, (c + 1) * P)
                    ins = pe.matmul(pB[:, j, :], kT[:, hh, tok], kT[:, hh, tok], start=True, stop=True)
                ins.then_inc(S("gram"), 1)
                gap(R, 0)
                pe.wait_ge(S("eg"), R + 1)
                for j, d, hh, c in prob:
                    tok = slice(c * P, (c + 1) * P)
                    ins = pe.matmul(pA[:, j, :], kT[:, hh, tok], qT[:, hh, tok], start=True, stop=True)
                ins.then_inc(S("kq"), 1)
                gap(R, 1)
                for lv in range(LEVELS):
                    pe.wait_ge(S("ls"), LEVELS * R + lv + 1)
                    if lv == 0:
                        wait(pe, "s_upd", (NC - 1) * half + r)
                        small(c0, ls[:, 0], None).then_inc(S("y"), 1)
                        gap(R, 2)
                        continue
                    pe.wait_ge(S("u_upd"), LEVELS * R + lv)
                    small(c0, ls[:, lv % 2], ub).then_inc(S("y"), 1)
                    if lv > 1:
                        small(ctr, ub, None).then_inc(S("tr"), 1)
                    gap(R, 2 * lv + 1)
                    pe.wait_ge(S("ycp"), LEVELS * R + lv)
                    wait(pe, "tcp", (LEVELS - 1) * R + lv - 1)
                    small(c1, tb, yb).then_inc(S("uy"), 1)
                    gap(R, 2 * lv + 2)
                pe.wait_ge(S("u_upd"), LEVELS * (R + 1))
                lo, hi = halves
                for j in range(J):
                    s, b = (hi, lo) if j < HH else (lo, hi)
                    ins = pe.matmul(c0[b, j, :], en[s, j, b], en[s, j, s], start=True, stop=True)
                ins.then_inc(S("yf"), 1)
                for j in range(J):
                    b = lo if j < HH else hi
                    ins = turned(ctr[b, j, :], en[b, j, b], b)
                ins.then_inc(S("tr"), 1)
                gap(R, 13)
                pe.wait_ge(S("ycp"), LEVELS * (R + 1))
                pe.wait_ge(S("tcp"), (LEVELS - 1) * (R + 1))
                for j in range(J):
                    b = lo if j < HH else hi
                    ins = pe.matmul(c1[b, j, :], tb[b, j, :], yb[b, j, :], start=True, stop=True)
                ins.then_inc(S("u12"), 1)
                gap(R, 14)
                pe.wait_ge(S("u12s"), R + 1)
                pe.wait_ge(S("kb"), R + 1)
                pe.wait_ge(S("qk"), R + 1)
                for j in range(J):
                    ins = pe.matmul(pA[:, j, :], kb[:, j, :], en[:, j, :], start=True, stop=True)
                ins.then_inc(S("wt"), 1)
                gap(R, 15)
                pe.wait_ge(S("bv"), R + 1)
                pe.wait_ge(S("wtcp"), R + 1)
                wait(pe, "s_upd", (NC - 1) * half + r)
                for j in range(J):
                    ins = pe.matmul(pB[:, j, :], en[:, j, :], bv[:, j, :], start=True, stop=r == 0)
                    if r:
                        ins = pe.matmul(pB[:, j, :], kb[:, j, :], st[:, j, :], start=False, stop=True)
                ins.then_inc(S("vn"), 1)
                gap(R, 16)
                pe.wait_ge(S("vcp"), R + 1)
                pe.wait_ge(S("qdm"), R + 1)
                for j in range(J):
                    if r:
                        pe.matmul(pA[:, j, :], st[:, j, :], qd[:, j, :], start=True, stop=False)
                    ins = pe.matmul(pA[:, j, :], bv[:, j, :], et[:, j, :], start=r == 0, stop=True)
                ins.then_inc(S("o"), 1)
                if r < NC - 1:
                    pe.wait_ge(S("kt"), R + 1)
                    for j in range(J):
                        ins = pe.matmul(pC[:, j, :], kt[:, j, :], bv[:, j, :], start=True, stop=True)
                    ins.then_inc(S("s"), 1)
                gap(R, 17)

            qkv(0)
            for R in range(4):
                delta(R)
            qkv(1)
            pe.wait_ge(S("csum"), KT - 1)
            column_sums(("mean",), acc[:])
            delta(4)
            pe.wait_ge(S("cva"), KT - 1)
            column_sums(("var",), rstd[:])
            delta(5)
            pe.wait_ge(S("a_lo"), set_count("conv", KT - 1))
            delta(6)
            delta(7)
            for h in range(H):
                pe.wait_ge(S("onsq"), h + 1)
                token_sums(nb[:, NC * h:NC * h + NC], (sq[:, h % 2, :],)).then_inc(S("ons"), 1)
            pe.wait_ge(S("on_r"), 1)
            for h in range(H):
                spread(begin(("on", h)), ost[:, NC * h:NC * h + NC]).then_inc(S("aux"), 1)
            for t in range(KT):
                unit(("do", t), ready=None if t else fresh("o"))
            for t in range(KT):
                unit(("wo", t), ((lambda k: yb_hi[:, k, :]), (lambda k: yb_lo[:, k, :])),
                     ready=None if t else ("yb_lo", 1))

            def ffn(f, nu, s):
                def step(i):
                    for j in range(4):
                        nm = ("fg" if j % 2 == 0 else "fu") + f
                        n = U.at[(nm, j // 2)] + 4 * i
                        pe.wait_ge(S("w_lo"), n + 1)
                        if isinstance(i, int):
                            dst = begin((nm, 2 * i + j // 2))
                        else:
                            o = O.at[(nm, 2 + j // 2)]
                            pe.wait_ge(S("evD"), O.count(o - 2) - 4 + 4 * i)
                            dst = pg[:, o % 2, :]
                        first = isinstance(i, int) and i == 0
                        if first and j == 1:
                            products(U.at[(nm, j // 2)], act_a(), KT, dst, w_tile, (0, NORM_AT))
                            norm_out(nu)
                        products(U.at[(nm, j // 2)], act_a(), KT, dst, w_tile,
                                 (NORM_AT, UNIT) if first and j == 1 else None,
                                 ready=fresh(s) if first and j == 0 else None).then_inc(S("gemm"), 1)
                        if first and j == 0:
                            norm(nu)

                step(0)
                with pe.Fori(1, FT // 2) as i:
                    step(i)
                for m in range(KT):
                    dst = begin(("fd" + f, m))
                    for q in range(2):
                        n = U.at[("fd" + f, 2 * m + q)]
                        pe.wait_ge(S("w_lo"), n + 1)
                        products(n, ((lambda k: h_hi[:, KH * q + k, :]), (lambda k: h_lo[:, KH * q + k, :])),
                                 KH, dst, w_tile, None, q == 0, q == 1,
                                 None if m else ("h_lo", FT * int(f) + KH * q + 1)).then_inc(S("gemm"), 1)

            ffn("0", 2, "ffn0")
            for t in range(KT):
                if t == 1:
                    unit(("pg", t), part=(0, NORM_AT))
                    norm_out(3)
                unit(("pg", t), part=(NORM_AT, UNIT) if t == 1 else None, ready=None if t else fresh("pg"))
                if t == 0:
                    norm(3)
            norm(4)
            norm_out(4)
            ffn("1", 5, "ffn1")
            norm(6)
            norm_out(6)
            def rotate(i):
                if i == 0:
                    pe.wait_ge(S("in_c2"), 16)
                ev_wait(pe, ("mq", i - 1) if i else ("mk", 0))
                column_sums(("rp", i), zq[:, i], perm)

            def pooled(g):
                pe.wait_ge(S("wd"), PT_ - g)
                column_sums(("yp", g), wd[:, g], wpool[:, g])

            unit(("mk", 0), ready=fresh("mix"))
            norm(7)
            unit(("mv", 0), part=(0, NORM_AT))
            norm_out(7)
            unit(("mv", 0), part=(NORM_AT, UNIT))
            unit(("mq", 0))
            rotate(0)
            ev_wait(pe, ("mv", 0))
            dst = begin(("vt",))
            for c in range(NB):
                ins = pe.transpose(dst[:, c * P:(c + 1) * P], zv[:, c * P:(c + 1) * P], ident)
            ins.then_inc(S("aux"), 1)
            unit(("mq", 1))
            rotate(1)
            unit(("mq", 2))
            rotate(2)
            heads = (slice(0, HD2), slice(HD2, P))

            def scores(s):
                i, n = divmod(s, NB)
                pe.wait_ge(S("qk2"), i + 2)
                wait(pe, "smask", s - 1)
                k0 = 1 if n == 0 else 0
                pe.matmul(pa2[:, s % 2, :, k0 * P:2 * P], qk2[:, i, n * P:(n + 1) * P],
                          kz[:, :, (n - 1 + k0) * P:(n + 1) * P], start=True, stop=True).then_inc(S("scores"), 1)

            def turn(s):
                k0 = 1 if s % NB == 0 else 0
                pe.wait_ge(S("prob"), s + 1)
                wait(pe, "ptcp", s - 1)
                for h in range(2):
                    for kb_ in range(k0, 2):
                        ins = pe.transpose(pb2[:, s % 2, h, kb_, :], sm[:, s % 3, h, kb_ * P:(kb_ + 1) * P], ident)
                ins.then_inc(S("turn"), 1)

            def values(s):
                i, n = divmod(s, NB)
                k0 = 1 if n == 0 else 0
                pe.wait_ge(S("ptcp"), s + 1)
                if s == 0:
                    ev_wait(pe, ("vt",))
                if n == 0:
                    wait(pe, "oat", i - 1)
                for h in range(2):
                    for kb_ in range(k0, 2):
                        ins = pe.matmul(pc2[heads[h], i % 2, n * P:(n + 1) * P],
                                        vt2[:, n - 1 + kb_, heads[h]], ptb[:, s % 2, h, kb_, :],
                                        start=kb_ == k0, stop=kb_ == 1)
                ins.then_inc(S("values"), 1)

            for s in range(16 + 3):
                if s < 16:
                    scores(s)
                if 0 <= s - 2 < 16:
                    turn(s - 2)
                if 0 <= s - 3 < 16:
                    values(s - 3)
                if s < 15:
                    unit(MFILL[s // 3], part=(s % 3 * UNIT // 3, (s % 3 + 1) * UNIT // 3))
                for k in MAUX.get(s, []):
                    (rotate if k[0] == "rp" else pooled)(k[1])
            pooled(0)

            norm(8)
            norm_out(8)
            norm(9)
            norm_out(9)
            for t in range(KT):
                unit(("mo", t), ready=None if t else fresh("out"))
            norm(10)
            norm_out(10)
            ffn("2", 11, "ffn2")
            norm(12)
            norm_out(12)

        @block.scalar
        def _(act):
            def hi(n, i=0, cols=None):
                act.wait_ge(S(f"w_in{n % 4}"), 16 * (n // 4 + 1) + 16 * i)
                if not (isinstance(i, int) and n < 2):
                    act.wait_ge(S("gemm"), n - 1 + 4 * i)
                c = U.cols[n] if cols is None else cols
                act.activation(w_hi[:, n % 2, 0:c], w_raw[:, n % 4, 0:c], ACT.Copy).then_inc(S("w_hi"), 1)

            def after(key):
                n = U.at[key]
                unit_out(act, key)
                if n + 2 < N_UNITS:
                    hi(n + 2)

            def square(nu, t, src):
                if t == 0:
                    wait(act, "nsum", nu)
                    dst = acc[:]
                else:
                    wait(act, "add", AD[nu] + t - 2 if t > 2 else 0)
                    dst = sq[:, t % 2, :]
                act.activation(dst, src, ACT.Square).then_inc(S("sq"), 1)

            def root(nu):
                act.wait_ge(S("nsum"), nu + 1)
                act.activation(nst[:, 0, 0:NC], nb[:, 0:NC], ACT.Sqrt, scale=1.0 / (P * NORMS[nu]),
                               bias=eps_t[:, 0:1]).then_inc(S("root"), 1)

            def high_o(h):
                act.wait_ge(S("on_z"), h + 1)
                act.activation(a_hi[:, h], oT[:, h], ACT.Copy).then_inc(S("a_hi"), 1)

            act.wait_ge(S("in_p"), 16)
            act.activation(p_hi[:], praw[:], ACT.Copy).then_inc(S("p_hi"), 1)
            hi(0)
            hi(1)
            act.wait_ge(S("in_x"), 16)
            for t in range(KT):
                square(0, t, xin[:, t])
            for n in range(4):
                after(("pl", n))
                for q in range(2):
                    t = 2 * n + q
                    act.activation(ptile[:, t], bank(("pl", t)), ACT.Copy).then_inc(S("evA"), 1)
            act.wait_ge(S("in_g"), 16)
            root(0)
            for t in range(KT):
                act.wait_ge(S("hx"), t + 1)
                act.activation(a_hi[:, t], xin[:, t], ACT.Copy).then_inc(S("a_hi"), 1)
            act.wait_ge(S("evA"), 8)
            for t in range(KT):
                square(1, t, ptile[:, t])
            for t in range(KT):
                after(("glb", t))
                if t >= 2:
                    ev_wait(act, ("gla", t - 2))
                act.activation(tmps[t % 2][:], bank(("glb", t)), ACT.Sigmoid).then_inc(S("evA"), 1)
                after(("gla", t))
                if t == 1:
                    root(1)
            after(("ab",))
            act.wait_ge(S("in_g"), 16)
            act.activation(gat[:, 5, 0, :], gate_p[:, 0:16], ACT.Exp).then_inc(S("gA"), 1)
            act.wait_ge(S("gD"), 1)
            act.activation(gat[:, 2], gat[:, 3], ACT.Exp).then_inc(S("gA"), 1)
            act.wait_ge(S("gA"), 2)
            act.activation(gat[:, 4], gat[:, 2], ACT.Ln, bias=1.0).then_inc(S("gA"), 1)
            ev_wait(act, ("ab",))
            act.activation(gat[:, 1], gat[:, 1], ACT.Sigmoid).then_inc(S("gA"), 1)
            aux_out(act, ("gc",))
            b = bank(("gc",))
            act.activation(gat[:, 2], quad(b[:, 0:64], NC), ACT.Copy).then_inc(S("gA"), 1)
            act.activation(gat[:, 4], quad(b[:, 64:128], NC), ACT.Copy).then_inc(S("evA"), 1)
            act.wait_ge(S("gA"), 5)
            act.activation(gat[:, 3], gat[:, 2], ACT.Exp).then_inc(S("gA"), 1)
            ev_wait(act, ("gc",))
            act.activation(gat[:, 5], gat[:, 4], ACT.Exp).then_inc(S("gA"), 1)
            act.wait_ge(S("gD"), 3)
            act.activation(gat[:, 4], gat[:, 4], ACT.Exp).then_inc(S("g_all"), 1)

            def qkv(half):
                def padded(h, i):
                    key = ("qkv", 3 * h + i)
                    unit_out(act, key)
                    if h == 0 and i == 0:
                        act.wait_ge(S("a_lo"), KT)
                        act.wait_ge(S("spp"), 16)
                    wait(act, "stap", SK * (3 * (h - 1) + i + 1))
                    act.activation(pad[:, i, SP_:SP_ + T], bank(key), ACT.Copy).then_inc(S("evA"), 1)
                    after(key)

                def silu(h, i):
                    act.wait_ge(S("stap"), SK * (3 * h + i + 1))
                    y = sacc[:, h % 2, i]
                    act.activation(y, y, ACT.Silu).then_inc(S("silu"), 1)
                    if i < 2:
                        act.wait_ge(S("silu"), 3 * h + i + 1)
                        wait(act, "l2s", h)
                        act.activation(sq[:, i, :], y, ACT.Square).then_inc(S("l2sq"), 1)

                for hh in range(HH + 1):
                    h = HH * half + hh
                    if hh < HH:
                        if hh == 0 and half:
                            act.wait_ge(S("o"), 4)
                            act.wait_ge(S("s_upd"), 3)
                        padded(h, 0)
                    if hh:
                        silu(h - 1, 2)
                        act.wait_ge(S("l2s"), h)
                        for i, s in enumerate((float(P), 1.0)):
                            c = slice(NC * i, NC * i + NC)
                            ins = act.activation(nst[:, 0, c], nb[:, c], ACT.Sqrt, scale=s, bias=eps_t[:, 1 + i:2 + i])
                        ins.then_inc(S("l2r"), 1)
                    if hh < HH:
                        padded(h, 1)
                        silu(h, 0)
                        padded(h, 2)
                        silu(h, 1)
                    if hh:
                        if half and hh == 1:
                            act.wait_ge(S("bv"), 4)
                            act.wait_ge(S("kb"), 4)
                            act.wait_ge(S("kt"), 4)
                        for i, dst in enumerate((ktok, vtok)):
                            act.wait_ge(S("trp"), 2 * (h - 1) + i + 1)
                            act.activation(dst[:, hh - 1], quad(trb[:, i], NC), ACT.Copy).then_inc(S("trc"), 1)

            spilled = [0]

            def gap(R, g):
                for key in filled(R, g):
                    after(key)
                    if key[0] == "co":
                        continue
                    k = spilled[0]
                    spilled[0] += 1
                    if k >= 2:
                        act.wait_ge(S(f"spill{k % 2}"), 16 * (k // 2))
                    else:
                        ev_wait(act, ("gla", 6 + k))
                    func, dst = (ACT.Sigmoid, spill_g[key[1]]) if key[0] == "gate" else (ACT.Silu, spill_z[key[1]])
                    act.activation(tmps[k % 2][:], bank(key), func).then_inc(S("evA"), 1)
                    ev_wait(act, key)
                    act.dma_start(dst, tmps[k % 2][:]).then_inc(S(f"spill{k % 2}"), 16)

            lo, hi_ = slice(0, W64), slice(W64, P)

            def delta(R):
                half, r = divmod(R, NC)
                act.wait_ge(S("pre"), 3 * R + 1)
                wait(act, "o", R)
                act.activation(qd[:], pA[:], ACT.Exp).then_inc(S("eg"), 1)
                act.wait_ge(S("pre"), 3 * R + 2)
                act.activation(en[:], en[:], ACT.Exp, scale=-1.0).then_inc(S("en"), 1)
                act.wait_ge(S("pre"), 3 * R + 3)
                act.activation(et[:], et[:], ACT.Exp).then_inc(S("et"), 1)
                act.wait_ge(S("L"), R + 1)
                wait(act, "ls", LEVELS * R)
                act.activation(lc[lo], en[lo, :, lo], ACT.Copy)
                act.activation(lc[hi_], en[hi_, :, hi_], ACT.Copy).then_inc(S("lc"), 1)
                gap(R, 0)
                gap(R, 1)
                for lv in range(1, LEVELS):
                    act.wait_ge(S("y"), LEVELS * R + lv + 1)
                    act.activation(yb[:], c0, ACT.Copy).then_inc(S("ycp"), 1)
                    gap(R, 2 * lv)
                    gap(R, 2 * lv + 1)
                act.wait_ge(S("yf"), R + 1)
                act.activation(yb[lo, 0:HH], c0[lo, 0:HH], ACT.Copy)
                act.activation(yb[hi_, HH:J], c0[hi_, HH:J], ACT.Copy).then_inc(S("ycp"), 1)
                gap(R, 12)
                gap(R, 13)
                act.wait_ge(S("wt"), R + 1)
                act.activation(kb[:, 0:HH], pA[:, 0:HH], ACT.Copy, scale=-1.0)
                act.activation(kb[:, HH:J], pA[:, HH:J], ACT.Copy, scale=-1.0).then_inc(S("wtcp"), 1)
                gap(R, 14)
                gap(R, 15)
                act.wait_ge(S("vn"), R + 1)
                act.activation(bv[:, 0:HH], pB[:, 0:HH], ACT.Copy)
                act.activation(bv[:, HH:J], pB[:, HH:J], ACT.Copy).then_inc(S("vcp"), 1)
                gap(R, 16)
                gap(R, 17)

            qkv(0)
            for R in range(4):
                delta(R)
            qkv(1)
            aux_out(act, ("mean",))
            act.activation(acc[:], bank(("mean",)), ACT.Copy, scale=1.0 / D).then_inc(S("evA"), 1)
            for t in range(KT):
                act.wait_ge(S("xc"), t + 1)
                if t > 2:
                    act.wait_ge(S("cva"), t - 2)
                act.activation(rstd[:] if t == 0 else sq[:, t % 2, :], cslot(t), ACT.Square).then_inc(S("cvs"), 1)
            delta(4)
            aux_out(act, ("var",))
            act.activation(acc[:], bank(("var",)), ACT.Sqrt, scale=1.0 / D, bias=eps_t[:, 3:4]).then_inc(S("evA"), 1)
            delta(5)
            for t in range(KT):
                act.wait_ge(S("xn"), t + 1)
                act.activation(cslot(t), cslot(t), ACT.Silu, scale=v("ln_g", t), bias=v("ln_b", t))\
                    .then_inc(S("ca"), 1)
            for t in range(KT):
                act.wait_ge(S("ca"), t + 1)
                act.activation(a_hi[:, t], cslot(t), ACT.Copy).then_inc(S("a_hi"), 1)
            delta(6)
            delta(7)
            for h in range(H):
                act.wait_ge(S("o_acc"), 8)
                if h >= 2:
                    act.wait_ge(S("ons"), h - 1)
                act.activation(sq[:, h % 2, :], oT[:, h], ACT.Square).then_inc(S("onsq"), 1)
            act.wait_ge(S("ons"), H)
            act.activation(ost[:], nb[:, 0:8 * NC], ACT.Sqrt, scale=1.0 / P, bias=eps_t[:, 0:1])\
                .then_inc(S("on_root"), 1)
            for h in range(H):
                high_o(h)
            for t in range(KT):
                after(("do", t))
                act.wait_ge(S("yv"), t + 1)
                act.activation(yb_hi[:, t], ya[:, t], ACT.Copy).then_inc(S("yb_hi"), 1)

            def xset(s, t, g, nu):
                act.activation(a_hi[:, t], x[:, t], ACT.Copy, scale=v(g, t)).then_inc(S("a_hi"), 1)
                square(nu, t, x[:, t])

            for t in range(KT):
                after(("wo", t))
                ev_wait(act, ("wo", t))
                xset("ffn0", t, "g_ffn", 2)

            def ffn(f, nu, g, nu2):
                def step(i):
                    for q in range(2):
                        n = U.at[("fg" + f, q)]
                        act.wait_ge(S("gemm"), n + 1 + 4 * i)
                        hi(n + 2, i, U.cols[n + 2 + (4 * i if isinstance(i, int) else 0)])
                        if q == 0 and isinstance(i, int) and i == 0:
                            root(nu)
                        dg = O.count(O.at[("fg" + f, q)])
                        act.wait_ge(S("evD"), dg + 4 * i)
                        act.activation(tmp1[:], tmp1[:], ACT.Silu).then_inc(S("sil"), 1)
                        act.wait_ge(S("gemm"), n + 2 + 4 * i)
                        hi(n + 3, i, U.cols[n + 3 + (4 * i if isinstance(i, int) else 0)])
                        act.wait_ge(S("hm"), FT * int(f) + q + 1 + 2 * i)
                        m = 2 * i + q
                        act.activation(h_hi[:, m] if isinstance(i, int) else
                                       h_hi[:, bass.ds(m, 1)].rearrange("p a n -> p (a n)"),
                                       tmp2[:], ACT.Copy).then_inc(S("h_hi"), 1)

                step(0)
                with act.Fori(1, FT // 2 - 1) as i:
                    step(i)
                step(FT // 2 - 1)
                if f == "0":
                    rope_tables()
                for m in range(KT):
                    after(("fd" + f, 2 * m))
                    after(("fd" + f, 2 * m + 1))
                    if f == "0":
                        ev_wait(act, ("fd" + f, m))
                        xset("pg", m, g, nu2)
                    else:
                        act.activation(hb[:, m], bank(("fd" + f, m)), ACT.Copy).then_inc(S("evA"), 1)
                        ev_wait(act, ("fd" + f, m))
                        square(nu2, m, hb[:, m])

            def rope_tables():
                act.wait_ge(S("rope"), 1)
                act.activation(rsin[:], rcos[:], ACT.Sin).then_inc(S("rsin"), 1)
                act.wait_ge(S("rsin"), 1)
                act.activation(rcos[:], rpos[:].bitcast(F32), ACT.Sin, scale=-1.0, bias=gate_p[:, 58:59])\
                    .then_inc(S("rsin"), 1)

            ffn("0", 2, "g_pl", 3)
            for t in range(KT):
                after(("pg", t))
                if t == 0:
                    root(3)
                ev_wait(act, ("pg", t))
                act.activation(tmps[t % 2][:], tmps[t % 2][:], ACT.Sigmoid).then_inc(S("pgs"), 1)
                act.wait_ge(S("x2"), t + 1)
                square(4, t, x[:, t])
            root(4)

            for t in range(KT):
                act.wait_ge(S("xf"), t + 1)
                xset("ffn1", t, "ffn1_pre", 5)
            ffn("1", 5, None, 6)

            def post(nu, k, s, g, nu2):
                root(nu)
                if s:
                    for t in range(KT):
                        act.wait_ge(S("xu"), KT * k + t + 1)
                        xset(s, t, g, nu2)

            post(6, 0, "mix", "mix_pre", 7)
            after(("mk", 0))
            root(7)
            after(("mv", 0))
            after(("mq", 0))
            aux_out(act, ("vt",))
            act.activation(vt2[:], quad(bank(("vt",)), NB), ACT.Copy).then_inc(S("evA"), 1)
            after(("mq", 1))
            after(("mq", 2))

            def prob(s):
                k0 = P if s % NB == 0 else 0
                act.wait_ge(S("bias"), s + 1)
                for h in range(2):
                    y = sm[:, s % 3, h, k0:]
                    act.activation(y, y, ACT.Exp, scale=HD2 ** -0.5, bias=sml[:, 1, s, h:h + 1],
                                   accum_out=sml[:, 2, s, h:h + 1])
                act.activation(sml[:, 3, s], sml[:, 3, s], ACT.Exp).then_inc(S("exp"), 1)

            def pt_copy(s):
                k0 = 1 if s % NB == 0 else 0
                act.wait_ge(S("turn"), s + 1)
                wait(act, "values", s - 1)
                act.activation(ptb[:, s % 2, :, k0:], pb2[:, s % 2, :, k0:], ACT.Copy).then_inc(S("ptcp"), 1)

            def pooled(g):
                aux_out(act, ("yp", g))
                act.activation(mo[:, g], bank(("yp", g)), ACT.Copy, scale=gate_p[:, 46 + g:47 + g])\
                    .then_inc(S("evA"), 1)
                ev_wait(act, ("yp", g))
                square(8, PT_ - 1 - g, mo[:, g])

            for s in range(16 + 3):
                if s < 16:
                    prob(s)
                if 0 <= s - 2 < 16:
                    pt_copy(s - 2)
                if s < 15 and s % 3 == 2:
                    after(MFILL[s // 3])
                for k in MAUX.get(s, []):
                    if k[0] == "yp":
                        pooled(k[1])
            pooled(0)
            root(8)
            for i in range(PT_):
                act.wait_ge(S("oat"), i + 1)
                square(9, i, mo[:, PT_ + i])
            for t in range(PT_):
                act.wait_ge(S("mh"), t + 1)
                act.activation(a_hi[:, t], mo[:, t], ACT.Copy).then_inc(S("a_hi"), 1)
            root(9)
            for t in range(PT_, KT):
                act.wait_ge(S("mh"), t + 1)
                act.activation(a_hi[:, t], mo[:, t], ACT.Copy).then_inc(S("a_hi"), 1)
            for t in range(KT):
                after(("mo", t))
                act.activation(hb2[:, t], bank(("mo", t)), ACT.Copy).then_inc(S("evA"), 1)
                ev_wait(act, ("mo", t))
                square(10, t, hb2[:, t])
            post(10, 1, "ffn2", "ffn2_pre", 11)
            ffn("2", 11, None, 12)
            post(12, 2, None, None, None)

        @block.vector
        def _(dve):
            def lo(n, i=0, cols=None):
                dve.wait_ge(S("w_hi"), n + 1 + 4 * i)
                c = U.cols[n] if cols is None else cols
                dve.tensor_tensor(w_lo[:, n % 2, 0:c], w_raw[:, n % 4, 0:c],
                                  w_hi[:, n % 2, 0:c].bitcast(F32), ALU.subtract).then_inc(S("w_lo"), 1)

            def after(key):
                if U.at[key] + 2 < N_UNITS:
                    lo(U.at[key] + 2)

            def recip(nu):
                dve.wait_ge(S("root"), nu + 1)
                wait(dve, "nout", nu)
                dve.reciprocal(nst[:, 1, 0:NC], nst[:, 0, 0:NC]).then_inc(S("recip"), 1)
                dve.wait_ge(S("nout"), nu + 1)
                dve.tensor_copy(rstd[:], nb).then_inc(S("rstd"), 1)
                dve.wait_ge(S("rstd"), nu + 1)

            def low(s, t, src, scale=None):
                dve.wait_ge(S("a_hi"), set_count(s, t))
                if scale is None:
                    ins = dve.tensor_tensor(a_lo[:, t], src, a_hi[:, t].bitcast(F32), ALU.subtract)
                else:
                    ins = dve.scalar_tensor_tensor(a_lo[:, t], src, scale, a_hi[:, t].bitcast(F32),
                                                   ALU.mult, ALU.subtract)
                ins.then_inc(S("a_lo"), 1)

            done_taps = [0]

            def taps(count):
                for q in range(done_taps[0], min(done_taps[0] + count, len(TAPS))):
                    t, j = TAPS[q]
                    src, w = cpad[:, t, j:j + T], vec[:, t, len(VEC) + j:len(VEC) + j + 1]
                    if j == 0:
                        ev_wait(dve, ("gla", t))
                        if t >= 2:
                            dve.wait_ge(S("tap"), TAPS.index((t - 2, CK - 1)) + 1)
                        ins = dve.tensor_scalar(cslot(t), src, w, v("conv_b", t), ALU.mult, ALU.add)
                    else:
                        dve.wait_ge(S("tap"), TAPS.index((t, j - 1)) + 1)
                        ins = dve.scalar_tensor_tensor(cslot(t), src, w, cslot(t), ALU.mult, ALU.add)
                    ins.then_inc(S("tap"), 1)
                done_taps[0] = min(done_taps[0] + count, len(TAPS))

            dve.memset(cpad[:, :, 0:CP], 0.0)
            dve.memset(cpad[:, :, CP + T:PAD], 0.0).then_inc(S("czero"), 1)
            dve.wait_ge(S("p_hi"), 1)
            dve.tensor_tensor(p_lo[:], praw[:], p_hi[:].bitcast(F32), ALU.subtract).then_inc(S("p_lo"), 1)
            lo(0)
            lo(1)
            for n in range(4):
                after(("pl", n))
            recip(0)
            dve.wait_ge(S("in_v"), 16)
            dve.wait_ge(S("in_x"), 16)
            for t in range(KT + 1):
                if t < KT:
                    dve.scalar_tensor_tensor(xin[:, t], xin[:, t], v("g_mix", t), rstd[:], ALU.mult, ALU.mult)\
                        .then_inc(S("hx"), 1)
                if t:
                    low("h", t - 1, xin[:, t - 1])
            dve.wait_ge(S("a_lo"), KT)
            dve.wait_ge(S("a_hi"), KT)
            dve.memset(pad[:, :, 0:SP_], 0.0)
            dve.memset(pad[:, :, SP_ + T:], 0.0).then_inc(S("pzero"), 1)
            dve.wait_ge(S("czero"), 1)
            for t in range(KT):
                after(("glb", t))
                unit_out(dve, ("gla", t))
                ev_wait(dve, ("glb", t))
                dve.tensor_tensor(cpad[:, t, CP:CP + T], bank(("gla", t)), tmps[t % 2][:], ALU.mult)\
                    .then_inc(S("evD"), 1)
                after(("gla", t))
                if t == 2:
                    recip(1)
                    for q in range(KT):
                        dve.wait_ge(S("sq"), 2 * KT)
                        dve.scalar_tensor_tensor(ptile[:, q], ptile[:, q], v("g_plp", q), rstd[:],
                                                 ALU.mult, ALU.mult).then_inc(S("plf"), 1)
                if t >= 2:
                    taps(taps_unit)
            after(("ab",))
            unit_out(dve, ("ab",))
            ab = quad(bank(("ab",))[:, 0:P], NC)
            dve.wait_ge(S("in_g"), 16)
            dt = gate_p[:, 16:32].unsqueeze(1).to_broadcast([P, NC, 16])
            dve.tensor_tensor(gat[:, 2], ab[:, :, 0:16], dt, ALU.add).then_inc(S("gd"), 1)
            dve.tensor_copy(gat[:, 1], ab[:, :, 16:32]).then_inc(S("evD"), 1)
            dve.wait_ge(S("gd"), 1)
            dve.scalar_tensor_tensor(gat[:, 3], gat[:, 2], -1.0, gat[:, 2], ALU.mult, ALU.min).then_inc(S("gd"), 1)
            dve.wait_ge(S("gd"), 2)
            dve.tensor_scalar(gat[:, 0], gat[:, 2], 0.0, None, ALU.max).then_inc(S("gD"), 1)
            dve.wait_ge(S("gD"), 1)
            dve.wait_ge(S("gA"), 3)
            dve.tensor_tensor(gat[:, 0], gat[:, 0], gat[:, 4], ALU.add).then_inc(S("gD"), 1)
            dve.wait_ge(S("gD"), 2)
            ea = gat[:, 5, 0, :].unsqueeze(1).to_broadcast([P, NC, 16])
            dve.scalar_tensor_tensor(gat[:, 0], gat[:, 0], -1.0, ea, ALU.mult, ALU.mult).then_inc(S("g_raw"), 1)
            dve.wait_ge(S("gA"), 7)
            dve.tensor_tensor(gat[:, 4], gat[:, 4], gat[:, 2], ALU.subtract).then_inc(S("gD"), 1)
            dve.tensor_tensor(gat[:, 3], gat[:, 3], gat[:, 1], ALU.mult).then_inc(S("g_k"), 1)

            def qkv(half):
                def short_taps(h, i):
                    n = 3 * h + i
                    ev_wait(dve, ("qkv", n))
                    if h == 0 and i == 0:
                        dve.wait_ge(S("in_s"), 16)
                        dve.wait_ge(S("pzero"), 1)
                    y = sacc[:, h % 2, i]
                    if i < 2:
                        wait(dve, "qk_fin", 2 * (h - 2) + i + 1)
                    else:
                        wait(dve, "trp", 2 * (h - 1))
                    for j in range(SK):
                        src, w = pad[:, i, j:j + T], swt[:, i * H + h, j:j + 1]
                        if j == 0:
                            ins = dve.tensor_scalar(y, src, w, None, ALU.mult)
                        else:
                            dve.wait_ge(S("stap"), SK * n + j)
                            ins = dve.scalar_tensor_tensor(y, src, w, y, ALU.mult, ALU.add)
                        ins.then_inc(S("stap"), 1)

                for hh in range(HH + 1):
                    h = HH * half + hh
                    if hh < HH:
                        after(("qkv", 3 * h))
                        if hh == 0 and half:
                            dve.wait_ge(S("o"), 4)
                            dve.memset(pad[:, :, 0:SP_], 0.0)
                            dve.memset(pad[:, :, SP_ + T:], 0.0).then_inc(S("pzero"), 1)
                            dve.wait_ge(S("pzero"), 2)
                        short_taps(h, 0)
                    if hh:
                        dve.wait_ge(S("l2r"), h)
                        dve.reciprocal(nst[:, 1], nst[:, 0]).then_inc(S("l2i"), 1)
                    if hh < HH:
                        after(("qkv", 3 * h + 1))
                    if hh:
                        for i, dst in enumerate((qT, kT)):
                            dve.wait_ge(S("l2f"), 2 * (h - 1) + i + 1)
                            if half and hh == 1:
                                dve.wait_ge(S("qdm"), 4)
                            dve.tensor_tensor(dst[:, hh - 1], sacc[:, (h - 1) % 2, i], l2b[:, i], ALU.mult)\
                                .then_inc(S("qk_fin"), 1)
                    if hh < HH:
                        short_taps(h, 1)
                        after(("qkv", 3 * h + 2))
                        short_taps(h, 2)

            def gap(R, g):
                done = [] if g % 2 and g < len(GAP) - 1 else \
                    [key for q in range(max(g - 2 + g % 2, 0), g + g % 2) for key in filled(R, q)]
                for key in done:
                    after(key)
                    if key[0] == "co":
                        t = key[1]
                        unit_out(dve, key)
                        dve.wait_ge(S(f"side{t % 2}"), 16 * (t // 2 + 1))
                        dve.tensor_tensor(ya[:, t], bank(key), tmps[t % 2][:], ALU.mult).then_inc(S("evD"), 1)
                if R < 4:
                    taps(TAP[g])

            lo_, hi_ = slice(0, W64), slice(W64, P)

            def delta(R):
                half, r = divmod(R, NC)

                def scal(k, j):
                    d, hh = divmod(j, HH)
                    q = d * 8 + HH * half + hh
                    return gat[:, k, chunk(d, r), q:q + 1]

                dve.wait_ge(S("grow"), R + 1)
                if r == 0:
                    dve.wait_ge(S("g_all"), 1)
                    dve.wait_ge(S("trc"), 2 * HH * (half + 1))
                wait(dve, "o", R)
                for d in range(2):
                    sl, q = slice(d * HH, d * HH + HH), d * 8 + HH * half
                    ins = dve.tensor_tensor(et[:, sl], pA[:, sl], gat[:, 2, chunk(d, r), q:q + HH].unsqueeze(2)
                                            .to_broadcast([P, HH, P]), ALU.subtract)
                ins.then_inc(S("pre"), 1)
                dve.wait_ge(S("pre"), 3 * R + 1)
                wait(dve, "vn", R)
                dve.tensor_scalar(en[:], et[:], 0.0, None, ALU.max).then_inc(S("pre"), 1)
                dve.wait_ge(S("pre"), 3 * R + 2)
                dve.tensor_scalar(et[:], et[:], 0.0, None, ALU.min).then_inc(S("pre"), 1)
                dve.wait_ge(S("gram"), R + 1)
                dve.wait_ge(S("en"), R + 1)
                for j in range(J):
                    ins = dve.scalar_tensor_tensor(en[:, j], pB[:, j], scal(1, j), en[:, j], ALU.mult, ALU.mult)
                ins.then_inc(S("L"), 1)
                gap(R, 0)
                gap(R, 1)
                dve.wait_ge(S("ls"), LEVELS * R + 1)
                i64 = id64.unsqueeze(1).to_broadcast([P, J, W64])
                dve.tensor_tensor(tb[:], i64, ls[:, 0], ALU.subtract)
                dve.wait_ge(S("y"), LEVELS * R + 1)
                dve.tensor_tensor(ub[:], i64, c0, ALU.subtract).then_inc(S("u_upd"), 1)
                dve.wait_ge(S("kq"), R + 1)
                dve.wait_ge(S("etm"), R + 1)
                for d in range(2):
                    s = slice(d * HH, d * HH + HH)
                    ins = dve.tensor_tensor(et[:, s], pA[:, s], et[:, s], ALU.mult)
                ins.then_inc(S("qk"), 1)
                gap(R, 2)
                for lv in range(1, LEVELS):
                    if lv > 1:
                        dve.wait_ge(S("tr"), (LEVELS - 1) * R + lv - 1)
                        dve.tensor_copy(tb[:], ctr).then_inc(S("tcp"), 1)
                    gap(R, 2 * lv + 1)
                    dve.wait_ge(S("uy"), (LEVELS - 1) * R + lv)
                    if lv < LEVELS - 1:
                        dve.tensor_tensor(ub[:], ub[:], c1, ALU.subtract).then_inc(S("u_upd"), 1)
                    else:
                        dve.tensor_tensor(en[lo_, :, lo_], ub[lo_], c1[lo_], ALU.subtract)
                        dve.tensor_tensor(en[hi_, :, hi_], ub[hi_], c1[hi_], ALU.subtract).then_inc(S("u_upd"), 1)
                    gap(R, 2 * lv + 2)
                dve.wait_ge(S("tr"), (LEVELS - 1) * (R + 1))
                dve.tensor_copy(tb[lo_, 0:HH], ctr[lo_, 0:HH])
                dve.tensor_copy(tb[hi_, HH:J], ctr[hi_, HH:J]).then_inc(S("tcp"), 1)
                dve.memset(en[hi_, 0:HH, lo_], 0.0)
                dve.memset(en[lo_, HH:J, hi_], 0.0)
                gap(R, 13)
                dve.wait_ge(S("u12"), R + 1)
                dve.tensor_scalar(en[lo_, 0:HH, hi_], c1[lo_, 0:HH], -1.0, None, ALU.mult)
                dve.tensor_scalar(en[hi_, HH:J, lo_], c1[hi_, HH:J], -1.0, None, ALU.mult).then_inc(S("u12s"), 1)
                for g in range(14, 17):
                    gap(R, g)
                dve.wait_ge(S("o"), R + 1)
                for d in range(2):
                    c = chunk(d, r)
                    dst = oT[:, HH * half:HH * half + HH, c * P:(c + 1) * P]
                    src = pA[:, d * HH:d * HH + HH]
                    if r < NC // 2:
                        ins = dve.tensor_copy(dst, src)
                    else:
                        if d == 0:
                            dve.wait_ge(S("o_acc"), R)
                        ins = dve.tensor_tensor(dst, dst, src, ALU.add)
                ins.then_inc(S("o_acc"), 1)
                if r < NC - 1:
                    dve.wait_ge(S("s"), (NC - 1) * half + r + 1)
                    if r == 0:
                        for d in range(2):
                            ins = dve.tensor_copy(st[:, d * HH:d * HH + HH], pC[:, d * HH:d * HH + HH])
                    else:
                        for j in range(J):
                            ins = dve.scalar_tensor_tensor(st[:, j], st[:, j], scal(5, j), pC[:, j],
                                                           ALU.mult, ALU.add)
                    ins.then_inc(S("s_upd"), 1)
                gap(R, 17)

            qkv(0)
            for R in range(4):
                delta(R)
            assert done_taps[0] == len(TAPS)
            qkv(1)
            ev_wait(dve, ("mean",))
            for t in range(KT):
                dve.tensor_tensor(cslot(t), csum_in(t), acc[:], ALU.subtract).then_inc(S("xc"), 1)
            delta(4)
            ev_wait(dve, ("var",))
            dve.reciprocal(rstd[:], acc[:]).then_inc(S("rv"), 1)
            dve.wait_ge(S("rv"), 1)
            for t in range(KT):
                dve.tensor_tensor(cslot(t), cslot(t), rstd[:], ALU.mult).then_inc(S("xn"), 1)
            delta(5)
            for t in range(KT):
                low("conv", t, cslot(t))
            delta(6)
            delta(7)
            dve.wait_ge(S("on_root"), 1)
            dve.reciprocal(ost[:], ost[:]).then_inc(S("on_r"), 1)
            for h in range(H):
                aux_out(dve, ("on", h))
                dve.scalar_tensor_tensor(oT[:, h], oT[:, h], gate_p[:, 32:33], bank(("on", h)), ALU.mult, ALU.mult)\
                    .then_inc(S("evD"), 1)
                ev_wait(dve, ("on", h))
                dve.wait_ge(S(f"side{h % 2}"), 16 * (4 + h // 2 + 1))
                dve.tensor_tensor(oT[:, h], oT[:, h], tmps[h % 2][:], ALU.mult).then_inc(S("on_z"), 1)
                if h >= 2:
                    low("o", h - 2, oT[:, h - 2])
            low("o", H - 2, oT[:, H - 2])
            low("o", H - 1, oT[:, H - 1])
            for t in range(KT):
                after(("do", t))
                unit_out(dve, ("do", t))
                dve.wait_ge(S(f"sgb{t % 2}"), 16 * (t // 2 + 1))
                dve.tensor_tensor(gst[:, t % 2], bank(("do", t)), gst[:, t % 2], ALU.mult).then_inc(S("evD"), 1)
                ev_wait(dve, ("do", t))
                dve.tensor_tensor(ya[:, t], ya[:, t], gst[:, t % 2], ALU.add).then_inc(S("yv"), 1)
                dve.wait_ge(S("yb_hi"), t + 1)
                dve.tensor_tensor(yb_lo[:, t], ya[:, t], yb_hi[:, t].bitcast(F32), ALU.subtract)\
                    .then_inc(S("yb_lo"), 1)
            for t in range(KT):
                after(("wo", t))
                unit_out(dve, ("wo", t))
                dve.wait_ge(S(f"side{t % 2}"), 16 * (8 + t // 2 + 1))
                dve.tensor_tensor(x[:, t], bank(("wo", t)), tmps[t % 2][:], ALU.add).then_inc(S("evD"), 1)
                low("ffn0", t, x[:, t], v("g_ffn", t))

            def ffn(f, nu, g):
                def step(i):
                    for q in range(2):
                        n = U.at[("fg" + f, q)]
                        du = O.at[("fu" + f, q)]
                        last = isinstance(i, int)
                        if last and i == 0 and q == 0:
                            lo(n + 2)
                            recip(nu)
                            pass
                        dve.wait_ge(S("gemm"), n + 1 + 4 * i)
                        if not (last and i == 0 and q == 0):
                            dve.wait_ge(S("h_hi"), FT * int(f) + q + 2 * i)
                        bg, bu = (pg[:, O.at[(k + f, 2 * i + q if last else 2 + q)] % 2, :] for k in ("fg", "fu"))
                        dve.tensor_tensor(tmp1[:], bg, rstd[:], ALU.mult).then_inc(S("evD"), 1)
                        if not (last and i == 0 and q == 0):
                            lo(n + 2, i, U.cols[n + 2 + (4 * i if last else 0)])
                        dve.wait_ge(S("gemm"), n + 2 + 4 * i)
                        wait(dve, "h_lo", FT * int(f) + q + 2 * i)
                        dve.tensor_tensor(tmp2[:], bu, rstd[:], ALU.mult).then_inc(S("evD"), 1)
                        lo(n + 3, i, U.cols[n + 3 + (4 * i if last else 0)])
                        dve.wait_ge(S("sil"), FT * int(f) + q + 1 + 2 * i)
                        dve.wait_ge(S("evD"), O.count(du) + 4 * i)
                        dve.tensor_tensor(tmp2[:], tmp2[:], tmp1[:], ALU.mult).then_inc(S("hm"), 1)
                        dve.wait_ge(S("h_hi"), FT * int(f) + q + 1 + 2 * i)
                        m = 2 * i + q
                        at_m = (lambda b: b[:, m]) if last else \
                            (lambda b: b[:, bass.ds(m, 1)].rearrange("p a n -> p (a n)"))
                        dve.tensor_tensor(at_m(h_lo), tmp2[:], at_m(h_hi).bitcast(F32), ALU.subtract)\
                            .then_inc(S("h_lo"), 1)

                step(0)
                with dve.Fori(1, FT // 2 - 1) as i:
                    step(i)
                step(FT // 2 - 1)
                if f == "0":
                    rope_angles()
                for m in range(KT):
                    after(("fd" + f, 2 * m))
                    after(("fd" + f, 2 * m + 1))
                    if f != "0":
                        continue
                    unit_out(dve, ("fd" + f, 2 * m + 1))
                    dve.tensor_tensor(x[:, m], bank(("fd" + f, m)), x[:, m], ALU.add).then_inc(S("evD"), 1)
                    low("pg", m, x[:, m], v(g, m))

            def rope_angles():
                def step(k, ins):
                    ins.then_inc(S("ra"), 1)
                    dve.wait_ge(S("ra"), k)

                whole = 12582912.0
                c_a, c_b = 6.28125, 0.00193500518798828125
                c_c = float(np.float64(2 * np.pi) - c_a - c_b)
                dve.wait_ge(S("in_r"), 16)
                step(1, dve.tensor_scalar(rcos[:], rpos[:], gate_p[:, 37:38], None, ALU.mult))
                step(2, dve.tensor_scalar(rsin[:], rcos[:], float(1 / (2 * np.pi)), whole, ALU.mult, ALU.add))
                step(3, dve.tensor_scalar(rsin[:], rsin[:], -whole, None, ALU.add))
                for q, c_ in enumerate((c_a, c_b, c_c)):
                    step(4 + q, dve.scalar_tensor_tensor(rcos[:], rsin[:], -c_, rcos[:], ALU.mult, ALU.add))
                step(7, dve.tensor_scalar(rcos[:], rcos[:], 3.1415925, -3.1415925, ALU.min, ALU.max))
                dve.scalar_tensor_tensor(rpos[:].bitcast(F32), rcos[:], -1.0, rcos[:], ALU.mult, ALU.max)\
                    .then_inc(S("rope"), 1)

            ffn("0", 2, "g_pl")
            for t in range(KT):
                after(("pg", t))
                if t == 0:
                    recip(3)
                    dve.wait_ge(S("in_pl"), 16)
                unit_out(dve, ("pg", t))
                dve.tensor_tensor(tmps[t % 2][:], bank(("pg", t)), rstd[:], ALU.mult).then_inc(S("evD"), 1)
                dve.wait_ge(S("pgs"), t + 1)
                dve.tensor_tensor(tmps[t % 2][:], tmps[t % 2][:], pl[:, t], ALU.mult).then_inc(S("pgm"), 1)
                dve.wait_ge(S("pgm"), t + 1)
                dve.tensor_tensor(x[:, t], x[:, t], tmps[t % 2][:], ALU.add).then_inc(S("x2"), 1)
            recip(4)
            for t in range(KT):
                dve.scalar_tensor_tensor(x[:, t], x[:, t], v("g_final", t), rstd[:], ALU.mult, ALU.mult)\
                    .then_inc(S("xf"), 1)
            for t in range(KT):
                low("ffn1", t, x[:, t], v("ffn1_pre", t))
            ffn("1", 5, None)

            def post(nu, k, src, g, half_, s, g2):
                recip(nu)
                for t in range(KT + 1):
                    if t < KT:
                        q = KT * k + t
                        wait(dve, "xu", q - 1)
                        dve.scalar_tensor_tensor(tmps[t % 2][:], src[:, t], v(g, t), rstd[:], ALU.mult, ALU.mult)\
                            .then_inc(S("xt"), 1)
                        dve.wait_ge(S("xt"), q + 1)
                        dve.scalar_tensor_tensor(x[:, t], tmps[t % 2][:], half_, x[:, t], ALU.mult, ALU.add)\
                            .then_inc(S("xu"), 1)
                    if t and s:
                        low(s, t - 1, x[:, t - 1], v(g2, t - 1))

            post(6, 0, hb, "ffn1_post", 0.5, "mix", "mix_pre")
            dve.memset(up[:, :, 0:PW], 0.0)
            dve.memset(kz[0:HD2, 1], 0.0)
            dve.memset(kz[HD2:P, 0], 0.0)
            dve.memset(win[:, :, 0:PW], 0.0).then_inc(S("uzero"), 1)
            dve.tensor_scalar(nsink[:], gate_p[:, 38:46].rearrange("p (h i) -> p i h", h=2), -1.0, None, ALU.mult)\
                .then_inc(S("nsink"), 1)
            dve.wait_ge(S("nsink"), 1)

            def rotated(i):
                dve.wait_ge(S("rsin"), 2)
                aux_out(dve, ("rp", i))
                wait(dve, "qk2", i)
                dve.tensor_tensor(rt[:, 0], zq[:, i], rcos[:], ALU.mult).then_inc(S("rt"), 1)
                dve.tensor_tensor(rt[:, 1], bank(("rp", i)), rsin[:], ALU.mult).then_inc(S("evD"), 1)
                ev_wait(dve, ("rp", i))
                if i:
                    dve.tensor_tensor(qk2[:, i - 1], rt[:, 0], rt[:, 1], ALU.add).then_inc(S("qk2"), 1)
                else:
                    for h, p_ in enumerate((slice(0, HD2), slice(HD2, P))):
                        ins = dve.tensor_tensor(kz[p_, h], rt[p_, 0], rt[p_, 1], ALU.add)
                    ins.then_inc(S("qk2"), 1)

            def evac(key, dst):
                unit_out(dve, key)
                dve.tensor_tensor(dst, bank(key), rstd[:], ALU.mult).then_inc(S("evD"), 1)

            def mixed(key):
                after(key)
                if key == ("mk", 0):
                    recip(7)
                name, i = key
                dst = {"mk": zq[:, 0], "mv": zv[:], "mq": zq[:, 1 + i] if name == "mq" else None,
                       "mu": up[:, i, PW:] if name == "mu" else None}[name]
                evac(key, dst)

            for key in MIX[:3]:
                mixed(key)
            rotated(0)
            mixed(("mq", 1))
            rotated(1)
            mixed(("mq", 2))
            rotated(2)

            def bias(s):
                i, n = divmod(s, NB)
                k0 = P if n == 0 else 0
                dve.wait_ge(S("scores"), s + 1)
                wait(dve, "turn", s - 2)
                y = sm[:, s % 3, :, k0:]
                mask = band[:, k0:].unsqueeze(1).to_broadcast([P, 2, 2 * P - k0])
                dve.tensor_tensor(y, pa2[:, s % 2, :, k0:], mask, ALU.add).then_inc(S("smask"), 1)
                dve.wait_ge(S("smask"), s + 1)
                dve.tensor_reduce(out=sml[:, 0, s], in_=y, axis=mybir.AxisListType.X, op=ALU.max)\
                    .then_inc(S("smax"), 1)
                dve.wait_ge(S("smax"), s + 1)
                dve.scalar_tensor_tensor(sml[:, 1, s], sml[:, 0, s], -HD2 ** -0.5, nsink[:, i], ALU.mult, ALU.min)\
                    .then_inc(S("sneg"), 1)
                dve.wait_ge(S("sneg"), s + 1)
                dve.tensor_tensor(sml[:, 3, s], sml[:, 1, s], nsink[:, i], ALU.subtract).then_inc(S("bias"), 1)

            def normed(s):
                k0 = P if s % NB == 0 else 0
                dve.wait_ge(S("exp"), s + 1)
                dve.tensor_tensor(sml[:, 4, s], sml[:, 2, s], sml[:, 3, s], ALU.add).then_inc(S("den"), 1)
                dve.wait_ge(S("den"), 2 * s + 1)
                dve.reciprocal(sml[:, 4, s], sml[:, 4, s]).then_inc(S("den"), 1)
                dve.wait_ge(S("den"), 2 * s + 2)
                for h in range(2):
                    y = sm[:, s % 3, h, k0:]
                    ins = dve.tensor_scalar(y, y, sml[:, 4, s, h:h + 1], None, ALU.mult)
                ins.then_inc(S("prob"), 1)

            def means(g):
                w, u = win[:, g % 2, PW:], up[:, g, PW:]
                dve.wait_ge(S("win"), PT_ - g)
                dve.scalar_tensor_tensor(wd[:, g], w, 1.0 / POOL_W[g], u, ALU.mult, ALU.subtract)\
                    .then_inc(S("wdm"), 1)
                dve.tensor_tensor(tmp1[:, 0:16], w[:, 0:16], edge[:, g], ALU.mult).then_inc(S("wdm"), 1)
                dve.wait_ge(S("wdm"), 2 * (PT_ - g))
                dve.tensor_tensor(wd[:, g, 0:16], tmp1[:, 0:16], u[:, 0:16], ALU.subtract).then_inc(S("wd"), 1)
                dve.wait_ge(S("wd"), PT_ - g)

            MEANS = {7: 3, 10: 2, 13: 1, 16: 0}
            for s in range(16 + 3):
                if s < 16:
                    bias(s)
                if 0 <= s - 1 < 16:
                    normed(s - 1)
                if s < 15 and s % 3 == 2:
                    mixed(MFILL[s // 3])
                for k in MAUX.get(s, []):
                    if k[0] == "rp":
                        rotated(k[1])
                if s in MEANS:
                    means(MEANS[s])
                if s >= 3 and (s - 3) % NB == NB - 1:
                    i = (s - 3) // NB
                    dve.wait_ge(S("values"), s - 2)
                    dve.tensor_copy(mo[:, PT_ + i], pc2[:, i % 2]).then_inc(S("oat"), 1)
            for nu, t0, at_ in ((8, 0, 50), (9, PT_, 54)):
                recip(nu)
                for t in range(t0, t0 + PT_):
                    g = at_ + t - t0
                    dve.scalar_tensor_tensor(mo[:, t], mo[:, t], gate_p[:, g:g + 1], rstd[:], ALU.mult, ALU.mult)\
                        .then_inc(S("mh"), 1)
                for t in range(t0, t0 + PT_):
                    low("out", t, mo[:, t])
            for t in range(KT):
                after(("mo", t))
            post(10, 1, hb2, "mix_post", 1.0, "ffn2", "ffn2_pre")
            ffn("2", 11, None)
            post(12, 2, hb, "ffn2_post", 0.5, None, None)

        @block.gpsimd
        def _(pool):
            def adds(nu):
                for t in range(1, NORMS[nu] - 1):
                    pool.wait_ge(S("sq"), SQ[nu] + t + 1)
                    wait(pool, "add", AD[nu] + t - 1)
                    pool.tensor_tensor(acc[:], acc[:], sq[:, t % 2, :], ALU.add).then_inc(S("add"), 1)

            def delta(R):
                half, r = divmod(R, NC)

                def toks(k, d):
                    q = d * 8 + HH * half
                    return gat[:, k, chunk(d, r), q:q + HH].unsqueeze(2).to_broadcast([P, HH, P])

                def level(lv):
                    pool.wait_ge(S("lc"), R + 1)
                    wait(pool, "y", LEVELS * R + lv - 1)
                    if lv == 2:
                        pool.wait_ge(S("u_upd"), LEVELS * R + 1)
                    q = C_LVL + lv * 2 * W64
                    mask = quad(consts[:, q:q + 2 * W64], 2).unsqueeze(2).to_broadcast([P, 2, HH, W64])
                    pool.tensor_tensor(ls[:, lv % 2].rearrange("p (d h) c -> p d h c", d=2),
                                       lc[:].rearrange("p (d h) c -> p d h c", d=2), mask, ALU.mult)\
                        .then_inc(S("ls"), 1)

                level(0)
                level(1)
                pool.wait_ge(S("et"), R + 1)
                for d in range(2):
                    s = slice(d * HH, d * HH + HH)
                    ins = pool.tensor_tensor(et[:, s], et[:, s], tri[d].unsqueeze(1).to_broadcast([P, HH, P]), ALU.mult)
                ins.then_inc(S("etm"), 1)
                pool.wait_ge(S("eg"), R + 1)
                for d in range(2):
                    s, c = slice(d * HH, d * HH + HH), chunk(d, r)
                    ins = pool.tensor_tensor(qd[:, s], qd[:, s], qT[:, :, c * P:(c + 1) * P], ALU.mult)
                ins.then_inc(S("qdm"), 1)
                pool.wait_ge(S("g_k"), 1)
                wait(pool, "s", (NC - 1) * half + r)
                wait(pool, "vn", R)
                level(2)
                for dst, src, k, name, lv in ((kb, ktok, 3, "kb", 3), (bv, vtok, 1, "bv", 4), (kt, ktok, 4, "kt", 5)):
                    if name != "kb":
                        wait(pool, "o", R)
                    for d in range(2):
                        ins = pool.tensor_tensor(dst[:, d * HH:d * HH + HH], src[:, :, chunk(d, r), :], toks(k, d),
                                                 ALU.mult)
                    ins.then_inc(S(name), 1)
                    level(lv)

            pool.wait_ge(S("in_c"), 16)
            adds(0)
            adds(1)
            pool.wait_ge(S("plf"), KT)
            ev_wait(pool, ("gla", KT - 1))
            t = KT - 1
            for j in range(CK):
                src, w = cpad[:, t, j:j + T], vec[:, t, len(VEC) + j:len(VEC) + j + 1]
                if j == 0:
                    pool.tensor_scalar(csum_in(t), src, w, v("conv_b", t), ALU.mult, ALU.add).then_inc(S("ptap"), 1)
                else:
                    b = (acc, rstd)[j % 2]
                    wait(pool, "ptap", j - 2)
                    pool.tensor_scalar(b[:], src, w, None, ALU.mult).then_inc(S("pprod"), 1)
                    pool.wait_ge(S("pprod"), j)
                    pool.wait_ge(S("ptap"), j)
                    pool.tensor_tensor(csum_in(t), csum_in(t), b[:], ALU.add).then_inc(S("ptap"), 1)
            for R in range(4):
                if R == 0:
                    pool.wait_ge(S("g_all"), 1)
                    pool.wait_ge(S("trc"), 2 * HH)
                delta(R)
            pool.wait_ge(S("tap"), len(TAPS))
            pool.wait_ge(S("ptap"), CK)
            for t in range(1, KT):
                wait(pool, "csum", t - 1)
                pool.tensor_tensor(acc[:], cslot(0) if t == 1 else acc[:], csum_in(t), ALU.add)\
                    .then_inc(S("csum"), 1)
            for t in range(1, KT):
                pool.wait_ge(S("cvs"), t + 1)
                wait(pool, "cva", t - 1)
                pool.tensor_tensor(rstd[:], rstd[:], sq[:, t % 2, :], ALU.add).then_inc(S("cva"), 1)
            for R in range(4, 8):
                delta(R)
            for nu in range(2, 8):
                adds(nu)
            pool.wait_ge(S("uzero"), 1)
            for g in reversed(range(PT_)):
                ev_wait(pool, ("mu", g))
                wait(pool, "wd", PT_ - 1 - g)
                for q in range(g + 1):
                    src = up[:, g] if q == 0 else win[:, (q - 1) % 2]
                    ins = pool.tensor_tensor(win[:, q % 2, PW:], src[:, PW:], src[:, PW - (1 << q):PW + T - (1 << q)],
                                             ALU.add)
                    if q < g:
                        n_add = sum(range(g + 1, PT_)) + q + 1
                        ins.then_inc(S("wadd"), 1)
                        pool.wait_ge(S("wadd"), n_add)
                ins.then_inc(S("win"), 1)
            for nu in range(8, 13):
                adds(nu)

    return


def kernel(**inputs):
    import concourse.bacc as bacc
    from concourse.bass_utils import run_bass_kernel_spmd

    def tiles(w):
        k, n = w.shape
        return np.ascontiguousarray(w.reshape(k // P, P, n // P, P).transpose(2, 1, 0, 3).reshape(n // P, P, k))

    def cols(w):
        return np.ascontiguousarray(w.T.reshape(w.shape[1] // P, P, w.shape[0]).transpose(1, 0, 2))

    f = {k: np.asarray(w) for k, w in inputs.items()}
    w_in = f["w_in"][0]
    pre = 2 * D + 4 * D
    arrays = {
        "x": cols(f["x"][0]),
        "p": cols(f["p"][0, 0]),
        "consts": constant_table(),
        "w_in": tiles(np.concatenate([w_in[:, :pre], w_in[:, pre + 32:]], 1)),
        "w_ab": np.ascontiguousarray(w_in[:, pre:pre + 32].reshape(KT, P, 32).transpose(1, 0, 2).reshape(P, KT * 32)),
        "w_plp": np.ascontiguousarray(
            tiles(f["w_pl_proj"][0]).reshape(4, 2, P, 2 * P).transpose(0, 2, 1, 3).reshape(4, P, 4 * P)),
        "w_co": tiles(f["w_conv_out"][0]),
        "w_do": tiles(f["w_delta_out"][0]),
        "w_wo": tiles(f["w_o"][0]),
        "w_gu0": tiles(f["w_gate_up"][0]),
        "w_dn0": np.ascontiguousarray(
            f["w_down"][0].reshape(2, KH, P, KT, P).transpose(3, 0, 2, 1, 4).reshape(KT, 2, P, KH * P)),
        "w_pg": tiles(f["w_pl_gate"][0]),
    }

    def down(w):
        return np.ascontiguousarray(w.reshape(2, KH, P, KT, P).transpose(3, 0, 2, 1, 4).reshape(KT, 2, P, KH * P))

    pairs = np.concatenate([np.arange(HD2) + HD2 * h for i in range(4) for h in (i, i + 4)])
    w2, half = f["w_in_2"][0], D // 2
    arrays.update({
        "w_gu1": tiles(f["ffn1_w_gu_2"][0]), "w_dn1": down(f["ffn1_w_down_2"][0]),
        "w_gu2": tiles(f["ffn2_w_gu_2"][0]), "w_dn2": down(f["ffn2_w_down_2"][0]),
        "w_in2": tiles(np.concatenate([w2[:, :half], w2[:, half + pairs], w2[:, D:]], 1)),
        "w_out2": tiles(np.concatenate([f["w_out_2"][0][:half], f["w_out_2"][0][half + pairs]], 0)),
        "pos": np.ascontiguousarray(np.broadcast_to(f["positions_2"].reshape(1, T), (P, T))),
        "c2": np.concatenate([mixer_table(), f["w_pool_2"][0].transpose(1, 0, 2).reshape(P, PT_ * P)], 1),
    })
    names = ["g_mix", "conv_dw_b", "conv_ln_g", "conv_ln_b", "g_ffn", "g_pl", "g_pl_proj", "g_final",
             "ffn1_pre_2", "ffn1_post_2", "mix_pre_2", "mix_post_2", "ffn2_pre_2", "ffn2_post_2"]
    rows = np.concatenate([f[n].reshape(1, D) for n in names] + [f["conv_dw_w"][0]], 0)
    arrays["vec"] = np.ascontiguousarray(rows.T.reshape(KT, P, NV).transpose(1, 0, 2))
    arrays["swt"] = np.ascontiguousarray(f["qkv_conv_w"][0].T.reshape(3 * H, P, SK).transpose(1, 0, 2))
    small = np.concatenate([f["a_log"].reshape(-1), f["dt_bias"].reshape(-1)])
    eps = np.array([EPS, P * EPS, EPS, LN_EPS], np.float32)
    dim = np.arange(P) % HD2
    freq = np.float32(THETA) ** (-np.arange(0, ROT, 2, dtype=np.float32) / np.float32(ROT))
    freq = np.where(dim < ROT, freq[dim % (ROT // 2)], 0).astype(np.float32).reshape(P, 1)
    arrays["gate_p"] = np.concatenate(
        [np.broadcast_to(small, (P, 32)), f["delta_norm_g"].reshape(P, 1), np.broadcast_to(eps, (P, 4)), freq,
         np.broadcast_to(f["sinks_2"].reshape(1, 8), (P, 8)), f["pool_scale_2"].reshape(PT_, P).T,
         f["g_pool_2"].reshape(PT_, P).T, f["g_attn_2"].reshape(-1)[pairs].reshape(PT_, P).T,
         np.full((P, 1), np.pi / 2, np.float32)], 1)
    nc = bacc.Bacc("TRN2", target_bir_lowering=False, num_devices=1)
    a = {n: nc.dram_tensor("in_" + n, w.shape, mybir.dt.from_np(w.dtype), kind="ExternalInput").ap()
         for n, w in arrays.items()}
    out = nc.dram_tensor("out", (KT, P, T), F32, kind="ExternalOutput").ap()
    build(nc, a, out)
    r = run_bass_kernel_spmd(nc, [{"in_" + n: w for n, w in arrays.items()}], core_ids=[0])
    y = np.asarray(r.results[0]["out"])
    return np.ascontiguousarray(y.transpose(2, 0, 1).reshape(1, T, D))
```

```python
import numpy as np
import concourse.bass as bass
from concourse import mybir
from contextlib import ExitStack

F32 = mybir.dt.float32
F32R = mybir.dt.float32r
ALU = mybir.AluOpType
ACT = mybir.ActivationFunctionType

P = 128
T = 512
D = 1024
KT = D // P
FT = 2816 // P
KH = FT // 2
H = 8
HH = 4
NC = T // P
CK = 31
CP = CK // 2
SK = 5
SP_ = SK // 2
W64 = 64
LEVELS = 6
PT_ = 4
HD2 = 64
NB = T // P
ROT = HD2 // 4
THETA = 500000.0
POOL_W = (2, 4, 8, 16)
NEG = -1e30
EPS = 1e-6
LN_EPS = 1e-5

VEC = ["g_mix", "conv_b", "ln_g", "ln_b", "g_ffn", "g_pl", "g_plp", "g_final",
       "ffn1_pre", "ffn1_post", "mix_pre", "mix_post", "ffn2_pre", "ffn2_post"]
NV = len(VEC) + CK

C_ID, C_ONE, C_TRI, C_LVL, C_I64 = 0, P, 2 * P, 4 * P, 4 * P + 2 * LEVELS * W64
C_END = C_I64 + W64


def constant_table():
    c = np.zeros((P, C_END), np.float32)
    r = np.arange(P)
    c[:, C_ID:C_ID + P] = np.eye(P)
    c[:, C_ONE:C_ONE + P] = 1.0
    c[:, C_TRI:C_TRI + P] = r[:, None] <= r[None, :]
    c[:, C_TRI + P:C_TRI + 2 * P] = r[:, None] >= r[None, :]
    row, col = r[:, None] % W64, np.arange(W64)[None, :]
    for lv in range(LEVELS):
        s = 1 << lv
        same = row // (2 * s) == col // (2 * s)
        low = same & (row // s % 2 == 1) & (col // s % 2 == 0)
        up = same & (row // s % 2 == 0) & (col // s % 2 == 1)
        at = C_LVL + lv * 2 * W64
        c[:, at:at + W64] = low
        c[:, at + W64:at + 2 * W64] = up
    c[:, C_I64:C_I64 + W64] = row == col
    return c


def mixer_table():
    perm = np.zeros((P, P), np.float32)
    for h in range(0, P, HD2):
        for d in range(ROT // 2):
            perm[h + d + ROT // 2, h + d] = -1.0
            perm[h + d, h + d + ROT // 2] = 1.0
    q, k = np.arange(P)[:, None], np.arange(2 * P)[None, :]
    band = np.where((k > q) & (k <= q + P), 0.0, NEG)
    t = np.arange(16)
    edge = np.concatenate([1.0 / np.minimum(t + 1, w) for w in POOL_W])
    return np.concatenate([perm, band, np.broadcast_to(edge, (P, 64))], 1).astype(np.float32)


class Units:

    def __init__(self):
        self.src, self.cols, self.at = [], [], {}

    def add(self, name, src, cols):
        self.at[name] = len(self.src)
        self.src.append(src)
        self.cols.append(cols)


class Outs:

    def __init__(self):
        self.reader, self.at = [], {}

    def add(self, name, reader):
        self.at[name] = len(self.reader)
        self.reader.append(reader)

    def count(self, o):
        return self.reader[:o + 1].count(self.reader[o])


def build(nc, a, out):
    ctx = ExitStack()
    with ctx:
        sems = {}

        def S(name):
            if name not in sems:
                sems[name] = ctx.enter_context(nc.semaphore(name))
            return sems[name]

        ALL = 212832
        base = [nc.sbuf_base + (-nc.sbuf_base) % 32]
        first = base[0]

        def at(name, cols, dtype=F32, offset=None, shape=None):
            if offset is None:
                offset = base[0]
                base[0] += cols * 4 + (-cols * 4) % 32
            assert offset + cols * 4 <= first + ALL, (name, offset + cols * 4 - first - ALL)
            return nc.alloc_sbuf_tensor_at(name, shape or [P, cols], dtype, offset=offset)

        UC = KH * P
        w_raw = at("w_raw", 4 * UC, shape=[P, 4, UC])
        w_hi = at("w_hi", 2 * UC, F32R, shape=[P, 2, UC])
        w_lo = at("w_lo", 2 * UC, F32R, shape=[P, 2, UC])
        A_OFF = base[0]
        a_hi = at("a_hi", KT * T, F32R, shape=[P, KT, T])
        a_lo = at("a_lo", KT * T, F32R, shape=[P, KT, T])
        X_OFF = base[0]
        x = at("x", KT * T, shape=[P, KT, T])
        consts = at("consts", C_END)
        vec = at("vec", KT * NV, shape=[P, KT, NV])
        swt = at("swt", 3 * H * SK, shape=[P, 3 * H, SK])
        gate_p = at("gate_p", 59)
        eps_t = gate_p[:, 33:37]
        tmp1 = at("tmp1", T)
        tmp2 = at("tmp2", T)
        sq = at("sq", 2 * T, shape=[P, 2, T])
        acc = at("acc", T)
        rstd = at("rstd", T)
        nst = at("nst", 16, shape=[P, 2, 8])
        ost = at("ost", 8 * NC, shape=[P, 8 * NC])
        R_OFF = base[0]

        ident = consts[:, C_ID:C_ID + P]
        ones = consts[:, C_ONE:C_ONE + P]
        tri = [consts[:, C_TRI + d * P:C_TRI + (d + 1) * P] for d in range(2)]
        id64 = consts[:, C_I64:C_I64 + W64]

        def v(name, t):
            return vec[:, t, VEC.index(name):VEC.index(name) + 1]

        base[0] = R_OFF
        PAD = T + 2 * CP
        cpad = at("cpad", KT * PAD, shape=[P, KT, PAD])
        cacc = at("cacc", 2 * T, shape=[P, 2, T])
        qT = at("qT", HH * T, shape=[P, HH, T])
        kT = at("kT", HH * T, shape=[P, HH, T])
        ktok = at("ktok", HH * T, shape=[P, HH, NC, P])
        vtok = at("vtok", HH * T, shape=[P, HH, NC, P])
        oT = at("oT", KT * T, offset=X_OFF, shape=[P, KT, T])
        gat = at("gat", 6 * 64, shape=[P, 6, NC, 16])
        D_OFF = base[0]
        J = 2 * HH
        en = at("en", J * P, shape=[P, J, P])
        et = at("et", J * P, shape=[P, J, P])
        lc = at("lc", J * W64, shape=[P, J, W64])
        ls = at("ls", 2 * J * W64, shape=[P, 2, J, W64])
        tb = at("tb", J * W64, shape=[P, J, W64])
        ub = at("ub", J * W64, shape=[P, J, W64])
        yb = at("yb", J * W64, shape=[P, J, W64])
        kb = at("kb", J * P, shape=[P, J, P])
        bv = at("bv", J * P, shape=[P, J, P])
        kt = at("kt", J * P, shape=[P, J, P])
        st = at("st", J * P, shape=[P, J, P])
        qd = at("qd", J * P, shape=[P, J, P])
        xin = at("xin", KT * T, offset=D_OFF, shape=[P, KT, T])
        praw = at("praw", 2 * T, offset=D_OFF + 16384, shape=[P, 2, T])
        p_hi = at("p_hi", 2 * T, F32R, offset=D_OFF + 20480, shape=[P, 2, T])
        p_lo = at("p_lo", 2 * T, F32R, offset=D_OFF + 24576, shape=[P, 2, T])
        ptile = at("ptile", KT * T, offset=R_OFF + KT * PAD * 4 + 4096, shape=[P, KT, T])
        pad = at("pad", 3 * (T + 4), offset=D_OFF, shape=[P, 3, T + 4])
        sacc = at("sacc", 6 * T, offset=D_OFF + 8192, shape=[P, 2, 3, T])
        ya = at("ya", KT * T, offset=R_OFF, shape=[P, KT, T])
        yb_hi = at("yb_hi", KT * T, F32R, offset=D_OFF, shape=[P, KT, T])
        yb_lo = at("yb_lo", KT * T, F32R, offset=D_OFF + 16384, shape=[P, KT, T])
        gst = at("gst", 2 * T, offset=D_OFF + 32768, shape=[P, 2, T])
        base[0] = R_OFF
        h_hi = at("h_hi", FT * T, F32R, shape=[P, FT, T])
        h_lo = at("h_lo", FT * T, F32R, shape=[P, FT, T])
        pl = at("pl", KT * T, offset=R_OFF, shape=[P, KT, T])
        hb = at("hb", KT * T, offset=A_OFF, shape=[P, KT, T])

        rcos = at("rcos", T)
        rsin = at("rsin", T)
        rpos = at("rpos", T, mybir.dt.int32)
        base[0] = R_OFF
        PW = 16
        c2 = at("c2", P + 2 * P + 4 * 16 + PT_ * P)
        perm, band = c2[:, 0:P], c2[:, P:3 * P]
        edge = c2[:, 3 * P:3 * P + 64].rearrange("p (g t) -> p g t", g=4)
        wpool = c2[:, 3 * P + 64:].rearrange("p (g d) -> p g d", g=4)
        Q_OFF = base[0]
        zq = at("zq", 5 * T, shape=[P, 5, T])
        kz = at("kz", 2 * T, shape=[P, 2, T])
        qk2 = at("qk2", 4 * T, shape=[P, 4, T])
        rt = at("rt", 2 * T, shape=[P, 2, T])
        zv = at("zv", T)
        vt2 = at("vt2", T, shape=[P, NB, P])
        up = at("up", PT_ * (PW + T), shape=[P, PT_, PW + T])
        win = at("win", 2 * (PW + T), shape=[P, 2, PW + T])
        wd = at("wd", PT_ * T, shape=[P, PT_, T])
        mo = at("mo", KT * T, shape=[P, KT, T])
        sm = at("sm", 3 * T, shape=[P, 3, 2, 2 * P])
        ptb = at("ptb", 2 * T, shape=[P, 2, 2, 2, P])
        sml = at("sml", 5 * 32, shape=[P, 5, 16, 2])
        nsink = at("nsink", 8, shape=[P, 4, 2])
        hb2 = at("hb2", KT * T, offset=Q_OFF, shape=[P, KT, T])

        pg = ctx.enter_context(nc.psum_tensor("pg", [P, 2, T], F32))
        pA = ctx.enter_context(nc.psum_tensor("pA", [P, J, P], F32))
        pB = ctx.enter_context(nc.psum_tensor("pB", [P, J, P], F32))
        pC = ctx.enter_context(nc.psum_tensor("pC", [P, J, P], F32))
        c0 = pC[:, 0:HH, :].rearrange("p (j a) b -> p (j a b)", a=1).rearrange("p (j c) -> p j c", c=W64)
        ctr = pB[:, 0:HH, :].rearrange("p (j a) b -> p (j a b)", a=1).rearrange("p (j c) -> p j c", c=W64)
        l2b = pC[:, :, :].rearrange("p (b k) c -> p b (k c)", b=2)
        trb = pA[:, :, :].rearrange("p (b k) c -> p b (k c)", b=2)
        nb2 = pB[:, 0:HH, :].rearrange("p j c -> p (j c)")
        nb = pB[:, HH:J, :].rearrange("p j c -> p (j c)")
        c1 = pC[:, HH:J, :].rearrange("p (j a) b -> p (j a b)", a=1).rearrange("p (j c) -> p j c", c=W64)

        spill_g = nc.dram_tensor("spill_g", [16, P, T], F32, kind="Internal").ap()
        spill_z = nc.dram_tensor("spill_z", [H, P, T], F32, kind="Internal").ap()
        spill_p = nc.dram_tensor("spill_p", [KT, P, T], F32, kind="Internal").ap()

        U = Units()
        for i in range(4):
            U.add(("pl", i), a["w_plp"][i], 4 * P)
        for t in range(KT):
            U.add(("glb", t), a["w_in"][KT + t], KT * P)
            U.add(("gla", t), a["w_in"][t], KT * P)
        U.add(("ab",), a["w_ab"], KT * 32)

        def qkv_units(half):
            for h in range(HH * half, HH * half + HH):
                for i in range(3):
                    U.add(("qkv", 3 * h + i), a["w_in"][(2 + i) * KT + h], KT * P)

        qkv_units(0)
        for i in range(16):
            U.add(("gate", i), a["w_in"][6 * KT + i], KT * P)
        qkv_units(1)
        for i in range(8):
            U.add(("z", i), a["w_in"][5 * KT + i], KT * P)
        for nm in ("co", "do", "wo"):
            for i in range(KT):
                U.add((nm, i), a["w_" + nm][i], KT * P)

        def ffn_units(f):
            for m in range(FT):
                U.add(("fg" + f, m), a["w_gu" + f][m], KT * P)
                U.add(("fu" + f, m), a["w_gu" + f][FT + m], KT * P)
            for m in range(KT):
                for i in range(2):
                    U.add(("fd" + f, 2 * m + i), a["w_dn" + f][m, i], KH * P)

        MIX = [("mk", 0), ("mv", 0), ("mq", 0), ("mq", 1), ("mq", 2), ("mu", 3), ("mq", 3),
               ("mu", 2), ("mu", 1), ("mu", 0)]
        MFILL = MIX[5:]
        COL = {"mu": 0, "mq": 4, "mk": 8, "mv": 9}

        ffn_units("0")
        for i in range(KT):
            U.add(("pg", i), a["w_pg"][i], KT * P)
        ffn_units("1")
        for key in MIX:
            U.add(key, a["w_in2"][COL[key[0]] + key[1]], KT * P)
        for i in range(KT):
            U.add(("mo", i), a["w_out2"][i], KT * P)
        ffn_units("2")
        N_UNITS = len(U.src)

        O = Outs()
        AUX = {}

        def aux(key, reader):
            O.add(key, reader)
            AUX[key] = len(AUX)

        for t in range(KT):
            O.add(("pl", t), "A")
        for t in range(KT):
            O.add(("glb", t), "A")
            O.add(("gla", t), "D")
        O.add(("ab",), "D")

        def qkv_outs(half):
            for q in range(3 * HH):
                O.add(("qkv", 3 * HH * half + q), "A")
                if q == half == 0:
                    aux(("gc",), "A")
                if half and q == 6:
                    aux(("mean",), "A")
            if half:
                aux(("var",), "D")

        qkv_outs(0)
        for i in range(16):
            O.add(("gate", i), "A")
        qkv_outs(1)
        for i in range(8):
            O.add(("z", i), "A")
        for i in range(8):
            O.add(("co", i), "D")
        for i in range(8):
            O.add(("do", i), "D")
        for i in range(8):
            O.add(("wo", i), "D")

        def ffn_outs(f):
            for m in range(FT):
                O.add(("fg" + f, m), "D")
                O.add(("fu" + f, m), "D")
            for m in range(KT):
                O.add(("fd" + f, m), "D" if f == "0" else "A")

        ffn_outs("0")
        for i in range(KT):
            O.add(("pg", i), "D")
        ffn_outs("1")
        MAUX = {2: [("rp", 3)], 8: [("rp", 4), ("yp", 3)], 11: [("yp", 2)], 14: [("yp", 1)]}
        O.add(("mk", 0), "D")
        O.add(("mv", 0), "D")
        O.add(("mq", 0), "D")
        O.add(("mq", 1), "D")
        O.add(("mq", 2), "D")
        for i, key in enumerate(MFILL):
            O.add(key, "D")
            for k in MAUX.get(3 * i + 2, []):
                aux(k, "D" if k[0] == "rp" else "A")
        aux(("yp", 0), "A")
        for i in range(KT):
            O.add(("mo", i), "A")
        ffn_outs("2")

        NORMS = [KT] * 8 + [PT_] * 2 + [KT] * 3
        SQ = [sum(NORMS[:i]) for i in range(len(NORMS))]
        AD = [0] + [sum(n - 2 for n in NORMS[1:i]) for i in range(1, len(NORMS))]

        def added(nu):
            return "add" if nu else "add0"

        TAPS = [(1 + 2 * pr + i, j) for pr in range(KT // 2 - 1) for j in range(CK) for i in range(2)]
        taps_unit = 8
        A_, B_ = 4, 4
        GAP = [16, 13, 4] + [A_, B_] * (LEVELS - 1) + [4, 5, 7, 7, 0]
        TAP = [0, 3, 0] + [0, 2] * 2 + [0, 3] * 3 + [0, 3, 4, 5, 5]
        PD = 4
        NORM_AT = 14
        UNIT = 3 * KT
        assert sum(GAP) == 4 * UNIT and taps_unit * (KT - 2) + 3 * HH + 4 * sum(TAP) >= len(TAPS)

        def cslot(t):
            return cacc[:, t - 1, :] if t in (1, 2) else cpad[:, max(t - 2, 0), 0:T]

        def csum_in(t):
            return oT[:, KT - 2 + (t > 0)] if t in (0, KT - 1) else cslot(t)

        def wait(eng, name, value):
            if not isinstance(value, int) or value > 0:
                eng.wait_ge(S(name), value)

        def ev_wait(eng, key):
            o = O.at[key]
            eng.wait_ge(S("ev" + O.reader[o]), O.count(o))

        def unit_out(eng, key, n=None):
            eng.wait_ge(S("gemm"), (U.at[key] if n is None else n) + 1)

        def aux_out(eng, key):
            eng.wait_ge(S("aux"), AUX[key] + 1)

        def bank(key):
            return pg[:, O.at[key] % 2, :]

        def onb(h):
            return (trb, l2b)[h // 2 % 2][:, h % 2]

        def quad(ap, n=HH):
            return ap.rearrange("p (n c) -> p n c", n=n)

        pa2 = pA[:, :, :].rearrange("p (b h k) c -> p b h (k c)", b=2, h=2)
        pb2 = pB[:, :, :].rearrange("p (b h k) c -> p b h k c", b=2, h=2)
        pc2 = pC[:, :, :].rearrange("p (b k) c -> p b (k c)", b=2)

        rpb = (pc2[:, 1], nb2, pc2[:, 1])

        def chunk(d, r):
            return r if d == 0 else NC - 1 - r

        def filler(R):
            name, i = (("gate", 4 * R) if R < 4 else ("z", 4 * (R - 4)) if R < 6 else ("co", 4 * (R - 6)))
            return [(name, i + f) for f in range(4)]

        def parts(R, g):
            q, end = sum(GAP[:g]), sum(GAP[:g + 1])
            while q < end:
                f = q // UNIT
                e = min(end, (f + 1) * UNIT)
                yield filler(R)[f], q - f * UNIT, e - f * UNIT
                q = e

        def filled(R, g):
            return [key for key, q, e in parts(R, g) if e == UNIT]

        tmps = (tmp1, tmp2)
        osq = (sq[:, 0, :], sq[:, 1, :], acc[:], rstd[:])
        SETS = ["h", "conv", "o", "ffn0", "pg", "ffn1", "mix", "out", "ffn2"]

        def set_count(s, t):
            return SETS.index(s) * KT + t + 1

        block = ctx.enter_context(nc.Block())

        @block.sync
        def _(sp):
            def load(n, src=None, i=0):
                if not (isinstance(i, int) and n < 4):
                    sp.wait_ge(S("w_lo"), n - 3 + 4 * i)
                sp.dma_start(w_raw[:, n % 4, 0:U.cols[n]], U.src[n] if src is None else src)\
                    .then_inc(S(f"w_in{n % 4}"), 16)

            def side(t, src, ready):
                sp.wait_ge(S(ready[0]), ready[1])
                sp.dma_start(tmps[t % 2][:], src).then_inc(S(f"side{t % 2}"), 16)

            def ev(key):
                return ("ev" + O.reader[O.at[key]], O.count(O.at[key]))

            sp.dma_start(praw[:], a["p"]).then_inc(S("in_p"), 16)
            load(0)
            for t in range(KT // 2):
                q = slice(2 * t, 2 * t + 2)
                sp.dma_start(xin[:, q], a["x"][:, q]).then_inc(S(f"in_x{t}"), 16)
            sp.dma_start(consts[:], a["consts"]).then_inc(S("in_c"), 16)
            sp.dma_start(vec[:], a["vec"]).then_inc(S("in_v"), 16)
            load(1)
            sp.dma_start(swt[:], a["swt"]).then_inc(S("in_s"), 16)
            sp.dma_start(gate_p[:], a["gate_p"]).then_inc(S("in_g"), 16)
            for n in range(2, U.at[("fg0", 0)] + 4):
                for t in range(KT):
                    if n == U.at[("co", max(t - 1, 0))] + 4:
                        if t < 2:
                            sp.wait_ge(S(f"spill{t}"), 16 * 10)
                        side(t, spill_g[t], ("spill1", 16 * 10) if t < 2 else ev(("co", t - 2)))
                    if n == U.at[("do", 0)] + 4 and t >= HH:
                        side(t, spill_z[t], ev(("co", 2 + t)) if t < 6 else ("on_z", t - 1))
                    if n == U.at[("do", max(t - 1, 0))] + 4:
                        if t < 2:
                            sp.wait_ge(S("s_upd"), 6)
                            sp.wait_ge(S("o_acc"), 8)
                        else:
                            sp.wait_ge(S("yv"), t - 1)
                        sp.dma_start(gst[:, t % 2], spill_g[KT + t]).then_inc(S(f"sgb{t % 2}"), 16)
                    if n == U.at[("wo", max(t - 1, 0))] + 4:
                        side(t, a["x"][:, t], ("on_z", 7 + t) if t < 2 else ev(("wo", t - 2)))
                load(n)
                if n == U.at[("ab",)]:
                    sp.wait_ge(S("plf"), KT)
                    sp.dma_start(spill_p.rearrange("t p n -> p t n"), ptile[:]).then_inc(S("spp"), 16)

            def ffn(f, more):
                g0 = U.at[("fg" + f, 0)]
                with sp.Fori(1, FT // 2) as i:
                    for j in range(4):
                        at_ = bass.ds(2 * i + (j // 2 + (j % 2) * FT), 1)
                        load(g0 + j, a["w_gu" + f][at_].rearrange("a p c -> (a p) c"), i)
                for n in range(U.at[("fd" + f, 0)], more):
                    if n == U.at[("pg", 0)] + 2:
                        unit_out(sp, ("fd0", 2 * KT - 1))
                        sp.dma_start(pl[:], spill_p.rearrange("t p n -> p t n")).then_inc(S("in_pl"), 16)
                    if n == U.at[("mk", 0)] + 3:
                        unit_out(sp, ("fd1", 2 * KT - 1))
                        sp.dma_start(c2[:], a["c2"]).then_inc(S("in_c2"), 16)
                    load(n)

            sp.dma_start(rpos[:], a["pos"]).then_inc(S("in_r"), 16)
            ffn("0", U.at[("fg1", 0)] + 4)
            ffn("1", U.at[("fg2", 0)] + 4)
            ffn("2", N_UNITS)
            for t in range(KT):
                sp.wait_ge(S("xu"), 2 * KT + t + 1)
                sp.dma_start(out[t], x[:, t]).then_inc(S("out"), 16)
            sp.wait_ge(S("out"), 16 * KT)

        @block.tensor
        def _(pe):
            def begin(key):
                o = O.at[key]
                if o >= 2:
                    q = o - 2
                    pe.wait_ge(S("ev" + O.reader[q]), O.count(q))
                return pg[:, o % 2, :]

            def products(n, act, k_n, dst, w_of, part=None, first=True, last=True, ready=None):
                hi, lo = act
                todo = [(k, w, b) for k in range(k_n) for w, b in ((w_hi, hi), (w_hi, lo), (w_lo, hi))]
                for q in range(*(part or (0, len(todo)))):
                    k, w, b = todo[q]
                    if ready and q % 3 == 0:
                        pe.wait_ge(S(ready[0]), ready[1] + k)
                    ins = pe.matmul(dst, w_of(w, n % 2, k), b(k), start=first and q == 0,
                                    stop=last and q == len(todo) - 1)
                return ins

            def fresh(s):
                return ("a_lo", set_count(s, 0))

            def w_tile(w, slot, k):
                return w[:, slot, k * P:(k + 1) * P]

            def act_a(k0=0):
                return (lambda k: a_hi[:, k0 + k, :]), (lambda k: a_lo[:, k0 + k, :])

            def unit(key, act=None, part=None, ready=None):
                n = U.at[key]
                if part is None or part[0] == 0:
                    pe.wait_ge(S("w_lo"), n + 1)
                    begin(key)
                ins = products(n, act or act_a(), KT, bank(key), w_tile, part, ready=ready)
                if part is None or part[1] == UNIT:
                    ins.then_inc(S("gemm"), 1)

            def column_sums(key, src, lhs=ones):
                pe.matmul(begin(key), lhs, src, start=True, stop=True).then_inc(S("aux"), 1)

            def token_sums(dst, srcs):
                for c in range(NC):
                    for q, src in enumerate(srcs):
                        ins = pe.matmul(dst[:, c:c + 1], src[:, c * P:(c + 1) * P], ones[:, 0:1], start=q == 0,
                                        stop=q == len(srcs) - 1)
                return ins

            def spread(dst, factors):
                for c in range(NC):
                    ins = pe.matmul(dst[:, c * P:(c + 1) * P], factors[:, c:c + 1].to_broadcast([P, P]), ident,
                                    start=True, stop=True)
                return ins

            def norm(nu):
                n = NORMS[nu]
                pe.wait_ge(S(added(nu)), AD[nu] + n - 2)
                pe.wait_ge(S("sq"), SQ[nu] + n)
                wait(pe, "rstd", nu)
                token_sums(nb[:, 0:NC], (acc[:], sq[:, (n - 1) % 2, :])).then_inc(S("nsum"), 1)

            def norm_out(nu):
                pe.wait_ge(S("recip"), nu + 1)
                spread(nb, nst[:, 1, 0:NC]).then_inc(S("nout"), 1)

            pe.wait_ge(S("p_lo"), 1)
            for n in range(4):
                pe.wait_ge(S("w_lo"), n + 1)
                for q in range(2):
                    dst = begin(("pl", 2 * n + q))
                    ins = products(n, ((lambda k: p_hi[:, k, :]), (lambda k: p_lo[:, k, :])), 2, dst,
                                   lambda w, s, k: w[:, s, (2 * q + k) * P:(2 * q + k + 1) * P])
                ins.then_inc(S("gemm"), 1)
                if n == 1:
                    pe.wait_ge(S("in_c"), 16)
                    norm(0)
                    norm_out(0)
            for t in range(KT):
                unit(("glb", t), ready=None if t else fresh("h"))
                if t == 5:
                    norm_out(1)
                unit(("gla", t))
                if t == 3:
                    norm(1)
            n = U.at[("ab",)]
            pe.wait_ge(S("w_lo"), n + 1)
            dst = begin(("ab",))
            for k in range(KT):
                for p_, (b, w) in enumerate(((a_hi, w_hi), (a_lo, w_hi), (a_hi, w_lo))):
                    ins = pe.matmul(dst[0:32, :], w[:, n % 2, k * 32:(k + 1) * 32], b[:, k, :],
                                    start=k == 0 and p_ == 0, stop=k == KT - 1 and p_ == 2)
            ins.then_inc(S("gemm"), 1)

            def decay_inputs():
                ev_wait(pe, ("ab",))
                for c in range(NC):
                    ins = pe.transpose(nb2[:, c * 32:(c + 1) * 32], acc[0:32, c * P:(c + 1) * P], ident[0:32, 0:32])
                ins.then_inc(S("abt"), 1)

            def decay_sums():
                pe.wait_ge(S("g_raw"), 1)
                dst = begin(("gc",))
                for d in range(2):
                    pe.matmul(quad(dst[:, 0:64], NC)[:, :, d * 8:d * 8 + 8], tri[d], gat[:, 0, :, d * 8:d * 8 + 8],
                              start=True, stop=True)
                pe.matmul(quad(dst[:, 64:128], NC), ones, gat[:, 0], start=True, stop=True).then_inc(S("aux"), 1)

            def output_sums(h0, h1):
                for h in range(h0, h1):
                    pe.wait_ge(S("onsq"), h + 1)
                    b, c = (nb2, tmps[h % 2]) if h < HH else (nb, osq[h - HH])
                    token_sums(b[:, NC * (h % HH):NC * (h % HH) + NC], (c,)).then_inc(S("ons"), 1)

            def qkv(half):
                if half:
                    pe.wait_ge(S("o_acc"), NC)
                    pe.wait_ge(S("s_upd"), NC - 1)
                for hh in range(HH + 1):
                    h = HH * half + hh
                    if h == 0:
                        unit(("qkv", 0), part=(0, NORM_AT))
                        decay_inputs()
                        unit(("qkv", 0), part=(NORM_AT, UNIT))
                        decay_sums()
                    elif hh < HH:
                        unit(("qkv", 3 * h))
                    if half and hh == 2:
                        pe.wait_ge(S("csum"), KT - 1)
                        column_sums(("mean",), acc[:])
                    if hh:
                        pe.wait_ge(S("l2sq"), 2 * h)
                        for i in range(2):
                            ins = token_sums(nb[:, NC * i:NC * i + NC], (sq[:, i, :],))
                        ins.then_inc(S("l2s"), 1)
                    if hh < HH:
                        unit(("qkv", 3 * h + 1))
                    if hh:
                        pe.wait_ge(S("l2i"), h)
                        wait(pe, "qk_fin", 2 * (h - 1))
                        for i in range(2):
                            spread(l2b[:, i], nst[:, 1, NC * i:NC * i + NC]).then_inc(S("l2f"), 1)
                    if half and hh == 0:
                        output_sums(0, 2)
                    if hh < HH:
                        unit(("qkv", 3 * h + 2))
                    if half and hh == 0:
                        output_sums(2, HH)
                    if half and hh:
                        pe.wait_ge(S("on_r"), 1)
                        wait(pe, "on_g", hh - 1)
                        spread(nb2, ost[:, NC * (hh - 1):NC * hh]).then_inc(S("onf"), 1)
                    if half and hh == HH:
                        pe.wait_ge(S("cva"), KT - 1)
                        token_sums(nb[:, 0:NC], (rstd[:],)).then_inc(S("vsum"), 1)
                    if hh:
                        pe.wait_ge(S("qk_fin"), 2 * h)
                        wait(pe, "trc", 2 * (h - 1))
                        for c in range(NC):
                            ins = pe.transpose(trb[:, 0, c * P:(c + 1) * P], kT[:, hh - 1, c * P:(c + 1) * P], ident)
                        ins.then_inc(S("trp"), 1)
                        pe.wait_ge(S("silu"), 3 * h)
                        for c in range(NC):
                            ins = pe.transpose(trb[:, 1, c * P:(c + 1) * P],
                                               sacc[:, (h - 1) % 2, 2, c * P:(c + 1) * P], ident)
                        ins.then_inc(S("trp"), 1)
                if half:
                    pe.wait_ge(S("vinv"), 1)
                    spread(begin(("var",)), nst[:, 1, 0:NC]).then_inc(S("aux"), 1)

            def gap(R, g):
                for key, q, e in parts(R, g):
                    unit(key, part=(q, e), ready=fresh("conv") if key == ("co", 0) else None)

            halves = (slice(0, W64), slice(W64, P))

            def turned(dst, src, s):
                if s == halves[0]:
                    return pe.transpose(dst, src, id64[s, :])
                return pe.matmul(dst, src, id64[s, :], start=True, stop=True)

            def small(dst, lhs, rhs):
                for j in range(J):
                    for s in halves:
                        if rhs is None:
                            ins = turned(dst[s, j, :], lhs[s, j, :], s)
                        else:
                            ins = pe.matmul(dst[s, j, :], lhs[s, j, :], rhs[s, j, :], start=True, stop=True)
                return ins

            def delta(R):
                half, r = divmod(R, NC)
                prob = [(j, j // HH, j % HH, chunk(j // HH, r)) for j in range(J)]
                wait(pe, "g_all", 1)
                wait(pe, "o_acc", R)
                if r == 0:
                    pe.wait_ge(S("trc"), 2 * HH * (half + 1))
                    if half:
                        pe.wait_ge(S("on_g"), HH)
                for j, d, hh, c in prob:
                    g_col = gat[:, 0, c, d * 8 + HH * half + hh:d * 8 + HH * half + hh + 1]
                    ins = pe.matmul(pA[:, j, :], g_col.to_broadcast([P, P]), tri[d], start=True, stop=True)
                ins.then_inc(S("grow"), 1)
                for j, d, hh, c in prob:
                    tok = slice(c * P, (c + 1) * P)
                    ins = pe.matmul(pB[:, j, :], kT[:, hh, tok], kT[:, hh, tok], start=True, stop=True)
                ins.then_inc(S("gram"), 1)
                gap(R, 0)
                pe.wait_ge(S("eg"), R + 1)
                for j, d, hh, c in prob:
                    tok = slice(c * P, (c + 1) * P)
                    ins = pe.matmul(pA[:, j, :], kT[:, hh, tok], qT[:, hh, tok], start=True, stop=True)
                ins.then_inc(S("kq"), 1)
                gap(R, 1)
                for lv in range(LEVELS):
                    pe.wait_ge(S("ls"), LEVELS * R + lv + 1)
                    if lv == 0:
                        wait(pe, "s_upd", (NC - 1) * half + r)
                        small(c0, ls[:, 0], None).then_inc(S("y"), 1)
                        gap(R, 2)
                        continue
                    pe.wait_ge(S("u_upd"), LEVELS * R + lv)
                    small(c0, ls[:, lv % 2], ub).then_inc(S("y"), 1)
                    if lv > 1:
                        small(ctr, ub, None).then_inc(S("tr"), 1)
                    gap(R, 2 * lv + 1)
                    pe.wait_ge(S("ycp"), LEVELS * R + lv)
                    wait(pe, "tcp", (LEVELS - 1) * R + lv - 1)
                    small(c1, tb, yb).then_inc(S("uy"), 1)
                    gap(R, 2 * lv + 2)
                pe.wait_ge(S("u_upd"), LEVELS * (R + 1))
                lo, hi = halves
                for j in range(J):
                    s, b = (hi, lo) if j < HH else (lo, hi)
                    ins = pe.matmul(c0[b, j, :], en[s, j, b], en[s, j, s], start=True, stop=True)
                ins.then_inc(S("yf"), 1)
                for j in range(J):
                    b = lo if j < HH else hi
                    ins = turned(ctr[b, j, :], en[b, j, b], b)
                ins.then_inc(S("tr"), 1)
                gap(R, 13)
                pe.wait_ge(S("ycp"), LEVELS * (R + 1))
                pe.wait_ge(S("tcp"), (LEVELS - 1) * (R + 1))
                for j in range(J):
                    b = lo if j < HH else hi
                    ins = pe.matmul(c1[b, j, :], tb[b, j, :], yb[b, j, :], start=True, stop=True)
                ins.then_inc(S("u12"), 1)
                gap(R, 14)
                pe.wait_ge(S("u12s"), R + 1)
                pe.wait_ge(S("kb"), R + 1)
                pe.wait_ge(S("qk"), 2 * R + 2)
                for j in range(J):
                    ins = pe.matmul(pA[:, j, :], kb[:, j, :], en[:, j, :], start=True, stop=True)
                ins.then_inc(S("wt"), 1)
                gap(R, 15)
                pe.wait_ge(S("bv"), R + 1)
                pe.wait_ge(S("wtcp"), R + 1)
                wait(pe, "s_upd", (NC - 1) * half + r)
                for j in range(J):
                    ins = pe.matmul(pB[:, j, :], en[:, j, :], bv[:, j, :], start=True, stop=r == 0)
                    if r:
                        ins = pe.matmul(pB[:, j, :], kb[:, j, :], st[:, j, :], start=False, stop=True)
                ins.then_inc(S("vn"), 1)
                gap(R, 16)
                pe.wait_ge(S("vcp"), R + 1)
                pe.wait_ge(S("qdm"), R + 1)
                for j in range(J):
                    if r:
                        pe.matmul(pA[:, j, :], st[:, j, :], qd[:, j, :], start=True, stop=False)
                    ins = pe.matmul(pA[:, j, :], bv[:, j, :], et[:, j, :], start=r == 0, stop=True)
                ins.then_inc(S("o"), 1)
                if r < NC - 1:
                    pe.wait_ge(S("kt"), (NC - 1) * half + r + 1)
                    for j in range(J):
                        ins = pe.matmul(pC[:, j, :], kt[:, j, :], bv[:, j, :], start=True, stop=True)
                    ins.then_inc(S("s"), 1)
                gap(R, 17)

            qkv(0)
            for R in range(4):
                delta(R)
            qkv(1)
            for R in range(4, 8):
                delta(R)
            output_sums(HH, H)
            for t in range(2):
                unit(("do", t), part=(0, UNIT // 2), ready=fresh("o"))
            pe.wait_ge(S("on_r"), 2)
            for h in range(HH, H):
                spread(onb(h), ost[:, NC * h:NC * h + NC]).then_inc(S("onf"), 1)
            for t in range(2):
                unit(("do", t), part=(UNIT // 2, UNIT), ready=fresh("o"))
            for t in range(2, KT):
                unit(("do", t))
            for t in range(KT):
                unit(("wo", t), ((lambda k: yb_hi[:, k, :]), (lambda k: yb_lo[:, k, :])),
                     ready=None if t else ("yb_lo", 1))

            def ffn(f, nu, s):
                def step(i):
                    for j in range(4):
                        nm = ("fg" if j % 2 == 0 else "fu") + f
                        n = U.at[(nm, j // 2)] + 4 * i
                        pe.wait_ge(S("w_lo"), n + 1)
                        if isinstance(i, int):
                            dst = begin((nm, 2 * i + j // 2))
                        else:
                            o = O.at[(nm, 2 + j // 2)]
                            pe.wait_ge(S("evD"), O.count(o - 2) - 4 + 4 * i)
                            dst = pg[:, o % 2, :]
                        first = isinstance(i, int) and i == 0
                        if first and j == 1:
                            products(U.at[(nm, j // 2)], act_a(), KT, dst, w_tile, (0, NORM_AT))
                            norm_out(nu)
                        products(U.at[(nm, j // 2)], act_a(), KT, dst, w_tile,
                                 (NORM_AT, UNIT) if first and j == 1 else None,
                                 ready=fresh(s) if first and j == 0 else None).then_inc(S("gemm"), 1)
                        if first and j == 0:
                            norm(nu)

                step(0)
                with pe.Fori(1, FT // 2) as i:
                    step(i)
                for m in range(KT):
                    dst = begin(("fd" + f, m))
                    for q in range(2):
                        n = U.at[("fd" + f, 2 * m + q)]
                        pe.wait_ge(S("w_lo"), n + 1)
                        products(n, ((lambda k: h_hi[:, KH * q + k, :]), (lambda k: h_lo[:, KH * q + k, :])),
                                 KH, dst, w_tile, None, q == 0, q == 1,
                                 None if m else ("h_lo", FT * int(f) + KH * q + 1)).then_inc(S("gemm"), 1)

            ffn("0", 2, "ffn0")
            for t in range(KT):
                if t == 1:
                    unit(("pg", t), part=(0, NORM_AT))
                    norm_out(3)
                unit(("pg", t), part=(NORM_AT, UNIT) if t == 1 else None, ready=None if t else fresh("pg"))
                if t == 0:
                    norm(3)
            norm(4)
            norm_out(4)
            ffn("1", 5, "ffn1")
            norm(6)
            norm_out(6)
            def rotate(i):
                if i == 0:
                    pe.wait_ge(S("in_c2"), 16)
                ev_wait(pe, ("mq", i - 1) if i else ("mk", 0))
                if i < 3:
                    wait(pe, "qk2", i - 1)
                    pe.matmul(rpb[i], perm, zq[:, i], start=True, stop=True).then_inc(S("rpart"), 1)
                else:
                    column_sums(("rp", i), zq[:, i], perm)

            def pooled(g):
                pe.wait_ge(S("wd"), PT_ - g)
                column_sums(("yp", g), wd[:, g], wpool[:, g])

            unit(("mk", 0), ready=fresh("mix"))
            norm(7)
            unit(("mv", 0), part=(0, NORM_AT))
            norm_out(7)
            unit(("mv", 0), part=(NORM_AT, UNIT))
            unit(("mq", 0))
            unit(("mq", 1), part=(0, NORM_AT))
            rotate(0)
            ev_wait(pe, ("mv", 0))
            for c in range(NB):
                ins = pe.transpose(pc2[:, 0, c * P:(c + 1) * P], zv[:, c * P:(c + 1) * P], ident)
            ins.then_inc(S("vtp"), 1)
            unit(("mq", 1), part=(NORM_AT, UNIT))
            unit(("mq", 2), part=(0, NORM_AT))
            rotate(1)
            unit(("mq", 2), part=(NORM_AT, UNIT))
            heads = (slice(0, HD2), slice(HD2, P))

            def scores(s):
                i, n = divmod(s, NB)
                pe.wait_ge(S("qk2"), i + 2)
                wait(pe, "smask", s - 1)
                k0 = 1 if n == 0 else 0
                pe.matmul(pa2[:, s % 2, :, k0 * P:2 * P], qk2[:, i, n * P:(n + 1) * P],
                          kz[:, :, (n - 1 + k0) * P:(n + 1) * P], start=True, stop=True).then_inc(S("scores"), 1)

            def turn(s):
                k0 = 1 if s % NB == 0 else 0
                pe.wait_ge(S("prob"), s + 1)
                if s == 0:
                    pe.wait_ge(S("qk2"), 2)
                wait(pe, "ptcp", s - 1)
                for h in range(2):
                    for kb_ in range(k0, 2):
                        ins = pe.transpose(pb2[:, s % 2, h, kb_, :], sm[:, s % 3, h, kb_ * P:(kb_ + 1) * P], ident)
                ins.then_inc(S("turn"), 1)

            def values(s):
                i, n = divmod(s, NB)
                k0 = 1 if n == 0 else 0
                pe.wait_ge(S("ptcp"), s + 1)
                if s == 0:
                    pe.wait_ge(S("vtc"), 1)
                if n == 0:
                    wait(pe, "oat", i - 1)
                for h in range(2):
                    for kb_ in range(k0, 2):
                        ins = pe.matmul(pc2[heads[h], i % 2, n * P:(n + 1) * P],
                                        vt2[:, n - 1 + kb_, heads[h]], ptb[:, s % 2, h, kb_, :],
                                        start=kb_ == k0, stop=kb_ == 1)
                ins.then_inc(S("values"), 1)

            for s in range(16 + 3):
                if s < 16:
                    scores(s)
                if 0 <= s - 2 < 16:
                    turn(s - 2)
                if 0 <= s - 3 < 16:
                    values(s - 3)
                if s < 15:
                    unit(MFILL[s // 3], part=(s % 3 * UNIT // 3, (s % 3 + 1) * UNIT // 3))
                if s == 0:
                    rotate(2)
                for k in MAUX.get(s, []):
                    (rotate if k[0] == "rp" else pooled)(k[1])
            pooled(0)

            norm(8)
            norm_out(8)
            norm(9)
            norm_out(9)
            for t in range(KT):
                unit(("mo", t), ready=None if t else fresh("out"))
            norm(10)
            norm_out(10)
            ffn("2", 11, "ffn2")
            norm(12)
            norm_out(12)

        @block.scalar
        def _(act):
            def hi(n, i=0, cols=None):
                act.wait_ge(S(f"w_in{n % 4}"), 16 * (n // 4 + 1) + 16 * i)
                if not (isinstance(i, int) and n < 2):
                    act.wait_ge(S("gemm"), n - 1 + 4 * i)
                c = U.cols[n] if cols is None else cols
                act.activation(w_hi[:, n % 2, 0:c], w_raw[:, n % 4, 0:c], ACT.Copy).then_inc(S("w_hi"), 1)

            def after(key):
                n = U.at[key]
                unit_out(act, key)
                if n + 2 < N_UNITS:
                    hi(n + 2)

            def square(nu, t, src):
                if t == 0:
                    wait(act, "nsum", nu)
                    dst = acc[:]
                else:
                    wait(act, added(nu), AD[nu] + t - 2 if t > 2 else 0)
                    dst = sq[:, t % 2, :]
                act.activation(dst, src, ACT.Square).then_inc(S("sq"), 1)

            def root(nu):
                act.wait_ge(S("nsum"), nu + 1)
                act.activation(nst[:, 0, 0:NC], nb[:, 0:NC], ACT.Sqrt, scale=1.0 / (P * NORMS[nu]),
                               bias=eps_t[:, 0:1]).then_inc(S("root"), 1)

            def high_o(h):
                act.wait_ge(S("on_z" if h < HH else "on_g"), h + 1)
                act.activation(a_hi[:, h], oT[:, h], ACT.Copy).then_inc(S("a_hi"), 1)

            act.wait_ge(S("in_p"), 16)
            act.activation(p_hi[:], praw[:], ACT.Copy).then_inc(S("p_hi"), 1)
            hi(0)
            hi(1)
            for n in range(4):
                after(("pl", n))
                for q in range(2):
                    t = 2 * n + q
                    act.activation(ptile[:, t], bank(("pl", t)), ACT.Copy).then_inc(S("evA"), 1)
                if n == 0:
                    for t in range(KT):
                        act.wait_ge(S(f"in_x{t // 2}"), 16)
                        square(0, t, xin[:, t])
                if n == 1:
                    act.wait_ge(S("in_g"), 16)
                    root(0)
            for t in range(KT):
                act.wait_ge(S("hx"), t + 1)
                act.activation(a_hi[:, t], xin[:, t], ACT.Copy).then_inc(S("a_hi"), 1)
            act.wait_ge(S("evA"), 8)
            for t in range(KT):
                after(("glb", t))
                if t >= 2:
                    ev_wait(act, ("gla", t - 2))
                act.activation(tmps[t % 2][:], bank(("glb", t)), ACT.Sigmoid).then_inc(S("evA"), 1)
                if t < 4:
                    square(1, 2 * t, ptile[:, 2 * t])
                if t == 4:
                    root(1)
                after(("gla", t))
                if t < 4:
                    square(1, 2 * t + 1, ptile[:, 2 * t + 1])
            after(("ab",))
            act.wait_ge(S("in_g"), 16)
            act.activation(gat[:, 5, 0, :], gate_p[:, 0:16], ACT.Exp).then_inc(S("gA"), 1)
            act.wait_ge(S("gD"), 1)
            act.activation(gat[:, 2], gat[:, 3], ACT.Exp).then_inc(S("gA"), 1)
            act.wait_ge(S("gA"), 2)
            act.activation(gat[:, 4], gat[:, 2], ACT.Ln, bias=1.0).then_inc(S("gA"), 1)
            act.wait_ge(S("gb"), 1)
            act.activation(gat[:, 1], gat[:, 1], ACT.Sigmoid).then_inc(S("gA"), 1)
            def decay_factors():
                aux_out(act, ("gc",))
                b = bank(("gc",))
                act.activation(gat[:, 2], quad(b[:, 0:64], NC), ACT.Copy).then_inc(S("gA"), 1)
                act.activation(gat[:, 4], quad(b[:, 64:128], NC), ACT.Copy).then_inc(S("evA"), 1)
                act.wait_ge(S("gA"), 5)
                act.activation(gat[:, 3], gat[:, 2], ACT.Exp).then_inc(S("gA"), 1)
                ev_wait(act, ("gc",))
                act.activation(gat[:, 5], gat[:, 4], ACT.Exp).then_inc(S("gA"), 1)
                act.wait_ge(S("gD"), 3)
                act.activation(gat[:, 4], gat[:, 4], ACT.Exp).then_inc(S("g_all"), 1)

            def qkv(half):
                def padded(h, i):
                    key = ("qkv", 3 * h + i)
                    unit_out(act, key)
                    if h == 0 and i == 0:
                        act.wait_ge(S("a_lo"), KT)
                        act.wait_ge(S("spp"), 16)
                    wait(act, "stap", SK * (3 * (h - 1) + i + 1))
                    act.activation(pad[:, i, SP_:SP_ + T], bank(key), ACT.Copy).then_inc(S("evA"), 1)
                    after(key)

                def silu(h, i):
                    act.wait_ge(S("stap"), SK * (3 * h + i + 1))
                    y = sacc[:, h % 2, i]
                    act.activation(y, y, ACT.Silu).then_inc(S("silu"), 1)
                    if i < 2:
                        act.wait_ge(S("silu"), 3 * h + i + 1)
                        wait(act, "l2s", h)
                        act.activation(sq[:, i, :], y, ACT.Square).then_inc(S("l2sq"), 1)

                def head_squares(h0, h1):
                    for g in range(h0, h1):
                        act.wait_ge(S("o_acc"), NC)
                        if g < 2:
                            act.wait_ge(S(f"spill{g}"), 16 * 8)
                        else:
                            act.wait_ge(S("ons"), g - 1)
                        act.activation(tmps[g % 2][:], oT[:, g], ACT.Square).then_inc(S("onsq"), 1)

                def conv_squares(t0, t1):
                    for t in range(t0, t1):
                        act.wait_ge(S("xc"), t + 1)
                        if t > 2:
                            act.wait_ge(S("cva"), t - 2)
                        act.activation(rstd[:] if t == 0 else tmps[t % 2][:], cslot(t), ACT.Square)\
                            .then_inc(S("cvs"), 1)

                for hh in range(HH + 1):
                    h = HH * half + hh
                    if hh < HH:
                        if hh == 0 and half:
                            act.wait_ge(S("o"), 4)
                            act.wait_ge(S("s_upd"), 3)
                        padded(h, 0)
                    if h == 0:
                        decay_factors()
                    if half and hh == 0:
                        head_squares(0, 2)
                    if half and hh == 2:
                        aux_out(act, ("mean",))
                        act.activation(acc[:], bank(("mean",)), ACT.Copy, scale=1.0 / D).then_inc(S("evA"), 1)
                    if half and hh == 3:
                        conv_squares(0, 4)
                    if hh:
                        silu(h - 1, 2)
                        act.wait_ge(S("l2s"), h)
                        for i, s in enumerate((float(P), 1.0)):
                            c = slice(NC * i, NC * i + NC)
                            ins = act.activation(nst[:, 0, c], nb[:, c], ACT.Sqrt, scale=s, bias=eps_t[:, 1 + i:2 + i])
                        ins.then_inc(S("l2r"), 1)
                    if half and hh == 1:
                        act.wait_ge(S("ons"), HH)
                        act.activation(ost[:, 0:HH * NC], nb2[:, 0:HH * NC], ACT.Sqrt, scale=1.0 / P,
                                       bias=eps_t[:, 0:1]).then_inc(S("on_root"), 1)
                    if hh < HH:
                        padded(h, 1)
                        if half and hh == 0:
                            head_squares(2, HH)
                        if half and hh == 3:
                            conv_squares(4, KT)
                        silu(h, 0)
                        padded(h, 2)
                        silu(h, 1)
                    if half and hh == HH:
                        act.wait_ge(S("vsum"), 1)
                        act.activation(nst[:, 0, 0:NC], nb[:, 0:NC], ACT.Sqrt, scale=1.0 / D, bias=eps_t[:, 3:4])\
                            .then_inc(S("vroot"), 1)
                    if hh:
                        if half and hh == 1:
                            act.wait_ge(S("bv"), 4)
                            act.wait_ge(S("kb"), 4)
                            act.wait_ge(S("kt"), NC - 1)
                        for i, dst in enumerate((ktok, vtok)):
                            act.wait_ge(S("trp"), 2 * (h - 1) + i + 1)
                            act.activation(dst[:, hh - 1], quad(trb[:, i], NC), ACT.Copy).then_inc(S("trc"), 1)

            spilled = [0]

            CA = {1: (0, 1), 3: (2,), 5: (3,), 7: (4,), 9: (5,), 11: (6,), 15: (7,)}

            def gap(R, g):
                if R == 5:
                    for t in CA.get(g, ()):
                        act.wait_ge(S("xn"), t + 1)
                        act.activation(cslot(t), cslot(t), ACT.Silu, scale=v("ln_g", t), bias=v("ln_b", t))\
                            .then_inc(S("ca"), 1)
                for key in filled(R, g):
                    after(key)
                    if key[0] == "co":
                        continue
                    k = spilled[0]
                    spilled[0] += 1
                    if k < 2:
                        ev_wait(act, ("gla", 6 + k))
                    elif k < 16:
                        act.wait_ge(S(f"spill{k % 2}"), 16 * (k // 2))
                    elif k < 18:
                        act.wait_ge(S("cva"), KT - 1)
                    elif k < 22:
                        act.wait_ge(S("on_z"), k - 17)
                    else:
                        act.wait_ge(S(f"spill{k % 2}"), 16 * (k // 2 - 2))
                    func, dst = (ACT.Sigmoid, spill_g[key[1]]) if key[0] == "gate" else (ACT.Silu, spill_z[key[1]])
                    act.activation(tmps[k % 2][:], bank(key), func).then_inc(S("evA"), 1)
                    if key[0] == "z" and key[1] < HH:
                        continue
                    ev_wait(act, key)
                    act.dma_start(dst, tmps[k % 2][:]).then_inc(S(f"spill{k % 2}"), 16)

            lo, hi_ = slice(0, W64), slice(W64, P)

            def conv_hi(t0, t1):
                for t in range(t0, t1):
                    act.wait_ge(S("ca"), t + 1)
                    act.activation(a_hi[:, t], cslot(t), ACT.Copy).then_inc(S("a_hi"), 1)

            def delta(R):
                half, r = divmod(R, NC)
                act.wait_ge(S("pre"), 3 * R + 1)
                wait(act, "o", R)
                act.activation(qd[:], pA[:], ACT.Exp).then_inc(S("eg"), 1)
                act.wait_ge(S("pre"), 3 * R + 2)
                act.activation(en[:], en[:], ACT.Exp, scale=-1.0).then_inc(S("en"), 1)
                act.wait_ge(S("pre"), 3 * R + 3)
                act.activation(et[:], et[:], ACT.Exp).then_inc(S("et"), 1)
                if R == 6:
                    conv_hi(3, KT)
                act.wait_ge(S("L"), R + 1)
                wait(act, "ls", LEVELS * R)
                act.activation(lc[lo], en[lo, :, lo], ACT.Copy)
                act.activation(lc[hi_], en[hi_, :, hi_], ACT.Copy).then_inc(S("lc"), 1)
                gap(R, 0)
                gap(R, 1)
                for lv in range(1, LEVELS):
                    act.wait_ge(S("y"), LEVELS * R + lv + 1)
                    act.activation(yb[:], c0, ACT.Copy).then_inc(S("ycp"), 1)
                    gap(R, 2 * lv)
                    gap(R, 2 * lv + 1)
                act.wait_ge(S("yf"), R + 1)
                act.activation(yb[lo, 0:HH], c0[lo, 0:HH], ACT.Copy)
                act.activation(yb[hi_, HH:J], c0[hi_, HH:J], ACT.Copy).then_inc(S("ycp"), 1)
                gap(R, 12)
                gap(R, 13)
                act.wait_ge(S("wt"), R + 1)
                act.activation(kb[:, 0:HH], pA[:, 0:HH], ACT.Copy, scale=-1.0)
                act.activation(kb[:, HH:J], pA[:, HH:J], ACT.Copy, scale=-1.0).then_inc(S("wtcp"), 1)
                gap(R, 14)
                gap(R, 15)
                act.wait_ge(S("vn"), R + 1)
                act.activation(bv[:, 0:HH], pB[:, 0:HH], ACT.Copy)
                act.activation(bv[:, HH:J], pB[:, HH:J], ACT.Copy).then_inc(S("vcp"), 1)
                gap(R, 16)
                gap(R, 17)

            qkv(0)
            for R in range(4):
                delta(R)
            qkv(1)
            for R in range(4, 8):
                if R == 6:
                    conv_hi(0, 3)
                delta(R)
            act.wait_ge(S("o_acc"), 8)
            for h in range(HH, H):
                act.activation(osq[h - HH], oT[:, h], ACT.Square).then_inc(S("onsq"), 1)
            act.wait_ge(S("ons"), H)
            act.activation(ost[:, HH * NC:], nb[:, 0:HH * NC], ACT.Sqrt, scale=1.0 / P, bias=eps_t[:, 0:1])\
                .then_inc(S("on_root"), 1)
            for h in range(H):
                high_o(h)
            for t in range(KT):
                after(("do", t))
                act.wait_ge(S("yv"), t + 1)
                act.activation(yb_hi[:, t], ya[:, t], ACT.Copy).then_inc(S("yb_hi"), 1)

            def xset(s, t, g, nu):
                act.activation(a_hi[:, t], x[:, t], ACT.Copy, scale=v(g, t)).then_inc(S("a_hi"), 1)
                square(nu, t, x[:, t])

            for t in range(KT):
                after(("wo", t))
                ev_wait(act, ("wo", t))
                xset("ffn0", t, "g_ffn", 2)

            def ffn(f, nu, g, nu2):
                def step(i):
                    for q in range(2):
                        n = U.at[("fg" + f, q)]
                        act.wait_ge(S("gemm"), n + 1 + 4 * i)
                        hi(n + 2, i, U.cols[n + 2 + (4 * i if isinstance(i, int) else 0)])
                        if q == 0 and isinstance(i, int) and i == 0:
                            root(nu)
                        dg = O.count(O.at[("fg" + f, q)])
                        act.wait_ge(S("evD"), dg + 4 * i)
                        act.activation(tmp1[:], tmp1[:], ACT.Silu).then_inc(S("sil"), 1)
                        act.wait_ge(S("gemm"), n + 2 + 4 * i)
                        hi(n + 3, i, U.cols[n + 3 + (4 * i if isinstance(i, int) else 0)])
                        act.wait_ge(S("hm"), FT * int(f) + q + 1 + 2 * i)
                        m = 2 * i + q
                        act.activation(h_hi[:, m] if isinstance(i, int) else
                                       h_hi[:, bass.ds(m, 1)].rearrange("p a n -> p (a n)"),
                                       tmp2[:], ACT.Copy).then_inc(S("h_hi"), 1)

                step(0)
                with act.Fori(1, FT // 2 - 1) as i:
                    step(i)
                step(FT // 2 - 1)
                if f == "0":
                    rope_tables()
                for m in range(KT):
                    after(("fd" + f, 2 * m))
                    if f == "0":
                        after(("fd" + f, 2 * m + 1))
                        ev_wait(act, ("fd" + f, m))
                        xset("pg", m, g, nu2)
                    else:
                        unit_out(act, ("fd" + f, 2 * m + 1))
                        square(nu2, m, bank(("fd" + f, m)))
                        act.activation(hb[:, m], bank(("fd" + f, m)), ACT.Copy, scale=v(g, m)).then_inc(S("evA"), 1)
                        after(("fd" + f, 2 * m + 1))

            def rope_tables():
                act.wait_ge(S("rope"), 1)
                act.activation(rsin[:], rcos[:], ACT.Sin).then_inc(S("rsin"), 1)
                act.wait_ge(S("rsin"), 1)
                act.activation(rcos[:], rpos[:].bitcast(F32), ACT.Sin, scale=-1.0, bias=gate_p[:, 58:59])\
                    .then_inc(S("rsin"), 1)

            ffn("0", 2, "g_pl", 3)
            for t in range(KT):
                if t == 0:
                    after(("pg", t))
                    root(3)
                ev_wait(act, ("pg", t))
                act.activation(tmps[t % 2][:], tmps[t % 2][:], ACT.Sigmoid).then_inc(S("pgs"), 1)
                if t:
                    after(("pg", t))
                act.wait_ge(S("x2"), t + 1)
                square(4, t, x[:, t])
            root(4)

            for t in range(KT):
                act.wait_ge(S("xf"), t + 1)
                xset("ffn1", t, "ffn1_pre", 5)
            ffn("1", 5, "ffn1_post", 6)

            def post(nu, k, s, g, nu2):
                root(nu)
                if s:
                    for t in range(KT):
                        act.wait_ge(S("xu"), KT * k + t + 1)
                        xset(s, t, g, nu2)

            post(6, 0, "mix", "mix_pre", 7)
            after(("mk", 0))
            root(7)
            after(("mv", 0))
            after(("mq", 0))
            act.wait_ge(S("vtp"), 1)
            act.activation(vt2[:], quad(pc2[:, 0], NB), ACT.Copy).then_inc(S("vtc"), 1)
            after(("mq", 1))
            after(("mq", 2))

            def prob(s):
                k0 = P if s % NB == 0 else 0
                act.wait_ge(S("bias"), s + 1)
                for h in range(2):
                    y = sm[:, s % 3, h, k0:]
                    act.activation(y, y, ACT.Exp, scale=HD2 ** -0.5, bias=sml[:, 1, s, h:h + 1],
                                   accum_out=sml[:, 2, s, h:h + 1])
                act.activation(sml[:, 3, s], sml[:, 3, s], ACT.Exp).then_inc(S("exp"), 1)

            def pt_copy(s):
                k0 = 1 if s % NB == 0 else 0
                act.wait_ge(S("turn"), s + 1)
                wait(act, "values", s - 1)
                act.activation(ptb[:, s % 2, :, k0:], pb2[:, s % 2, :, k0:], ACT.Copy).then_inc(S("ptcp"), 1)

            def pooled(g):
                aux_out(act, ("yp", g))
                act.activation(mo[:, g], bank(("yp", g)), ACT.Copy, scale=gate_p[:, 46 + g:47 + g])\
                    .then_inc(S("evA"), 1)
                ev_wait(act, ("yp", g))
                square(8, PT_ - 1 - g, mo[:, g])

            for s in range(16 + 3):
                if s < 16:
                    prob(s)
                if 0 <= s - 2 < 16:
                    pt_copy(s - 2)
                if s < 15 and s % 3 == 2:
                    after(MFILL[s // 3])
                for k in MAUX.get(s, []):
                    if k[0] == "yp":
                        pooled(k[1])
            pooled(0)
            root(8)
            for i in range(PT_):
                act.wait_ge(S("oat"), i + 1)
                square(9, i, mo[:, PT_ + i])
            for t in range(PT_):
                act.wait_ge(S("mh"), t + 1)
                act.activation(a_hi[:, t], mo[:, t], ACT.Copy).then_inc(S("a_hi"), 1)
            root(9)
            for t in range(PT_, KT):
                act.wait_ge(S("mh"), t + 1)
                act.activation(a_hi[:, t], mo[:, t], ACT.Copy).then_inc(S("a_hi"), 1)
            for t in range(KT):
                unit_out(act, ("mo", t))
                square(10, t, bank(("mo", t)))
                act.activation(hb2[:, t], bank(("mo", t)), ACT.Copy, scale=v("mix_post", t)).then_inc(S("evA"), 1)
                after(("mo", t))
            post(10, 1, "ffn2", "ffn2_pre", 11)
            ffn("2", 11, "ffn2_post", 12)
            post(12, 2, None, None, None)

        @block.vector
        def _(dve):
            def lo(n, i=0, cols=None):
                dve.wait_ge(S("w_hi"), n + 1 + 4 * i)
                c = U.cols[n] if cols is None else cols
                dve.tensor_tensor(w_lo[:, n % 2, 0:c], w_raw[:, n % 4, 0:c],
                                  w_hi[:, n % 2, 0:c].bitcast(F32), ALU.subtract).then_inc(S("w_lo"), 1)

            def after(key):
                if U.at[key] + 2 < N_UNITS:
                    lo(U.at[key] + 2)

            def recip(nu, parts_=(0, 1)):
                if 0 in parts_:
                    dve.wait_ge(S("root"), nu + 1)
                    wait(dve, "nout", nu)
                    dve.reciprocal(nst[:, 1, 0:NC], nst[:, 0, 0:NC]).then_inc(S("recip"), 1)
                if 1 not in parts_:
                    return
                dve.wait_ge(S("nout"), nu + 1)
                dve.tensor_copy(rstd[:], nb).then_inc(S("rstd"), 1)
                dve.wait_ge(S("rstd"), nu + 1)

            def low(s, t, src, scale=None):
                dve.wait_ge(S("a_hi"), set_count(s, t))
                if scale is None:
                    ins = dve.tensor_tensor(a_lo[:, t], src, a_hi[:, t].bitcast(F32), ALU.subtract)
                else:
                    ins = dve.scalar_tensor_tensor(a_lo[:, t], src, scale, a_hi[:, t].bitcast(F32),
                                                   ALU.mult, ALU.subtract)
                ins.then_inc(S("a_lo"), 1)

            done_taps = [0]

            def taps(count):
                for q in range(done_taps[0], min(done_taps[0] + count, len(TAPS))):
                    t, j = TAPS[q]
                    src, w = cpad[:, t, j:j + T], vec[:, t, len(VEC) + j:len(VEC) + j + 1]
                    if j == 0:
                        ev_wait(dve, ("gla", t))
                        if t >= 3:
                            dve.wait_ge(S("tap"), TAPS.index((t - 2, CK - 1)) + 1)
                        ins = dve.tensor_scalar(cslot(t), src, w, v("conv_b", t), ALU.mult, ALU.add)
                    else:
                        dve.wait_ge(S("tap"), TAPS.index((t, j - 1)) + 1)
                        ins = dve.scalar_tensor_tensor(cslot(t), src, w, cslot(t), ALU.mult, ALU.add)
                    ins.then_inc(S("tap"), 1)
                done_taps[0] = min(done_taps[0] + count, len(TAPS))

            dve.memset(cpad[:, :, 0:CP], 0.0)
            dve.memset(cpad[:, :, CP + T:PAD], 0.0).then_inc(S("czero"), 1)
            dve.wait_ge(S("p_hi"), 1)
            dve.tensor_tensor(p_lo[:], praw[:], p_hi[:].bitcast(F32), ALU.subtract).then_inc(S("p_lo"), 1)
            lo(0)
            lo(1)
            after(("pl", 0))
            for t in range(1, KT - 1):
                dve.wait_ge(S("sq"), t + 1)
                wait(dve, "add0", t - 1)
                dve.tensor_tensor(acc[:], acc[:], sq[:, t % 2, :], ALU.add).then_inc(S("add0"), 1)
            after(("pl", 1))
            recip(0)
            after(("pl", 2))
            dve.wait_ge(S("in_v"), 16)
            for t in range(KT // 2):
                dve.wait_ge(S(f"in_x{t}"), 16)
            for t in range(KT + 1):
                if t == KT - 1:
                    after(("pl", 3))
                if t < KT:
                    dve.scalar_tensor_tensor(xin[:, t], xin[:, t], v("g_mix", t), rstd[:], ALU.mult, ALU.mult)\
                        .then_inc(S("hx"), 1)
                if t:
                    low("h", t - 1, xin[:, t - 1])
            dve.wait_ge(S("a_lo"), KT)
            dve.wait_ge(S("a_hi"), KT)
            dve.memset(pad[:, :, 0:SP_], 0.0)
            dve.memset(pad[:, :, SP_ + T:], 0.0).then_inc(S("pzero"), 1)
            dve.wait_ge(S("czero"), 1)
            for t in range(KT):
                after(("glb", t))
                if t == 5:
                    recip(1, (1,))
                    dve.wait_ge(S("sq"), 2 * KT)
                    for q in range(KT):
                        dve.scalar_tensor_tensor(ptile[:, q], ptile[:, q], v("g_plp", q), rstd[:],
                                                 ALU.mult, ALU.mult).then_inc(S("plf"), 1)
                unit_out(dve, ("gla", t))
                ev_wait(dve, ("glb", t))
                dve.tensor_tensor(cpad[:, t, CP:CP + T], bank(("gla", t)), tmps[t % 2][:], ALU.mult)\
                    .then_inc(S("evD"), 1)
                after(("gla", t))
                if t == 4:
                    recip(1, (0,))
                if t >= 2:
                    taps(taps_unit)
            unit_out(dve, ("ab",))
            dve.wait_ge(S("nout"), 2)
            dve.tensor_copy(acc[0:32], bank(("ab",))[0:32]).then_inc(S("evD"), 1)
            after(("ab",))
            dve.wait_ge(S("abt"), 1)
            ab = quad(nb2[:, 0:P], NC)
            dve.wait_ge(S("in_g"), 16)
            dt = gate_p[:, 16:32].unsqueeze(1).to_broadcast([P, NC, 16])
            dve.tensor_tensor(gat[:, 2], ab[:, :, 0:16], dt, ALU.add).then_inc(S("gd"), 1)
            dve.tensor_copy(gat[:, 1], ab[:, :, 16:32]).then_inc(S("gb"), 1)
            dve.wait_ge(S("gd"), 1)
            dve.scalar_tensor_tensor(gat[:, 3], gat[:, 2], -1.0, gat[:, 2], ALU.mult, ALU.min).then_inc(S("gd"), 1)
            dve.wait_ge(S("gd"), 2)
            dve.tensor_scalar(gat[:, 0], gat[:, 2], 0.0, None, ALU.max).then_inc(S("gD"), 1)
            dve.wait_ge(S("gD"), 1)
            dve.wait_ge(S("gA"), 3)
            dve.tensor_tensor(gat[:, 0], gat[:, 0], gat[:, 4], ALU.add).then_inc(S("gD"), 1)
            dve.wait_ge(S("gD"), 2)
            ea = gat[:, 5, 0, :].unsqueeze(1).to_broadcast([P, NC, 16])
            dve.scalar_tensor_tensor(gat[:, 0], gat[:, 0], -1.0, ea, ALU.mult, ALU.mult).then_inc(S("g_raw"), 1)
            def decay_rest():
                dve.wait_ge(S("gA"), 7)
                dve.tensor_tensor(gat[:, 4], gat[:, 4], gat[:, 2], ALU.subtract).then_inc(S("gD"), 1)
                dve.tensor_tensor(gat[:, 3], gat[:, 3], gat[:, 1], ALU.mult).then_inc(S("g_k"), 1)

            def scaled(h, factors):
                dve.wait_ge(S("onf"), h + 1)
                dve.scalar_tensor_tensor(oT[:, h], oT[:, h], gate_p[:, 32:33], factors, ALU.mult, ALU.mult)\
                    .then_inc(S("on_g"), 1)
                dve.wait_ge(S("on_g"), h + 1)

            def centred(t0, t1):
                ev_wait(dve, ("mean",))
                for t in range(t0, t1):
                    dve.tensor_tensor(cslot(t), csum_in(t), acc[:], ALU.subtract).then_inc(S("xc"), 1)

            def qkv(half):
                def short_taps(h, i):
                    n = 3 * h + i
                    ev_wait(dve, ("qkv", n))
                    if h == 0 and i == 0:
                        dve.wait_ge(S("in_s"), 16)
                        dve.wait_ge(S("pzero"), 1)
                    y = sacc[:, h % 2, i]
                    if i < 2:
                        wait(dve, "qk_fin", 2 * (h - 2) + i + 1)
                    else:
                        wait(dve, "trp", 2 * (h - 1))
                    for j in range(SK):
                        src, w = pad[:, i, j:j + T], swt[:, i * H + h, j:j + 1]
                        if j == 0:
                            ins = dve.tensor_scalar(y, src, w, None, ALU.mult)
                        else:
                            dve.wait_ge(S("stap"), SK * n + j)
                            ins = dve.scalar_tensor_tensor(y, src, w, y, ALU.mult, ALU.add)
                        ins.then_inc(S("stap"), 1)

                for hh in range(HH + 1):
                    h = HH * half + hh
                    if hh < HH:
                        after(("qkv", 3 * h))
                        if hh == 0 and half:
                            dve.wait_ge(S("o"), 4)
                            dve.memset(pad[:, :, 0:SP_], 0.0)
                            dve.memset(pad[:, :, SP_ + T:], 0.0).then_inc(S("pzero"), 1)
                            dve.wait_ge(S("pzero"), 2)
                        short_taps(h, 0)
                    if h == 0:
                        decay_rest()
                    if half and hh == 3:
                        centred(KT // 2, KT)
                    if hh:
                        dve.wait_ge(S("l2r"), h)
                        dve.reciprocal(nst[:, 1], nst[:, 0]).then_inc(S("l2i"), 1)
                    if half and hh == 1:
                        dve.wait_ge(S("on_root"), 1)
                        dve.reciprocal(ost[:, 0:HH * NC], ost[:, 0:HH * NC]).then_inc(S("on_r"), 1)
                    if hh < HH:
                        after(("qkv", 3 * h + 1))
                    if hh:
                        for i, dst in enumerate((qT, kT)):
                            dve.wait_ge(S("l2f"), 2 * (h - 1) + i + 1)
                            if half and hh == 1:
                                dve.wait_ge(S("qdm"), 4)
                            dve.tensor_tensor(dst[:, hh - 1], sacc[:, (h - 1) % 2, i], l2b[:, i], ALU.mult)\
                                .then_inc(S("qk_fin"), 1)
                    if hh < HH:
                        short_taps(h, 1)
                        after(("qkv", 3 * h + 2))
                        short_taps(h, 2)
                        if half == 0:
                            taps(3)
                    if half and hh:
                        scaled(hh - 1, nb2)
                    if half and hh == 2:
                        centred(0, KT // 2)

            XN = (4, 6, 8, 10, 12, 14, 16, 17)

            def taken(key):
                name, t = key
                if name == "co":
                    unit_out(dve, key)
                    dve.wait_ge(S(f"side{t % 2}"), 16 * (t // 2 + 1))
                    dve.tensor_tensor(ya[:, t], bank(key), tmps[t % 2][:], ALU.mult).then_inc(S("evD"), 1)
                if name == "z" and t < HH:
                    ev_wait(dve, key)
                    dve.tensor_tensor(oT[:, t], oT[:, t], tmps[t % 2][:], ALU.mult).then_inc(S("on_z"), 1)

            def gap(R, g):
                n, last = len(GAP), g == len(GAP) - 1
                if g % 2 and g > 1:
                    for q in range(g - 2 if g > 3 else 0, n if last else g):
                        for key in filled(R, q):
                            after(key)
                if g % 2 == 0 and g > 2 or last:
                    for q in range(g - 2 if last else g - 3 if g > 4 else 0, n if last else g - 1):
                        for key in filled(R, q):
                            taken(key)
                if R == 4 and g in XN:
                    t = XN.index(g)
                    dve.tensor_tensor(cslot(t), cslot(t), rstd[:], ALU.mult).then_inc(S("xn"), 1)
                if R < 4:
                    taps(TAP[g])

            lo_, hi_ = slice(0, W64), slice(W64, P)

            def delta(R):
                half, r = divmod(R, NC)

                def scal(k, j):
                    d, hh = divmod(j, HH)
                    q = d * 8 + HH * half + hh
                    return gat[:, k, chunk(d, r), q:q + 1]

                dve.wait_ge(S("grow"), R + 1)
                if r == 0:
                    dve.wait_ge(S("g_all"), 1)
                    dve.wait_ge(S("trc"), 2 * HH * (half + 1))
                wait(dve, "o", R)
                for d in range(2):
                    sl, q = slice(d * HH, d * HH + HH), d * 8 + HH * half
                    ins = dve.tensor_tensor(et[:, sl], pA[:, sl], gat[:, 2, chunk(d, r), q:q + HH].unsqueeze(2)
                                            .to_broadcast([P, HH, P]), ALU.subtract)
                ins.then_inc(S("pre"), 1)
                dve.wait_ge(S("pre"), 3 * R + 1)
                wait(dve, "vn", R)
                dve.tensor_scalar(en[:], et[:], 0.0, None, ALU.max).then_inc(S("pre"), 1)
                dve.wait_ge(S("pre"), 3 * R + 2)
                dve.tensor_scalar(et[:], et[:], 0.0, None, ALU.min).then_inc(S("pre"), 1)
                if R == 6:
                    for t in range(3):
                        low("conv", t, cslot(t))
                dve.wait_ge(S("gram"), R + 1)
                dve.wait_ge(S("en"), R + 1)
                for j in range(J):
                    ins = dve.scalar_tensor_tensor(en[:, j], pB[:, j], scal(1, j), en[:, j], ALU.mult, ALU.mult)
                ins.then_inc(S("L"), 1)
                if R == 6:
                    for t in range(3, KT):
                        low("conv", t, cslot(t))
                gap(R, 0)
                gap(R, 1)
                dve.wait_ge(S("ls"), LEVELS * R + 1)
                i64 = id64.unsqueeze(1).to_broadcast([P, J, W64])
                dve.tensor_tensor(tb[:], i64, ls[:, 0], ALU.subtract)
                dve.wait_ge(S("y"), LEVELS * R + 1)
                dve.tensor_tensor(ub[:], i64, c0, ALU.subtract).then_inc(S("u_upd"), 1)
                for lv in range(1, LEVELS):
                    if lv > 1:
                        dve.wait_ge(S("tr"), (LEVELS - 1) * R + lv - 1)
                        dve.tensor_copy(tb[:], ctr).then_inc(S("tcp"), 1)
                    gap(R, 2 * lv + 1)
                    dve.wait_ge(S("uy"), (LEVELS - 1) * R + lv)
                    if lv < LEVELS - 1:
                        dve.tensor_tensor(ub[:], ub[:], c1, ALU.subtract).then_inc(S("u_upd"), 1)
                    else:
                        dve.tensor_tensor(en[lo_, :, lo_], ub[lo_], c1[lo_], ALU.subtract)
                        dve.tensor_tensor(en[hi_, :, hi_], ub[hi_], c1[hi_], ALU.subtract).then_inc(S("u_upd"), 1)
                    if lv in (1, 2):
                        dve.wait_ge(S("kq"), R + 1)
                        dve.wait_ge(S("etm"), R + 1)
                        s = slice((lv - 1) * HH, lv * HH)
                        dve.tensor_tensor(et[:, s], pA[:, s], et[:, s], ALU.mult).then_inc(S("qk"), 1)
                    gap(R, 2 * lv + 2)
                dve.wait_ge(S("tr"), (LEVELS - 1) * (R + 1))
                dve.tensor_copy(tb[lo_, 0:HH], ctr[lo_, 0:HH])
                dve.tensor_copy(tb[hi_, HH:J], ctr[hi_, HH:J]).then_inc(S("tcp"), 1)
                dve.memset(en[hi_, 0:HH, lo_], 0.0)
                dve.memset(en[lo_, HH:J, hi_], 0.0)
                gap(R, 13)
                dve.wait_ge(S("u12"), R + 1)
                dve.tensor_scalar(en[lo_, 0:HH, hi_], c1[lo_, 0:HH], -1.0, None, ALU.mult)
                dve.tensor_scalar(en[hi_, HH:J, lo_], c1[hi_, HH:J], -1.0, None, ALU.mult).then_inc(S("u12s"), 1)
                for g in range(14, 17):
                    gap(R, g)
                dve.wait_ge(S("o"), R + 1)
                for d in range(2):
                    c = chunk(d, r)
                    dst = oT[:, HH * half:HH * half + HH, c * P:(c + 1) * P]
                    src = pA[:, d * HH:d * HH + HH]
                    if r < NC // 2:
                        ins = dve.tensor_copy(dst, src)
                    else:
                        if d == 0:
                            dve.wait_ge(S("o_acc"), R)
                        ins = dve.tensor_tensor(dst, dst, src, ALU.add)
                ins.then_inc(S("o_acc"), 1)
                if r < NC - 1:
                    dve.wait_ge(S("s"), (NC - 1) * half + r + 1)
                    if r == 0:
                        for d in range(2):
                            ins = dve.tensor_copy(st[:, d * HH:d * HH + HH], pC[:, d * HH:d * HH + HH])
                    else:
                        for j in range(J):
                            ins = dve.scalar_tensor_tensor(st[:, j], st[:, j], scal(5, j), pC[:, j],
                                                           ALU.mult, ALU.add)
                    ins.then_inc(S("s_upd"), 1)
                gap(R, 17)

            qkv(0)
            for R in range(4):
                delta(R)
            assert done_taps[0] == len(TAPS)
            qkv(1)
            dve.wait_ge(S("vroot"), 1)
            dve.wait_ge(S("l2f"), 2 * H)
            dve.reciprocal(nst[:, 1, 0:NC], nst[:, 0, 0:NC]).then_inc(S("vinv"), 1)
            aux_out(dve, ("var",))
            dve.tensor_copy(rstd[:], bank(("var",))).then_inc(S("evD"), 1)
            ev_wait(dve, ("var",))
            for R in range(4, 8):
                delta(R)
            def gated(h):
                dve.wait_ge(S("onsq"), h + 1)
                dve.wait_ge(S(f"side{h % 2}"), 16 * (4 + (h - HH) // 2 + 1))
                dve.scalar_tensor_tensor(oT[:, h], oT[:, h], gate_p[:, 32:33], tmps[h % 2][:], ALU.mult, ALU.mult)\
                    .then_inc(S("on_z"), 1)

            gated(HH)
            gated(HH + 1)
            dve.wait_ge(S("on_root"), 2)
            dve.reciprocal(ost[:, HH * NC:], ost[:, HH * NC:]).then_inc(S("on_r"), 1)
            for h in range(HH):
                low("o", h, oT[:, h])
            gated(HH + 2)
            gated(HH + 3)
            for h in range(HH, H + 1):
                if h < H:
                    dve.wait_ge(S("onf"), h + 1)
                    dve.wait_ge(S("on_z"), h + 1)
                    dve.tensor_tensor(oT[:, h], oT[:, h], onb(h), ALU.mult).then_inc(S("on_g"), 1)
                if h > HH:
                    low("o", h - 1, oT[:, h - 1])
            for t in range(KT):
                unit_out(dve, ("do", t))
                dve.wait_ge(S(f"sgb{t % 2}"), 16 * (t // 2 + 1))
                dve.tensor_tensor(gst[:, t % 2], bank(("do", t)), gst[:, t % 2], ALU.mult).then_inc(S("evD"), 1)
                after(("do", t))
                ev_wait(dve, ("do", t))
                dve.tensor_tensor(ya[:, t], ya[:, t], gst[:, t % 2], ALU.add).then_inc(S("yv"), 1)
                dve.wait_ge(S("yb_hi"), t + 1)
                dve.tensor_tensor(yb_lo[:, t], ya[:, t], yb_hi[:, t].bitcast(F32), ALU.subtract)\
                    .then_inc(S("yb_lo"), 1)
            for t in range(KT):
                unit_out(dve, ("wo", t))
                dve.wait_ge(S(f"side{t % 2}"), 16 * (6 + t // 2 + 1))
                dve.tensor_tensor(x[:, t], bank(("wo", t)), tmps[t % 2][:], ALU.add).then_inc(S("evD"), 1)
                after(("wo", t))
                low("ffn0", t, x[:, t], v("g_ffn", t))

            def ffn(f, nu, g):
                def step(i):
                    for q in range(2):
                        n = U.at[("fg" + f, q)]
                        du = O.at[("fu" + f, q)]
                        last = isinstance(i, int)
                        if last and i == 0 and q == 0:
                            lo(n + 2)
                            recip(nu)
                        dve.wait_ge(S("gemm"), n + 1 + 4 * i)
                        if not (last and i == 0 and q == 0):
                            dve.wait_ge(S("h_hi"), FT * int(f) + q + 2 * i)
                        bg, bu = (pg[:, O.at[(k + f, 2 * i + q if last else 2 + q)] % 2, :] for k in ("fg", "fu"))
                        dve.tensor_tensor(tmp1[:], bg, rstd[:], ALU.mult).then_inc(S("evD"), 1)
                        if not (last and i == 0 and q == 0):
                            lo(n + 2, i, U.cols[n + 2 + (4 * i if last else 0)])
                        dve.wait_ge(S("gemm"), n + 2 + 4 * i)
                        wait(dve, "h_lo", FT * int(f) + q + 2 * i)
                        dve.tensor_tensor(tmp2[:], bu, rstd[:], ALU.mult).then_inc(S("evD"), 1)
                        lo(n + 3, i, U.cols[n + 3 + (4 * i if last else 0)])
                        dve.wait_ge(S("sil"), FT * int(f) + q + 1 + 2 * i)
                        dve.wait_ge(S("evD"), O.count(du) + 4 * i)
                        dve.tensor_tensor(tmp2[:], tmp2[:], tmp1[:], ALU.mult).then_inc(S("hm"), 1)
                        dve.wait_ge(S("h_hi"), FT * int(f) + q + 1 + 2 * i)
                        m = 2 * i + q
                        at_m = (lambda b: b[:, m]) if last else \
                            (lambda b: b[:, bass.ds(m, 1)].rearrange("p a n -> p (a n)"))
                        dve.tensor_tensor(at_m(h_lo), tmp2[:], at_m(h_hi).bitcast(F32), ALU.subtract)\
                            .then_inc(S("h_lo"), 1)

                step(0)
                with dve.Fori(1, FT // 2 - 1) as i:
                    step(i)
                step(FT // 2 - 1)
                if f == "0":
                    rope_angles()
                for m in range(KT):
                    after(("fd" + f, 2 * m))
                    after(("fd" + f, 2 * m + 1))
                    if f != "0":
                        continue
                    unit_out(dve, ("fd" + f, 2 * m + 1))
                    dve.tensor_tensor(x[:, m], bank(("fd" + f, m)), x[:, m], ALU.add).then_inc(S("evD"), 1)
                    low("pg", m, x[:, m], v(g, m))

            def rope_angles():
                def step(k, ins):
                    ins.then_inc(S("ra"), 1)
                    dve.wait_ge(S("ra"), k)

                whole = 12582912.0
                c_a, c_b = 6.28125, 0.00193500518798828125
                c_c = float(np.float64(2 * np.pi) - c_a - c_b)
                dve.wait_ge(S("in_r"), 16)
                step(1, dve.tensor_scalar(rcos[:], rpos[:], gate_p[:, 37:38], None, ALU.mult))
                step(2, dve.tensor_scalar(rsin[:], rcos[:], float(1 / (2 * np.pi)), whole, ALU.mult, ALU.add))
                step(3, dve.tensor_scalar(rsin[:], rsin[:], -whole, None, ALU.add))
                for q, c_ in enumerate((c_a, c_b, c_c)):
                    step(4 + q, dve.scalar_tensor_tensor(rcos[:], rsin[:], -c_, rcos[:], ALU.mult, ALU.add))
                step(7, dve.tensor_scalar(rcos[:], rcos[:], 3.1415925, -3.1415925, ALU.min, ALU.max))
                dve.scalar_tensor_tensor(rpos[:].bitcast(F32), rcos[:], -1.0, rcos[:], ALU.mult, ALU.max)\
                    .then_inc(S("rope"), 1)

            ffn("0", 2, "g_pl")
            for t in range(KT):
                if t == 0:
                    after(("pg", t))
                    recip(3)
                    dve.wait_ge(S("in_pl"), 16)
                unit_out(dve, ("pg", t))
                dve.tensor_tensor(tmps[t % 2][:], bank(("pg", t)), rstd[:], ALU.mult).then_inc(S("evD"), 1)
                dve.wait_ge(S("pgs"), t + 1)
                dve.tensor_tensor(tmps[t % 2][:], tmps[t % 2][:], pl[:, t], ALU.mult).then_inc(S("pgm"), 1)
                dve.wait_ge(S("pgm"), t + 1)
                dve.tensor_tensor(x[:, t], x[:, t], tmps[t % 2][:], ALU.add).then_inc(S("x2"), 1)
                if t:
                    after(("pg", t))
            recip(4)
            for t in range(KT):
                dve.scalar_tensor_tensor(x[:, t], x[:, t], v("g_final", t), rstd[:], ALU.mult, ALU.mult)\
                    .then_inc(S("xf"), 1)
                if t:
                    low("ffn1", t - 1, x[:, t - 1], v("ffn1_pre", t - 1))
            low("ffn1", KT - 1, x[:, KT - 1], v("ffn1_pre", KT - 1))
            ffn("1", 5, None)

            def post(nu, k, src, half_, s, g2):
                recip(nu)
                for t in range(KT + 1):
                    if t < KT:
                        q = KT * k + t
                        if t < PD:
                            dve.tensor_tensor(src[:, t], src[:, t], rstd[:], ALU.mult).then_inc(S("xt"), 1)
                            dve.wait_ge(S("xt"), PD * k + t + 1)
                        else:
                            dve.wait_ge(S("xp"), (KT - PD) * k + t - PD + 1)
                        dve.scalar_tensor_tensor(x[:, t], src[:, t], half_, x[:, t], ALU.mult, ALU.add)\
                            .then_inc(S("xu"), 1)
                    if t and s:
                        low(s, t - 1, x[:, t - 1], v(g2, t - 1))

            post(6, 0, hb, 0.5, "mix", "mix_pre")
            dve.memset(up[:, :, 0:PW], 0.0)
            dve.memset(kz[0:HD2, 1], 0.0)
            dve.memset(kz[HD2:P, 0], 0.0)
            dve.memset(win[:, :, 0:PW], 0.0).then_inc(S("uzero"), 1)
            dve.tensor_scalar(nsink[:], gate_p[:, 38:46].rearrange("p (h i) -> p i h", h=2), -1.0, None, ALU.mult)\
                .then_inc(S("nsink"), 1)
            dve.wait_ge(S("nsink"), 1)

            def rotated(i):
                dve.wait_ge(S("rsin"), 2)
                if i < 3:
                    dve.wait_ge(S("rpart"), i + 1)
                else:
                    aux_out(dve, ("rp", i))
                wait(dve, "qk2", i)
                dve.tensor_tensor(rt[:, 0], zq[:, i], rcos[:], ALU.mult).then_inc(S("rt"), 1)
                if i < 3:
                    dve.tensor_tensor(rt[:, 1], rpb[i], rsin[:], ALU.mult).then_inc(S("rt"), 1)
                else:
                    dve.tensor_tensor(rt[:, 1], bank(("rp", i)), rsin[:], ALU.mult).then_inc(S("evD"), 1)
                    ev_wait(dve, ("rp", i))
                dve.wait_ge(S("rt"), i + 1 + min(i + 1, 3))
                if i:
                    dve.tensor_tensor(qk2[:, i - 1], rt[:, 0], rt[:, 1], ALU.add).then_inc(S("qk2"), 1)
                else:
                    for h, p_ in enumerate((slice(0, HD2), slice(HD2, P))):
                        ins = dve.tensor_tensor(kz[p_, h], rt[p_, 0], rt[p_, 1], ALU.add)
                    ins.then_inc(S("qk2"), 1)

            def evac(key, dst):
                unit_out(dve, key)
                dve.tensor_tensor(dst, bank(key), rstd[:], ALU.mult).then_inc(S("evD"), 1)

            def mixed(key):
                if key == ("mk", 0):
                    after(key)
                    recip(7)
                name, i = key
                evac(key, {"mk": zq[:, 0], "mv": zv[:], "mq": zq[:, 1 + i]}[name])
                if key != ("mk", 0):
                    after(key)

            for key in MIX[:3]:
                mixed(key)
            rotated(0)
            mixed(("mq", 1))
            rotated(1)
            mixed(("mq", 2))

            def bias(s):
                i, n = divmod(s, NB)
                k0 = P if n == 0 else 0
                dve.wait_ge(S("scores"), s + 1)
                wait(dve, "turn", s - 2)
                y = sm[:, s % 3, :, k0:]
                mask = band[:, k0:].unsqueeze(1).to_broadcast([P, 2, 2 * P - k0])
                dve.tensor_tensor(y, pa2[:, s % 2, :, k0:], mask, ALU.add).then_inc(S("smask"), 1)
                dve.wait_ge(S("smask"), s + 1)
                dve.tensor_reduce(out=sml[:, 0, s], in_=y, axis=mybir.AxisListType.X, op=ALU.max)\
                    .then_inc(S("smax"), 1)
                dve.wait_ge(S("smax"), s + 1)
                dve.scalar_tensor_tensor(sml[:, 1, s], sml[:, 0, s], -HD2 ** -0.5, nsink[:, i], ALU.mult, ALU.min)\
                    .then_inc(S("sneg"), 1)
                dve.wait_ge(S("sneg"), s + 1)
                dve.tensor_tensor(sml[:, 3, s], sml[:, 1, s], nsink[:, i], ALU.subtract).then_inc(S("bias"), 1)

            def normed(s):
                k0 = P if s % NB == 0 else 0
                dve.wait_ge(S("exp"), s + 1)
                dve.tensor_tensor(sml[:, 4, s], sml[:, 2, s], sml[:, 3, s], ALU.add).then_inc(S("den"), 1)
                dve.wait_ge(S("den"), 2 * s + 1)
                dve.reciprocal(sml[:, 4, s], sml[:, 4, s]).then_inc(S("den"), 1)
                dve.wait_ge(S("den"), 2 * s + 2)
                for h in range(2):
                    y = sm[:, s % 3, h, k0:]
                    ins = dve.tensor_scalar(y, y, sml[:, 4, s, h:h + 1], None, ALU.mult)
                ins.then_inc(S("prob"), 1)

            def means(g):
                w, u = win[:, g % 2, PW:], up[:, g, PW:]
                dve.wait_ge(S("win"), PT_ - g)
                dve.scalar_tensor_tensor(wd[:, g], w, 1.0 / POOL_W[g], u, ALU.mult, ALU.subtract)\
                    .then_inc(S("wdm"), 1)
                dve.tensor_tensor(tmp1[:, 0:16], w[:, 0:16], edge[:, g], ALU.mult).then_inc(S("wdm"), 1)
                dve.wait_ge(S("wdm"), 2 * (PT_ - g))
                dve.tensor_tensor(wd[:, g, 0:16], tmp1[:, 0:16], u[:, 0:16], ALU.subtract).then_inc(S("wd"), 1)
                dve.wait_ge(S("wd"), PT_ - g)

            MEANS = {7: 3, 10: 2, 13: 1, 16: 0}
            for s in range(16 + 3):
                if s < 16:
                    bias(s)
                if s == 0:
                    rotated(2)
                if 0 <= s - 1 < 16:
                    normed(s - 1)
                if s < 15 and s % 3 == 2:
                    key = MFILL[s // 3]
                    evac(key, zq[:, 1 + key[1]] if key[0] == "mq" else up[:, key[1], PW:])
                if s % 3 == 0 and 0 < s < 16:
                    after(MFILL[s // 3 - 1])
                for k in MAUX.get(s, []):
                    if k[0] == "rp":
                        rotated(k[1])
                if s in MEANS:
                    means(MEANS[s])
                if s >= 3 and (s - 3) % NB == NB - 1:
                    i = (s - 3) // NB
                    dve.wait_ge(S("values"), s - 2)
                    dve.tensor_copy(mo[:, PT_ + i], pc2[:, i % 2]).then_inc(S("oat"), 1)
            for nu, t0, at_ in ((8, 0, 50), (9, PT_, 54)):
                recip(nu)
                for t in range(t0, t0 + PT_):
                    g = at_ + t - t0
                    dve.scalar_tensor_tensor(mo[:, t], mo[:, t], gate_p[:, g:g + 1], rstd[:], ALU.mult, ALU.mult)\
                        .then_inc(S("mh"), 1)
                for t in range(t0, t0 + PT_):
                    low("out", t, mo[:, t])
            for t in range(KT):
                after(("mo", t))
            post(10, 1, hb2, 1.0, "ffn2", "ffn2_pre")
            ffn("2", 11, None)
            post(12, 2, hb, 0.5, None, None)

        @block.gpsimd
        def _(pool):
            def adds(nu):
                for t in range(1, NORMS[nu] - 1):
                    pool.wait_ge(S("sq"), SQ[nu] + t + 1)
                    wait(pool, "add", AD[nu] + t - 1)
                    pool.tensor_tensor(acc[:], acc[:], sq[:, t % 2, :], ALU.add).then_inc(S("add"), 1)

            def delta(R):
                half, r = divmod(R, NC)

                def toks(k, d):
                    q = d * 8 + HH * half
                    return gat[:, k, chunk(d, r), q:q + HH].unsqueeze(2).to_broadcast([P, HH, P])

                def level(lv):
                    pool.wait_ge(S("lc"), R + 1)
                    wait(pool, "y", LEVELS * R + lv - 1)
                    if lv == 2:
                        pool.wait_ge(S("u_upd"), LEVELS * R + 1)
                    q = C_LVL + lv * 2 * W64
                    mask = quad(consts[:, q:q + 2 * W64], 2).unsqueeze(2).to_broadcast([P, 2, HH, W64])
                    pool.tensor_tensor(ls[:, lv % 2].rearrange("p (d h) c -> p d h c", d=2),
                                       lc[:].rearrange("p (d h) c -> p d h c", d=2), mask, ALU.mult)\
                        .then_inc(S("ls"), 1)

                level(0)
                level(1)
                pool.wait_ge(S("et"), R + 1)
                for d in range(2):
                    s = slice(d * HH, d * HH + HH)
                    ins = pool.tensor_tensor(et[:, s], et[:, s], tri[d].unsqueeze(1).to_broadcast([P, HH, P]), ALU.mult)
                ins.then_inc(S("etm"), 1)
                level(2)
                pool.wait_ge(S("eg"), R + 1)
                for d in range(2):
                    s, c = slice(d * HH, d * HH + HH), chunk(d, r)
                    ins = pool.tensor_tensor(qd[:, s], qd[:, s], qT[:, :, c * P:(c + 1) * P], ALU.mult)
                ins.then_inc(S("qdm"), 1)
                level(3)
                pool.wait_ge(S("g_k"), 1)
                wait(pool, "s", (NC - 1) * half + r)
                wait(pool, "vn", R)
                for dst, src, k, name, lv in ((kb, ktok, 3, "kb", 4), (bv, vtok, 1, "bv", 5), (kt, ktok, 4, "kt", 6)):
                    if name == "kt" and r == NC - 1:
                        continue
                    if name != "kb":
                        wait(pool, "o", R)
                    for d in range(2):
                        ins = pool.tensor_tensor(dst[:, d * HH:d * HH + HH], src[:, :, chunk(d, r), :], toks(k, d),
                                                 ALU.mult)
                    ins.then_inc(S(name), 1)
                    if lv < LEVELS:
                        level(lv)

            pool.wait_ge(S("in_c"), 16)
            adds(1)
            for q, t in enumerate((0, KT - 1)):
                ev_wait(pool, ("gla", t))
                for j in range(CK):
                    src, w = cpad[:, t, j:j + T], vec[:, t, len(VEC) + j:len(VEC) + j + 1]
                    y, b = csum_in(t), oT[:, HH + j % 2]
                    if j == 0:
                        pool.tensor_scalar(y, src, w, v("conv_b", t), ALU.mult, ALU.add).then_inc(S("ptap"), 1)
                        continue
                    wait(pool, "ptap", q * CK + j - 2)
                    pool.tensor_tensor(b, src, w.to_broadcast([P, T]), ALU.mult).then_inc(S("pprod"), 1)
                    pool.wait_ge(S("pprod"), q * (CK - 1) + j)
                    pool.wait_ge(S("ptap"), q * CK + j)
                    pool.tensor_tensor(y, y, b, ALU.add).then_inc(S("ptap"), 1)
            for R in range(4):
                if R == 0:
                    pool.wait_ge(S("g_all"), 1)
                    pool.wait_ge(S("trc"), 2 * HH)
                delta(R)
            pool.wait_ge(S("tap"), len(TAPS))
            pool.wait_ge(S("ptap"), 2 * CK)
            for t in range(1, KT):
                wait(pool, "csum", t - 1)
                pool.tensor_tensor(acc[:], csum_in(0) if t == 1 else acc[:], csum_in(t), ALU.add)\
                    .then_inc(S("csum"), 1)
            for t in range(1, KT):
                pool.wait_ge(S("cvs"), t + 1)
                wait(pool, "cva", t - 1)
                pool.tensor_tensor(rstd[:], rstd[:], tmps[t % 2][:], ALU.add).then_inc(S("cva"), 1)
            for R in range(4, 8):
                delta(R)
            def post(nu, k, src):
                pool.wait_ge(S("rstd"), nu + 1)
                for t in range(PD, KT):
                    pool.tensor_tensor(src[:, t], src[:, t], rstd[:], ALU.mult).then_inc(S("xp"), 1)

            for nu in range(2, 7):
                adds(nu)
            post(6, 0, hb)
            adds(7)
            pool.wait_ge(S("uzero"), 1)
            for g in reversed(range(PT_)):
                ev_wait(pool, ("mu", g))
                wait(pool, "wd", PT_ - 1 - g)
                for q in range(g + 1):
                    src = up[:, g] if q == 0 else win[:, (q - 1) % 2]
                    ins = pool.tensor_tensor(win[:, q % 2, PW:], src[:, PW:], src[:, PW - (1 << q):PW + T - (1 << q)],
                                             ALU.add)
                    if q < g:
                        n_add = sum(range(g + 1, PT_)) + q + 1
                        ins.then_inc(S("wadd"), 1)
                        pool.wait_ge(S("wadd"), n_add)
                ins.then_inc(S("win"), 1)
            for nu in range(8, 11):
                adds(nu)
            post(10, 1, hb2)
            adds(11)
            adds(12)
            post(12, 2, hb)



def kernel(**inputs):
    import concourse.bacc as bacc
    from concourse.bass_utils import run_bass_kernel_spmd

    def tiles(w):
        k, n = w.shape
        return np.ascontiguousarray(w.reshape(k // P, P, n // P, P).transpose(2, 1, 0, 3).reshape(n // P, P, k))

    def cols(w):
        return np.ascontiguousarray(w.T.reshape(w.shape[1] // P, P, w.shape[0]).transpose(1, 0, 2))

    f = {k: np.asarray(w) for k, w in inputs.items()}
    w_in = f["w_in"][0]
    pre = 2 * D + 4 * D
    arrays = {
        "x": cols(f["x"][0]),
        "p": cols(f["p"][0, 0]),
        "consts": constant_table(),
        "w_in": tiles(np.concatenate([w_in[:, :pre], w_in[:, pre + 32:]], 1)),
        "w_ab": np.ascontiguousarray(w_in[:, pre:pre + 32].reshape(KT, P, 32).transpose(1, 0, 2).reshape(P, KT * 32)),
        "w_plp": np.ascontiguousarray(
            tiles(f["w_pl_proj"][0]).reshape(4, 2, P, 2 * P).transpose(0, 2, 1, 3).reshape(4, P, 4 * P)),
        "w_co": tiles(f["w_conv_out"][0]),
        "w_do": tiles(f["w_delta_out"][0]),
        "w_wo": tiles(f["w_o"][0]),
        "w_gu0": tiles(f["w_gate_up"][0]),
        "w_dn0": np.ascontiguousarray(
            f["w_down"][0].reshape(2, KH, P, KT, P).transpose(3, 0, 2, 1, 4).reshape(KT, 2, P, KH * P)),
        "w_pg": tiles(f["w_pl_gate"][0]),
    }

    def down(w):
        return np.ascontiguousarray(w.reshape(2, KH, P, KT, P).transpose(3, 0, 2, 1, 4).reshape(KT, 2, P, KH * P))

    pairs = np.concatenate([np.arange(HD2) + HD2 * h for i in range(4) for h in (i, i + 4)])
    w2, half = f["w_in_2"][0], D // 2
    arrays.update({
        "w_gu1": tiles(f["ffn1_w_gu_2"][0]), "w_dn1": down(f["ffn1_w_down_2"][0]),
        "w_gu2": tiles(f["ffn2_w_gu_2"][0]), "w_dn2": down(f["ffn2_w_down_2"][0]),
        "w_in2": tiles(np.concatenate([w2[:, :half], w2[:, half + pairs], w2[:, D:]], 1)),
        "w_out2": tiles(np.concatenate([f["w_out_2"][0][:half], f["w_out_2"][0][half + pairs]], 0)),
        "pos": np.ascontiguousarray(np.broadcast_to(f["positions_2"].reshape(1, T), (P, T))),
        "c2": np.concatenate([mixer_table(), f["w_pool_2"][0].transpose(1, 0, 2).reshape(P, PT_ * P)], 1),
    })
    names = ["g_mix", "conv_dw_b", "conv_ln_g", "conv_ln_b", "g_ffn", "g_pl", "g_pl_proj", "g_final",
             "ffn1_pre_2", "ffn1_post_2", "mix_pre_2", "mix_post_2", "ffn2_pre_2", "ffn2_post_2"]
    rows = np.concatenate([f[n].reshape(1, D) for n in names] + [f["conv_dw_w"][0]], 0)
    arrays["vec"] = np.ascontiguousarray(rows.T.reshape(KT, P, NV).transpose(1, 0, 2))
    arrays["swt"] = np.ascontiguousarray(f["qkv_conv_w"][0].T.reshape(3 * H, P, SK).transpose(1, 0, 2))
    small = np.concatenate([f["a_log"].reshape(-1), f["dt_bias"].reshape(-1)])
    eps = np.array([EPS, P * EPS, EPS, LN_EPS], np.float32)
    dim = np.arange(P) % HD2
    freq = np.float32(THETA) ** (-np.arange(0, ROT, 2, dtype=np.float32) / np.float32(ROT))
    freq = np.where(dim < ROT, freq[dim % (ROT // 2)], 0).astype(np.float32).reshape(P, 1)
    arrays["gate_p"] = np.concatenate(
        [np.broadcast_to(small, (P, 32)), f["delta_norm_g"].reshape(P, 1), np.broadcast_to(eps, (P, 4)), freq,
         np.broadcast_to(f["sinks_2"].reshape(1, 8), (P, 8)), f["pool_scale_2"].reshape(PT_, P).T,
         f["g_pool_2"].reshape(PT_, P).T, f["g_attn_2"].reshape(-1)[pairs].reshape(PT_, P).T,
         np.full((P, 1), np.pi / 2, np.float32)], 1)
    nc = bacc.Bacc("TRN2", target_bir_lowering=False, num_devices=1)
    a = {n: nc.dram_tensor("in_" + n, w.shape, mybir.dt.from_np(w.dtype), kind="ExternalInput").ap()
         for n, w in arrays.items()}
    out = nc.dram_tensor("out", (KT, P, T), F32, kind="ExternalOutput").ap()
    build(nc, a, out)
    r = run_bass_kernel_spmd(nc, [{"in_" + n: w for n, w in arrays.items()}], core_ids=[0])
    y = np.asarray(r.results[0]["out"])
    return np.ascontiguousarray(y.transpose(2, 0, 1).reshape(1, T, D))
```
